# Optimizing a Trainium2 kernel written in Bass

```python
import math
import jax, jax.numpy as jnp
from jax import lax
import numpy as np

D_MODEL = 2048
BATCH = 1
SEQ = 512
DEPTH = 1

N_MIXERS = 2
NSA_HEADS = 16
NSA_GROUPS = 4
NSA_HEAD_DIM = 128
NSA_REP = NSA_HEADS // NSA_GROUPS
CMP_LEN = 32
CMP_STRIDE = 16
SEL_BLOCK = 64
N_SELECT = 16
WINDOW = 512
Q_BLOCK = 128
NSA_IN = NSA_HEADS * NSA_HEAD_DIM + 6 * NSA_GROUPS * NSA_HEAD_DIM + 3 * NSA_HEADS
ML_HEADS = 8
ML_V_DIM = D_MODEL // ML_HEADS
ML_QK_DIM = ML_V_DIM // 2
ML_CHUNK = 64
ML_IN = 2 * ML_HEADS * ML_QK_DIM + 2 * ML_HEADS * ML_V_DIM + 2 * ML_HEADS
D_FF = -(-8 * D_MODEL // (3 * 256)) * 256
EPS = 1e-6
NEG_INIT = -1e30

kernel_name = 'hybrid_nsa_mlstm_swiglu_trunk'

def rms_norm(x, g):
    x32 = x.astype(jnp.float32)
    y = x32 * lax.rsqrt(jnp.mean(x32 * x32, axis=-1, keepdims=True) + EPS)
    return (y * g.astype(jnp.float32)).astype(x.dtype)

def masked_softmax(s, mask):
    s = jnp.where(mask, s.astype(jnp.float32), -jnp.inf)
    m = jnp.max(s, axis=-1, keepdims=True)
    m = jnp.where(jnp.isfinite(m), m, 0.0)
    p = jnp.exp(s - m)
    return p / jnp.maximum(jnp.sum(p, axis=-1, keepdims=True), 1e-30)

def compress_kv(kv, pos, w1, b1, w2):
    B, S, G, dh = kv.shape
    n_cmp = (S - CMP_LEN) // CMP_STRIDE + 1
    idx = jnp.arange(n_cmp)[:, None] * CMP_STRIDE + jnp.arange(CMP_LEN)[None, :]
    blocks = kv[:, idx] + pos[None, None, :, None, :]
    blocks = jnp.transpose(blocks, (0, 1, 3, 2, 4)).reshape(B, n_cmp, G, CMP_LEN * dh)
    hdn = jax.nn.gelu(blocks @ w1 + b1)
    return hdn @ w2

def nsa_mixer(h, w_in, b_gate, q_g, k_g, cmp_pos, cmp_w1, cmp_b1, cmp_w2, w_out):
    B, S, _ = h.shape
    G, R, dh = NSA_GROUPS, NSA_REP, NSA_HEAD_DIM
    qd, kvd = NSA_HEADS * dh, G * dh
    proj = h @ w_in
    q = rms_norm(proj[..., :qd].reshape(B, S, G, R, dh), q_g)
    kv = proj[..., qd:qd + 6 * kvd].reshape(B, S, 6, G, dh)
    gates = jax.nn.sigmoid(proj[..., qd + 6 * kvd:] + b_gate).reshape(B, S, G, R, 3)
    k_cmp = rms_norm(compress_kv(kv[:, :, 0], cmp_pos[0], cmp_w1[0], cmp_b1[0], cmp_w2[0]), k_g[0])
    v_cmp = compress_kv(kv[:, :, 1], cmp_pos[1], cmp_w1[1], cmp_b1[1], cmp_w2[1])
    k_sel = rms_norm(kv[:, :, 2], k_g[1])
    v_sel = kv[:, :, 3]
    k_win = rms_norm(kv[:, :, 4], k_g[2])
    v_win = kv[:, :, 5]

    n_cmp = k_cmp.shape[1]
    n_sel = S // SEL_BLOCK
    k_top = min(N_SELECT, n_sel)
    cmp_start = jnp.arange(n_cmp) * CMP_STRIDE
    cmp_end = cmp_start + CMP_LEN - 1
    sel_start = jnp.arange(n_sel) * SEL_BLOCK
    overlap = ((cmp_start[:, None] < sel_start[None, :] + SEL_BLOCK)
               & (cmp_start[:, None] + CMP_LEN > sel_start[None, :])).astype(jnp.float32)
    ks_blk = jnp.transpose(k_sel.reshape(B, n_sel, SEL_BLOCK, G, dh), (0, 3, 1, 2, 4))
    vs_blk = jnp.transpose(v_sel.reshape(B, n_sel, SEL_BLOCK, G, dh), (0, 3, 1, 2, 4))
    kw_pad = jnp.pad(k_win, ((0, 0), (WINDOW, 0), (0, 0), (0, 0)))
    vw_pad = jnp.pad(v_win, ((0, 0), (WINDOW, 0), (0, 0), (0, 0)))
    scale = dh ** -0.5
    bi = jnp.arange(B)[:, None, None, None]
    gi = jnp.arange(G)[None, :, None, None]
    jj = jnp.arange(n_sel)

    def block(qb):
        s0 = qb * Q_BLOCK
        t = s0 + jnp.arange(Q_BLOCK)
        qx = lax.dynamic_slice_in_dim(q, s0, Q_BLOCK, axis=1)
        gx = lax.dynamic_slice_in_dim(gates, s0, Q_BLOCK, axis=1)
        s = jnp.einsum('bqgrd,bcgd->bgrqc', qx, k_cmp) * scale
        p_cmp = masked_softmax(s, cmp_end[None, :] <= t[:, None])
        o_cmp = jnp.einsum('bgrqc,bcgd->bqgrd', p_cmp.astype(v_cmp.dtype), v_cmp)
        imp = jnp.einsum('bgrqc,cj->bgqj', p_cmp, overlap)
        cur = t // SEL_BLOCK
        valid = jj[None, :] <= cur[:, None]
        forced = (jj[None, :] == 0) | (jj[None, :] == cur[:, None]) | (jj[None, :] == cur[:, None] - 1)
        score = jnp.where(valid, jnp.where(forced, jnp.inf, imp), -jnp.inf)
        top_val, top_idx = lax.top_k(score, k_top)
        blk_ok = top_val > -jnp.inf
        kg = ks_blk[bi, gi, top_idx]
        vg = vs_blk[bi, gi, top_idx]
        s = jnp.einsum('bqgrd,bgqknd->bgrqkn', qx, kg) * scale
        key_pos = top_idx[..., None] * SEL_BLOCK + jnp.arange(SEL_BLOCK)
        smask = blk_ok[..., None] & (key_pos <= t[None, None, :, None, None])
        nk = k_top * SEL_BLOCK
        p = masked_softmax(s.reshape(B, G, R, Q_BLOCK, nk), smask.reshape(B, G, 1, Q_BLOCK, nk))
        o_sel = jnp.einsum('bgrqm,bgqmd->bqgrd', p.astype(vg.dtype), vg.reshape(B, G, Q_BLOCK, nk, dh))
        kw = lax.dynamic_slice_in_dim(kw_pad, s0, WINDOW + Q_BLOCK, axis=1)
        vw = lax.dynamic_slice_in_dim(vw_pad, s0, WINDOW + Q_BLOCK, axis=1)
        pos = s0 - WINDOW + jnp.arange(WINDOW + Q_BLOCK)
        wmask = (pos[None, :] >= 0) & (pos[None, :] <= t[:, None]) & (t[:, None] - pos[None, :] < WINDOW)
        s = jnp.einsum('bqgrd,bkgd->bgrqk', qx, kw) * scale
        p = masked_softmax(s, wmask)
        o_win = jnp.einsum('bgrqk,bkgd->bqgrd', p.astype(vw.dtype), vw)
        return gx[..., 0:1] * o_cmp + gx[..., 1:2] * o_sel + gx[..., 2:3] * o_win

    out = lax.map(block, jnp.arange(S // Q_BLOCK))
    out = jnp.moveaxis(out, 0, 1).reshape(B, S, NSA_HEADS * dh)
    return out @ w_out

def mlstm_mixer(h, w_in, b_if, out_g, w_out):
    B, S, _ = h.shape
    H, dk, dv, L = ML_HEADS, ML_QK_DIM, ML_V_DIM, ML_CHUNK
    nc = S // L
    proj = (h @ w_in).astype(jnp.float32)
    cuts = [H * dk, 2 * H * dk, 2 * H * dk + H * dv, 2 * H * dk + 2 * H * dv, 2 * H * dk + 2 * H * dv + H]
    q, k, v, o, ig, fg = jnp.split(proj, cuts, axis=-1)
    b_if = b_if.astype(jnp.float32)
    ig = ig + b_if[:H]
    lf = jax.nn.log_sigmoid(fg + b_if[H:])

    def chunks(a, d):
        return jnp.transpose(a.reshape(B, nc, L, H, d), (1, 0, 3, 2, 4))

    qc = chunks(q, dk)
    kc = chunks(k * dk ** -0.5, dk)
    vc = chunks(v, dv)
    igc = jnp.transpose(ig.reshape(B, nc, L, H), (1, 0, 3, 2))
    lfc = jnp.transpose(lf.reshape(B, nc, L, H), (1, 0, 3, 2))
    tril = jnp.tril(jnp.ones((L, L), dtype=bool))

    def step(carry, xs):
        C, n, m = carry
        qx, kx, vx, ix, fx = xs
        b = jnp.cumsum(fx, axis=-1)
        D = jnp.where(tril, b[..., :, None] - b[..., None, :] + ix[..., None, :], -jnp.inf)
        m_inter = b + m[..., None]
        m_t = jnp.maximum(m_inter, jnp.max(D, axis=-1))
        A = jnp.exp(D - m_t[..., None]) * jnp.einsum('bhtd,bhsd->bhts', qx, kx)
        dec = jnp.exp(m_inter - m_t)
        num = jnp.einsum('bhts,bhsv->bhtv', A, vx) + dec[..., None] * jnp.einsum('bhtd,bhdv->bhtv', qx, C)
        den = jnp.sum(A, axis=-1) + dec * jnp.einsum('bhtd,bhd->bht', qx, n)
        hx = num / jnp.maximum(jnp.abs(den), jnp.exp(-m_t))[..., None]
        b_last = b[..., -1]
        g = b_last[..., None] - b + ix
        m_new = jnp.maximum(b_last + m, jnp.max(g, axis=-1))
        w = jnp.exp(g - m_new[..., None])
        cd = jnp.exp(b_last + m - m_new)
        C = cd[..., None, None] * C + jnp.einsum('bhs,bhsd,bhsv->bhdv', w, kx, vx)
        n = cd[..., None] * n + jnp.einsum('bhs,bhsd->bhd', w, kx)
        return (C, n, m_new), hx

    init = (jnp.zeros((B, H, dk, dv), jnp.float32), jnp.zeros((B, H, dk), jnp.float32),
            jnp.full((B, H), NEG_INIT, jnp.float32))
    _, hs = lax.scan(step, init, (qc, kc, vc, igc, lfc))
    hs = jnp.transpose(hs, (1, 0, 3, 2, 4)).reshape(B, S, H, dv)
    hs = rms_norm(hs, out_g.reshape(H, dv)).reshape(B, S, H * dv)
    y = jax.nn.sigmoid(o) * hs
    return y.astype(h.dtype) @ w_out

def swiglu(h, wg, wu, wd):
    return (jax.nn.silu(h @ wg) * (h @ wu)) @ wd

def setup_inputs(seed: int = 0) -> dict:
    key = jax.random.key(seed)
    ks = jax.random.split(key, 24)
    n_nsa = sum(1 for i in range(DEPTH) if i % N_MIXERS == 0)
    n_ml = sum(1 for i in range(DEPTH) if i % N_MIXERS == 1)
    dh = NSA_HEAD_DIM
    f32 = jnp.float32

    def nrm(k, shape, scale):
        return jax.random.normal(k, shape, f32) * scale

    f_bias = jnp.linspace(3.0, 6.0, ML_HEADS, dtype=f32)
    b_if = jnp.concatenate([nrm(ks[14], (n_ml, ML_HEADS), 0.1),
                            f_bias[None, :] + nrm(ks[15], (n_ml, ML_HEADS), 0.1)], axis=-1)
    return {
        'x': nrm(ks[0], (BATCH, SEQ, D_MODEL), 1.0),
        'norm_mix_g': 1.0 + nrm(ks[1], (DEPTH, D_MODEL), 0.02),
        'norm_ffn_g': 1.0 + nrm(ks[2], (DEPTH, D_MODEL), 0.02),
        'nsa_w_in': nrm(ks[3], (n_nsa, D_MODEL, NSA_IN), D_MODEL ** -0.5),
        'nsa_b_gate': nrm(ks[4], (n_nsa, 3 * NSA_HEADS), 0.1),
        'nsa_q_norm_g': 1.0 + nrm(ks[5], (n_nsa, dh), 0.02),
        'nsa_k_norm_g': 1.0 + nrm(ks[6], (n_nsa, 3, dh), 0.02),
        'nsa_cmp_pos': nrm(ks[7], (n_nsa, 2, CMP_LEN, dh), 0.1),
        'nsa_cmp_w1': nrm(ks[8], (n_nsa, 2, CMP_LEN * dh, dh), (CMP_LEN * dh) ** -0.5),
        'nsa_cmp_b1': nrm(ks[9], (n_nsa, 2, dh), 0.02),
        'nsa_cmp_w2': nrm(ks[10], (n_nsa, 2, dh, dh), dh ** -0.5),
        'nsa_w_out': nrm(ks[11], (n_nsa, NSA_HEADS * dh, D_MODEL), (NSA_HEADS * dh) ** -0.5),
        'ml_w_in': nrm(ks[12], (n_ml, D_MODEL, ML_IN), D_MODEL ** -0.5),
        'ml_b_if': b_if,
        'ml_out_norm_g': 1.0 + nrm(ks[13], (n_ml, ML_HEADS * ML_V_DIM), 0.02),
        'ml_w_out': nrm(ks[16], (n_ml, ML_HEADS * ML_V_DIM, D_MODEL), (ML_HEADS * ML_V_DIM) ** -0.5),
        'ffn_w_gate': nrm(ks[17], (DEPTH, D_MODEL, D_FF), D_MODEL ** -0.5),
        'ffn_w_up': nrm(ks[18], (DEPTH, D_MODEL, D_FF), D_MODEL ** -0.5),
        'ffn_w_down': nrm(ks[19], (DEPTH, D_FF, D_MODEL), D_FF ** -0.5),
    }

def reference(x, norm_mix_g, norm_ffn_g, nsa_w_in, nsa_b_gate, nsa_q_norm_g, nsa_k_norm_g,
              nsa_cmp_pos, nsa_cmp_w1, nsa_cmp_b1, nsa_cmp_w2, nsa_w_out,
              ml_w_in, ml_b_if, ml_out_norm_g, ml_w_out,
              ffn_w_gate, ffn_w_up, ffn_w_down):
    for i in range(DEPTH):
        j = i // N_MIXERS
        h = rms_norm(x, norm_mix_g[i])
        if i % N_MIXERS == 0:
            x = x + nsa_mixer(h, nsa_w_in[j], nsa_b_gate[j], nsa_q_norm_g[j], nsa_k_norm_g[j],
                              nsa_cmp_pos[j], nsa_cmp_w1[j], nsa_cmp_b1[j], nsa_cmp_w2[j], nsa_w_out[j])
        else:
            x = x + mlstm_mixer(h, ml_w_in[j], ml_b_if[j], ml_out_norm_g[j], ml_w_out[j])
        h = rms_norm(x, norm_ffn_g[i])
        x = x + swiglu(h, ffn_w_gate[i], ffn_w_up[i], ffn_w_down[i])
    return x


_drawn_inputs = setup_inputs


def setup_inputs(seed=0):
    import zlib

    import numpy as np

    out = dict(_drawn_inputs(seed))
    spreads = {}
    factors = {'norm_mix_g': 8.0,
     'norm_ffn_g': 3.832,
     'nsa_b_gate': 7.011,
     'nsa_q_norm_g': 8.0,
     'nsa_k_norm_g': 8.0,
     'nsa_cmp_b1': 8.0}
    for name, (base, spread) in spreads.items():
        noise = np.random.default_rng([zlib.crc32(name.encode()), seed]).standard_normal(out[name].shape)
        drawn = base * np.exp(spread * noise) if base else spread * noise
        out[name] = __import__('jax').numpy.asarray(drawn.astype(out[name].dtype))
    for name, factor in factors.items():
        out[name] = (out[name] * factor).astype(out[name].dtype)
    return out
```

```python
import concourse.bass as bass
from concourse import mybir
from contextlib import ExitStack

P = 128
S, D = 512, 2048
HEADS, GROUPS, DH = 16, 4, 128
REP = HEADS // GROUPS
CMP_LEN, CMP_STRIDE = 32, 16
N_CMP = (S - CMP_LEN) // CMP_STRIDE + 1
CPAD = 32
SEL_BLOCK, N_SELECT, WINDOW = 64, 16, 512
D_FF = 5632
EPS = 1e-6
MASKED = -2.0 ** 100
FLOOR = -2.0 ** 66

TT = S // P
KD = D // P
QCOL = 0
KVCOL = [HEADS * DH + n * GROUPS * DH for n in range(6)]
GATECOL = HEADS * DH + 6 * GROUPS * DH
NG = 3 * HEADS

UNIT = 1024
RAW, RING = 2, 4
CMP_UNITS = 12
G0, G_UNITS = 2 * CMP_UNITS, 16
O0, O_UNITS = G0 + GROUPS * G_UNITS, 8
F0, F_UNITS = O0 + 4 * O_UNITS, 24
SLABS = D_FF // 512
ALL_UNITS = F0 + SLABS * F_UNITS

assert S // SEL_BLOCK <= N_SELECT and WINDOW >= S


def nsa_swiglu_block(nc, x, mix_g, ffn_g, w_in, b_gate, q_g, k_g, cmp_pos, cmp_w1, cmp_b1, cmp_w2,
                     w_out, w_gate, w_up, w_down, out):
    f32, f32r, bf16 = mybir.dt.float32, mybir.dt.float32r, mybir.dt.bfloat16
    ACT, ALU, AX = mybir.ActivationFunctionType, mybir.AluOpType, mybir.AxisListType
    ctx = ExitStack()
    with ctx:
        def sb(name, shape, dt=f32):
            return ctx.enter_context(nc.sbuf_tensor(name, shape, dt))

        def sem(name):
            return ctx.enter_context(nc.semaphore(name))

        hTh, hTl = sb("hTh", [P, KD, S], f32r), sb("hTl", [P, KD, S], f32r)
        raw = sb("raw", [P, RAW, UNIT])
        wh, wl = sb("wh", [P, RING, UNIT], f32r), sb("wl", [P, RING, UNIT], f32r)
        ot = sb("ot", [P, HEADS, S])
        rows_of_x = ot[:, :, :].rearrange("p a b -> p (a b)").rearrange("p (t d) -> p t d", t=TT)
        x2_at = nc.sbuf_base
        qh, ql = sb("qh", [P, REP, S], f32r), sb("ql", [P, REP, S], f32r)
        kh, kl = sb("kh", [P, 2, S], f32r), sb("kl", [P, 2, S], f32r)
        vh, vl = sb("vh", [P, TT, 2 * DH], f32r), sb("vl", [P, TT, 2 * DH], f32r)
        assert nc.sbuf_base - x2_at == 4 * S * D // P
        x2 = nc.alloc_sbuf_tensor_at("x2", [P, TT, D], f32, offset=x2_at)
        pbuf = sb("pbuf", [P, 2, 2, S])
        pth, ptl = sb("pth", [P, 2, 2, S], f32r), sb("ptl", [P, 2, 2, S], f32r)
        mTh = pth[:, :, :, :].rearrange("p a b c -> p (a b) c")
        mTl = ptl[:, :, :, :].rearrange("p a b c -> p (a b) c")
        ident, ident16 = sb("ident", [P, P]), sb("ident16", [P, P], bf16)
        inv128 = sb("inv128", [P, P])
        neg_half = sb("neg_half", [P, 1])
        causal = sb("causal", [P, P], bf16)
        causal_cmp = sb("causal_cmp", [P, TT, CPAD], bf16)
        rows = sb("rows", [P, P])
        cols = sb("cols", [P, 72])
        gains = sb("gains", [P, 3])
        posh, posl = sb("posh", [P, 66], f32r), sb("posl", [P, 66], f32r)
        bgate = sb("bgate", [P, NG])
        gates = sb("gates", [P, TT, NG])
        gates_g = sb("gates_g", [P, TT, 3 * REP])
        w2 = sb("w2", [P, 2, DH])
        hb = sb("hb", [P, 2])
        hdn = sb("hdn", [P, 2, N_CMP, GROUPS])
        kch, kcl = sb("kch", [P, GROUPS, CPAD], f32r), sb("kcl", [P, GROUPS, CPAD], f32r)
        kcgh, kcgl = sb("kcgh", [P, CPAD], f32r), sb("kcgl", [P, CPAD], f32r)
        vc, vcg = sb("vc", [CPAD, GROUPS, DH]), sb("vcg", [CPAD, DH])
        pc = sb("pc", [P, REP * TT, CPAD])
        ptc = sb("ptc", [CPAD, S])
        rqs = sb("rqs", [P, REP * TT])
        ss, rr = sb("ss", [P, 16]), sb("rr", [P, 4])
        cmx, csum = sb("cmx", [P, REP * TT]), sb("csum", [P, REP * TT])
        nmax, nb, sums, wgt = (sb(n, [P, 2, 2]) for n in ("nmax", "nb", "sums", "wgt"))

        ps = ctx.enter_context(nc.psum_tensor("ps", [P, 8, S], f32))

        def bank(b):
            return ps[:, b, :]

        flat_p = pbuf[:, :, :, :].rearrange("p a b c -> p (a b c)")
        gain_row = flat_p
        sq = [pbuf[:, 0, 0, :], pbuf[:, 0, 1, :]]
        knorm = [pbuf[:, 1, 0, :], pbuf[:, 1, 1, :]]
        x2_flat = x2[:, :, :].rearrange("p t d -> p (t d)")
        wg_raw = x2_flat[:, 0:KD * NG].rearrange("p (k c) -> p k c", k=KD)
        wgh = pth[:, :, :, :].rearrange("p a b c -> p (a b c)")[:, 0:KD * NG].rearrange("p (k c) -> p k c", k=KD)
        wgl = ptl[:, :, :, :].rearrange("p a b c -> p (a b c)")[:, 0:KD * NG].rearrange("p (k c) -> p k c", k=KD)
        cbh = qh[:, :, :].rearrange("p a b -> p (a b)").rearrange("p (l c g) -> p l c g", l=CMP_STRIDE, g=GROUPS)
        cbl = ql[:, :, :].rearrange("p a b -> p (a b)").rearrange("p (l c g) -> p l c g", l=CMP_STRIDE, g=GROUPS)

        rows_loaded, gain_loaded, gain2_loaded = sem("rows_loaded"), sem("gain_loaded"), sem("gain2_loaded")
        wg_loaded, w2_loaded, bgate_loaded = sem("wg_loaded"), sem("w2_loaded"), sem("bgate_loaded")
        x_loaded = [sem(f"x_loaded{t}") for t in range(TT)]
        x2_loaded = sem("x2_loaded")
        raw_loaded = [sem(f"raw_loaded{i}") for i in range(RAW)]
        hi_ready, lo_ready, units_used = sem("hi_ready"), sem("lo_ready"), sem("units_used")
        zeroed, consts_ready, ident16_ready = sem("zeroed"), sem("consts_ready"), sem("ident16_ready")
        vector_done = sem("vector_done")
        ss_done, rms_den, rms_ready, h_ready = sem("ss_done"), sem("rms_den"), sem("rms_ready"), sem("h_ready")
        hT_banks, hT_hi, hT_lo = sem("hT_banks"), sem("hT_hi"), sem("hT_lo")
        rowsT_done, cols_ready = sem("rowsT_done"), sem("cols_ready")
        wg_hi, wg_lo, gates_done = sem("wg_hi"), sem("wg_lo"), sem("gates_done")
        gate_arg, gate_exp, gates_ready = sem("gate_arg"), sem("gate_exp"), sem("gates_ready")
        c_hi, c_lo, hb_ready, gelu_done = sem("c_hi"), sem("c_lo"), sem("hb_ready"), sem("gelu_done")
        kc_done, kc_sq, kcsum_done, kc_den = sem("kc_done"), sem("kc_sq"), sem("kcsum_done"), sem("kc_den")
        kc_inv, kc_ready, kc_hi, kc_lo = sem("kc_inv"), sem("kc_ready"), sem("kc_hi"), sem("kc_lo")
        vc_done, vc_ready, group_ready = sem("vc_done"), sem("vc_ready"), sem("group_ready")
        q_hi, q_lo, sq_ready = sem("q_hi"), sem("q_lo"), sem("sq_ready")
        rq_done, rq_den, rq_ready = sem("rq_done"), sem("rq_den"), sem("rq_ready")
        ksum_done, k_den, k_inv, k_norm = sem("ksum_done"), sem("k_den"), sem("k_inv"), sem("k_norm")
        k_hi, k_lo, v_hi, v_lo = sem("k_hi"), sem("k_lo"), sem("v_hi"), sem("v_lo")
        cs_done, cs_ready, c_exp, pc_ready = sem("cs_done"), sem("cs_ready"), sem("c_exp"), sem("pc_ready")
        trc_done, ptc_ready = sem("trc_done"), sem("ptc_ready")
        s_done, nb_ready, exp_done, p_ready = sem("s_done"), sem("nb_ready"), sem("exp_done"), sem("p_ready")
        tr_done, pt_hi, pt_lo, pv_done, o_ready = (sem(n) for n in ("tr_done", "pt_hi", "pt_lo", "pv_done", "o_ready"))
        o_hi, o_lo, x2_added, x2_sq = sem("o_hi"), sem("o_lo"), sem("x2_added"), sem("x2_sq")
        silu_done, m_ready, m_hi, m_lo = sem("silu_done"), sem("m_ready"), sem("m_hi"), sem("m_lo")
        y_added, stored = sem("y_added"), sem("stored")

        w_in_v = w_in[0].rearrange("(q k p) c -> q p k c", k=4, p=P)
        w_gate_v = w_gate[0].rearrange("(q k p) c -> q p k c", k=4, p=P)
        w_up_v = w_up[0].rearrange("(q k p) c -> q p k c", k=4, p=P)
        w1_v = cmp_w1[0].rearrange("t (j l p) c -> t j p l c", l=8, p=P)
        w_out_v = w_out[0].rearrange("(q k p) c -> q p k c", k=2, p=P)
        w_down_v = w_down[0].rearrange("(q k p) c -> p q k c", k=2, p=P)

        def wait(eng, s, base, per=0, i=None):
            eng.wait_ge(s, base if i is None or per == 0 else i * per + base)

        class Own:
            def __init__(self, eng):
                self.eng, self.base, self.local, self.per, self.i = eng, 0, 0, 0, None

            def done(self, ins):
                ins.then_inc(vector_done, 1)
                self.local += 1

            def settle(self):
                wait(self.eng, vector_done, self.base + self.local, self.per, self.i)

            def enter(self, i, per):
                self.base += self.local
                self.local, self.per, self.i = 0, per, i

            def leave(self, turns):
                assert self.local == self.per, (self.local, self.per)
                self.base += turns * self.per
                self.local, self.per, self.i = 0, 0, None

        block = ctx.enter_context(nc.Block())

        @block.sync
        def _(sp):
            def unit(n, halves, per=0, i=None):
                if n >= RAW:
                    wait(sp, lo_ready, n - RAW + 1, per, i)
                for dst, src in halves:
                    sp.dma_start(dst, src).then_inc(raw_loaded[n % RAW], 16)

            def k_halves(n, src, k):
                dst = raw[:, n % RAW, :].rearrange("p (k c) -> p k c", k=k)
                return [(dst[:, a:a + k // 2, :], src[:, a:a + k // 2, :]) for a in (0, k // 2)]

            def column_halves(n, src_a, src_b):
                dst = raw[:, n % RAW, :].rearrange("p (k c) -> p k c", k=4)
                return [(dst[:, :, 0:P], src_a), (dst[:, :, P:2 * P], src_b)]

            for t in range(TT):
                sp.dma_start(rows_of_x[:, t, :], x[0, t * P:(t + 1) * P, :]).then_inc(x_loaded[t], 16)
                if t == 0:
                    sp.dma_start(gain_row, mix_g.to_broadcast([P, D])).then_inc(gain_loaded, 16)
            for ty in range(2):
                n = ty * CMP_UNITS
                for b in range(2):
                    for q in range(4):
                        c = KVCOL[ty] + b * 256
                        unit(n, k_halves(n, w_in_v[q][:, :, c:c + 256], 4))
                        n += 1
                for j in range(4):
                    unit(n, k_halves(n, w1_v[ty, j], 8))
                    n += 1
            with sp.Fori(0, GROUPS) as g:
                for b in range(2):
                    for q in range(4):
                        n = G0 + 4 * b + q
                        unit(n, k_halves(n, w_in_v[q][:, :, bass.ds(g * (REP * DH) + (QCOL + b * 256), 256)], 4),
                             G_UNITS, g)
                for b, (ca, cb) in enumerate(((KVCOL[2], KVCOL[4]), (KVCOL[3], KVCOL[5]))):
                    for q in range(4):
                        n = G0 + 8 + 4 * b + q
                        unit(n, column_halves(n, w_in_v[q][:, :, bass.ds(g * DH + ca, DH)],
                                              w_in_v[q][:, :, bass.ds(g * DH + cb, DH)]), G_UNITS, g)
            with sp.Fori(0, 4) as c:
                for q in range(O_UNITS):
                    n = O0 + q
                    unit(n, k_halves(n, w_out_v[q][:, :, bass.ds(c * 512, 512)], 2), O_UNITS, c)
            with sp.Fori(0, SLABS) as s:
                for b in range(2):
                    for q in range(4):
                        for u, w in enumerate((w_gate_v, w_up_v)):
                            n = F0 + 8 * b + 2 * q + u
                            unit(n, k_halves(n, w[q][:, :, bass.ds(s * 512 + b * 256, 256)], 4), F_UNITS, s)
                for c in range(4):
                    for q in range(2):
                        n = F0 + 16 + 2 * c + q
                        src = w_down_v[:, bass.ds(s * 2 + q, 1), :, c * 512:(c + 1) * 512]
                        unit(n, k_halves(n, src.rearrange("p q k c -> p (q k) c"), 2), F_UNITS, s)
            out_v = out[0].rearrange("(t p) d -> p t d", p=P)
            for c in range(4):
                wait(sp, y_added, (SLABS - 1) * 16 + 4 * (c + 1))
                sp.dma_start(out_v[:, :, c * 512:(c + 1) * 512], x2[:, :, c * 512:(c + 1) * 512])\
                  .then_inc(stored, 16)
            sp.wait_ge(stored, 64)

        @block.gpsimd
        def _(pool):
            pool.dma_start(rows[0:64, :], cmp_pos[0].rearrange("t l d -> (t l) d")).then_inc(rows_loaded, 16)
            pool.dma_start(rows[64:66, :], cmp_b1[0]).then_inc(rows_loaded, 16)
            pool.dma_start(rows[66:67, :], q_g).then_inc(rows_loaded, 16)
            pool.dma_start(rows[67:70, :], k_g[0]).then_inc(rows_loaded, 16)
            pool.dma_start(bgate[:, :], b_gate.to_broadcast([P, NG])).then_inc(bgate_loaded, 16)
            pool.dma_start(wg_raw, w_in[0].rearrange("(k p) c -> p k c", p=P)[:, :, GATECOL:GATECOL + NG])\
                .then_inc(wg_loaded, 16)
            pool.dma_start(w2[:, :, :], cmp_w2[0].rearrange("t p d -> p t d")).then_inc(w2_loaded, 16)
            pool.memset(ident[:, :], 0.0).then_inc(zeroed, 1)
            pool.memset(causal[:, :], 0.0).then_inc(zeroed, 1)
            pool.memset(causal_cmp[:, :, :], 0.0).then_inc(zeroed, 1)
            pool.memset(inv128[:, :], 1.0 / P).then_inc(zeroed, 1)
            pool.memset(neg_half[:, :], -0.5).then_inc(zeroed, 1)
            pool.memset(kch[:, :, :].bitcast(f32), 0.0).then_inc(zeroed, 1)
            pool.memset(kcl[:, :, :].bitcast(f32), 0.0).then_inc(zeroed, 1)
            pool.memset(vc[:, :, :], 0.0).then_inc(zeroed, 1)
            pool.wait_ge(zeroed, 8)
            pool.affine_select(out=ident[:, :], in_=ident[:, :], compare_op=ALU.not_equal, fill=1.0, base=0,
                               pattern=[[-1, P]], channel_multiplier=1).then_inc(consts_ready, 1)
            pool.affine_select(out=causal[:, :], in_=causal[:, :], compare_op=ALU.is_ge, fill=MASKED, base=0,
                               pattern=[[-1, P]], channel_multiplier=1).then_inc(consts_ready, 1)
            pool.affine_select(out=causal_cmp[:, :, :], in_=causal_cmp[:, :, :], compare_op=ALU.is_ge,
                               fill=MASKED, base=-(CMP_LEN - 1), pattern=[[P, TT], [-CMP_STRIDE, CPAD]],
                               channel_multiplier=1).then_inc(consts_ready, 1)

            def inv_root(ap, m, done):
                pool.tensor_tensor(ap, ap, neg_half[:, 0:1].to_broadcast([P, m]), ALU.pow).then_inc(done, 1)

            for t in range(TT):
                pool.wait_ge(rms_den, t + 1)
                inv_root(rr[:, t:t + 1], 1, rms_ready)
            pool.wait_ge(kc_den, 1)
            inv_root(knorm[0][:, 0:N_CMP * GROUPS], N_CMP * GROUPS, kc_inv)
            with pool.Fori(0, GROUPS) as g:
                wait(pool, rq_den, 1, 1, g)
                inv_root(rqs[:, :], REP * TT, rq_ready)
                for b in range(2):
                    wait(pool, k_den, b + 1, 2, g)
                    inv_root(knorm[b], S, k_inv)
            pool.wait_ge(o_ready, HEADS)
            pool.dma_start(x2[:, :, :], x[0].rearrange("(t p) d -> p t d", p=P)).then_inc(x2_loaded, 16)
            pool.wait_ge(x2_sq, 16)
            pool.dma_start(gain_row, ffn_g.to_broadcast([P, D])).then_inc(gain2_loaded, 16)
            pool.wait_ge(rms_den, TT + 1)
            inv_root(rr[:, :], TT, rms_ready)

        @block.scalar
        def _(act):
            def copy(dst, src):
                return nc.scalar.activation(dst, src, ACT.Copy)

            def split(n, per=0, i=None):
                wait(act, raw_loaded[n % RAW], 32 * (n // RAW + 1), 32 * per // RAW, i)
                if n >= RING:
                    wait(act, units_used, n - RING + 1, per, i)
                copy(wh[:, n % RING, :], raw[:, n % RAW, :]).then_inc(hi_ready, 1)

            def hT_part(first):
                for t in range(TT):
                    for q in range(4):
                        n = first + 4 * t + q
                        act.wait_ge(hT_banks, n + 1)
                        copy(hTh[:, 4 * q:4 * q + 4, t * P:(t + 1) * P],
                             bank(4 * (t % 2) + q).rearrange("p (k c) -> p k c", k=4)).then_inc(hT_hi, 1)

            for t in range(TT):
                act.wait_ge(x_loaded[t], 16)
                if t >= 1:
                    act.wait_ge(ss_done, t)
                nc.scalar.activation(x2[:, 3, :], rows_of_x[:, t, :], ACT.Square,
                                     accum_out=ss[:, t:t + 1]).then_inc(ss_done, 1)
            act.wait_ge(wg_loaded, 16)
            copy(wgh, wg_raw).then_inc(wg_hi, 1)
            hT_part(0)
            for n in range(RING):
                split(n)
            act.wait_ge(gate_arg, 1)
            nc.scalar.activation(gates[:, :, :], gates[:, :, :], ACT.Exp, scale=-1.0).then_inc(gate_exp, 1)
            for ty in range(2):
                for j in range(CMP_UNITS):
                    n = ty * CMP_UNITS + j
                    if j in (3, 7):
                        act.wait_ge(units_used, n + 1)
                        for grp in ((j - 3) // 2, (j - 3) // 2 + 1):
                            src = bank(grp).rearrange("p (c l) -> p l c", l=CMP_STRIDE)
                            copy(cbh[:, :, :, grp], src).then_inc(c_hi, 1)
                    split(n + RING)
                    if n == CMP_UNITS:
                        act.wait_ge(kc_done, 1)
                        nc.scalar.activation(sq[0][:, 0:N_CMP * GROUPS], bank(6)[:, 0:N_CMP * GROUPS],
                                             ACT.Square).then_inc(kc_sq, 1)
                    if n == CMP_UNITS + 4:
                        act.wait_ge(kc_ready, 1)
                        copy(kch[:, :, 0:N_CMP],
                             knorm[1][:, 0:N_CMP * GROUPS].rearrange("p (c g) -> p g c", g=GROUPS))\
                            .then_inc(kc_hi, 1)
                    if j == CMP_UNITS - 1:
                        act.wait_ge(hb_ready, ty + 1)
                        nc.scalar.activation(hdn[:, ty, :, :].rearrange("p c g -> p (c g)"),
                                             bank(4)[:, 0:N_CMP * GROUPS], ACT.Gelu_apprx_tanh,
                                             bias=hb[:, ty:ty + 1]).then_inc(gelu_done, 1)
            with act.Fori(0, GROUPS) as g:
                for j in range(G_UNITS):
                    n = G0 + j
                    if j in (3, 7):
                        wait(act, units_used, n + 1, G_UNITS, g)
                        if j == 7:
                            wait(act, rq_done, 1, 2, g)
                        for h in ((j - 3) // 2, (j - 3) // 2 + 1):
                            copy(qh[:, h, :], bank(h)).then_inc(q_hi, 1)
                            nc.scalar.activation(sq[h % 2], bank(h), ACT.Square).then_inc(sq_ready, 1)
                    if j == 11:
                        wait(act, units_used, n + 1, G_UNITS, g)
                        wait(act, rq_done, 2, 2, g)
                        for b in range(2):
                            nc.scalar.activation(sq[b], bank(4 + b), ACT.Square).then_inc(sq_ready, 1)
                    if j == 15:
                        wait(act, units_used, n + 1, G_UNITS, g)
                        for t in range(TT):
                            copy(vh[:, t, :], bank(t)[:, 0:2 * DH]).then_inc(v_hi, 1)
                    split(n + RING, G_UNITS, g)
                    if j == 14:
                        for b in range(2):
                            wait(act, k_norm, b + 1, 2, g)
                            copy(kh[:, b, :], knorm[b]).then_inc(k_hi, 1)
                wait(act, rq_ready, 1, 1, g)
                wait(act, cs_ready, 1, 1, g)
                nc.scalar.activation(pc[:, :, :], pc[:, :, :], ACT.Exp).then_inc(c_exp, 1)

                def probs(i):
                    nk = (i % TT + 1) * P
                    wait(act, nb_ready, i + 1, 16, g)
                    for b in range(2):
                        nc.scalar.activation(pbuf[:, i % 2, b, 0:nk], bank(2 + 2 * (i % 2) + b)[:, 0:nk], ACT.Exp,
                                             bias=nb[:, i % 2, b:b + 1], scale=rqs[:, i:i + 1],
                                             accum_out=sums[:, i % 2, b:b + 1]).then_inc(exp_done, 1)

                def pt_part(i):
                    nk = (i % TT + 1) * P
                    wait(act, tr_done, i + 1, 16, g)
                    if i >= 2:
                        wait(act, pv_done, i - 1, 16, g)
                    copy(pth[:, i % 2, :, 0:nk], ps[:, 6:8, 0:nk]).then_inc(pt_hi, 1)

                def head_out(h):
                    wait(act, pv_done, TT * h + TT, 16, g)
                    copy(ot[:, bass.ds(g * REP + h, 1), :].rearrange("p a b -> p (a b)"), bank(1))\
                        .then_inc(o_ready, 1)

                for i in range(REP * TT + 1):
                    if i < REP * TT:
                        probs(i)
                    if i >= 1:
                        pt_part(i - 1)
                        if i > TT and (i - 1) % TT == 0:
                            head_out((i - 1) // TT - 1)
                head_out(REP - 1)
            act.wait_ge(o_ready, HEADS)
            for q in range(HEADS // 2):
                copy(hTh[:, 2 * q:2 * q + 2, :], ot[:, 2 * q:2 * q + 2, :]).then_inc(o_hi, 1)
            with act.Fori(0, 2) as cc:
                for c in range(2):
                    for q in range(O_UNITS):
                        split(O0 + c * O_UNITS + q + RING, 2 * O_UNITS, cc)
                    for t in range(TT):
                        wait(act, x2_added, 4 * c + t + 1, 8, cc)
                        if c or t:
                            wait(act, x2_sq, 4 * c + t, 8, cc)
                        nc.scalar.activation(flat_p[:, 0:512], x2[:, t, bass.ds(cc * 1024 + c * 512, 512)], ACT.Square,
                                             accum_out=ss[:, bass.ds(cc * 8 + 4 * c + t, 1)]).then_inc(x2_sq, 1)
            hT_part(16)
            def slab(s, last):
                for j in range(F_UNITS):
                    n = F0 + j
                    if j in (6, 14):
                        wait(act, units_used, n + 1, F_UNITS, s)
                        for c in range(2):
                            nc.scalar.activation(flat_p[:, c * 512:(c + 1) * 512], bank(j // 8 * 4 + c), ACT.Silu)\
                                .then_inc(silu_done, 1)
                    if j in (7, 15):
                        for c in range(2):
                            wait(act, m_ready, (j - 7) // 4 + c + 1, 4, s)
                            copy(mTh[:, (j - 7) // 4 + c, :], flat_p[:, 1024 + c * 512:1536 + c * 512])\
                                .then_inc(m_hi, 1)
                    if not last or j + RING < F_UNITS:
                        split(n + RING, F_UNITS, s)

            with act.Fori(0, SLABS - 1) as s:
                slab(s, False)
            slab(SLABS - 1, True)

        @block.vector
        def _(dve):
            own = Own(dve)

            def lo(dst, src, hi, done):
                nc.vector.tensor_tensor(dst, src, hi.bitcast(f32), ALU.subtract).then_inc(done, 1)

            def split(n, per=0, i=None):
                wait(dve, hi_ready, n + 1, per, i)
                lo(wl[:, n % RING, :], raw[:, n % RAW, :], wh[:, n % RING, :], lo_ready)

            def hT_part(first):
                for t in range(TT):
                    for q in range(4):
                        dve.wait_ge(hT_hi, first + 4 * t + q + 1)
                        at = (slice(None), slice(4 * q, 4 * q + 4), slice(t * P, (t + 1) * P))
                        lo(hTl[at], bank(4 * (t % 2) + q).rearrange("p (k c) -> p k c", k=4), hTh[at], hT_lo)

            dve.wait_ge(consts_ready, 1)
            nc.vector.tensor_copy(ident16[:, :], ident[:, :]).then_inc(ident16_ready, 1)
            for t in range(TT):
                dve.wait_ge(ss_done, t + 1)
                nc.vector.tensor_scalar(rr[:, t:t + 1], ss[:, t:t + 1], 1.0 / D, EPS, ALU.mult, ALU.add)\
                    .then_inc(rms_den, 1)
                if t == 0:
                    dve.wait_ge(gain_loaded, 16)
                dve.wait_ge(rms_ready, t + 1)
                nc.vector.scalar_tensor_tensor(out=rows_of_x[:, t, :], in0=rows_of_x[:, t, :], scalar=rr[:, t:t + 1],
                                               in1=gain_row, op0=ALU.mult, op1=ALU.mult).then_inc(h_ready, 1)
            dve.wait_ge(rowsT_done, 1)
            own.done(nc.vector.tensor_copy(cols[:, 0:70], bank(0)[:, 0:70]))
            own.settle()
            nc.vector.tensor_copy(posh[:, :], cols[:, 0:66]).then_inc(cols_ready, 1)
            own.done(nc.vector.tensor_scalar(gains[:, :], cols[:, 67:70], cols[:, 66:67], None, ALU.mult))
            dve.wait_ge(cols_ready, 1)
            lo(posl[:, :], cols[:, 0:66], posh[:, :], cols_ready)
            dve.wait_ge(wg_hi, 1)
            lo(wgl, wg_raw, wgh, wg_lo)
            hT_part(0)
            for n in range(RING):
                split(n)
            dve.wait_ge(gates_done, 1)
            dve.wait_ge(bgate_loaded, 16)
            nc.vector.tensor_tensor(gates[:, :, :], bank(4)[:, 0:TT * NG].rearrange("p (t c) -> p t c", t=TT),
                                    bgate[:, :].rearrange("p (a c) -> p a c", a=1).to_broadcast([P, TT, NG]),
                                    ALU.add).then_inc(gate_arg, 1)
            dve.wait_ge(gate_exp, 1)
            own.done(nc.vector.tensor_scalar_add(gates[:, :, :], gates[:, :, :], 1.0))
            own.settle()
            nc.vector.reciprocal(gates[:, :, :], gates[:, :, :]).then_inc(gates_ready, 1)
            NC4 = N_CMP * GROUPS
            for ty in range(2):
                for j in range(CMP_UNITS):
                    n = ty * CMP_UNITS + j
                    if j in (3, 7):
                        for grp in ((j - 3) // 2, (j - 3) // 2 + 1):
                            dve.wait_ge(c_hi, 4 * ty + grp + 1)
                            src = bank(grp).rearrange("p (c l) -> p l c", l=CMP_STRIDE)
                            lo(cbl[:, :, :, grp], src, cbh[:, :, :, grp], c_lo)
                    split(n + RING)
                    if n == CMP_UNITS + 3:
                        dve.wait_ge(kcsum_done, 1)
                        nc.vector.tensor_scalar_add(knorm[0][:, 0:NC4], bank(7)[:, 0:NC4], EPS).then_inc(kc_den, 1)
                        dve.wait_ge(kc_inv, 1)
                        nc.vector.scalar_tensor_tensor(out=knorm[1][:, 0:NC4], in0=bank(6)[:, 0:NC4],
                                                       scalar=gains[:, 0:1], in1=knorm[0][:, 0:NC4],
                                                       op0=ALU.mult, op1=ALU.mult).then_inc(kc_ready, 1)
                    if n == CMP_UNITS + 4:
                        dve.wait_ge(kc_hi, 1)
                        lo(kcl[:, :, 0:N_CMP], knorm[1][:, 0:NC4].rearrange("p (c g) -> p g c", g=GROUPS),
                           kch[:, :, 0:N_CMP], kc_lo)
                    if j == CMP_UNITS - 1:
                        dve.wait_ge(units_used, n + 1)
                        nc.vector.tensor_tensor(hb[:, ty:ty + 1], bank(5)[:, 0:1], cols[:, 64 + ty:65 + ty],
                                                ALU.add).then_inc(hb_ready, 1)
            dve.wait_ge(vc_done, 1)
            nc.vector.tensor_copy(vc[0:N_CMP, :, :],
                                  bank(6)[0:N_CMP, :].rearrange("p (g d) -> p g d", g=GROUPS)).then_inc(vc_ready, 1)
            dve.wait_ge(vc_ready, 1)
            dve.wait_ge(kc_lo, 1)
            dve.wait_ge(gates_ready, 1)
            with dve.Fori(0, GROUPS) as g:
                own.enter(g, DVE_GROUP)
                for j in range(G_UNITS):
                    n = G0 + j
                    if j in (3, 7):
                        for h in ((j - 3) // 2, (j - 3) // 2 + 1):
                            wait(dve, sq_ready, h + 1, 6, g)
                            lo(ql[:, h, :], bank(h), qh[:, h, :], q_lo)
                    if j == 3:
                        own.done(nc.vector.tensor_copy(kcgh[:, :], kch[:, bass.ds(g, 1), :].bitcast(f32)
                                                       .rearrange("p a c -> p (a c)")))
                        own.done(nc.vector.tensor_copy(kcgl[:, :], kcl[:, bass.ds(g, 1), :].bitcast(f32)
                                                       .rearrange("p a c -> p (a c)")))
                        own.done(nc.vector.tensor_copy(gates_g[:, :, :], gates[:, :, bass.ds(g * (3 * REP), 3 * REP)]))
                        nc.vector.tensor_copy(vcg[:, :], vc[:, bass.ds(g, 1), :].rearrange("p a d -> p (a d)"))\
                            .then_inc(group_ready, 1)
                    if j == 13:
                        wait(dve, rq_done, 2, 2, g)
                        nc.vector.tensor_scalar(rqs[:, :], bank(6)[:, 0:REP * TT], EPS, float(DH),
                                                ALU.add, ALU.mult).then_inc(rq_den, 1)
                        for b in range(2):
                            wait(dve, ksum_done, b + 1, 2, g)
                            nc.vector.tensor_scalar_add(knorm[b], bank(7 - b), EPS).then_inc(k_den, 1)
                    if j == 14:
                        for b in range(2):
                            wait(dve, k_inv, b + 1, 2, g)
                            nc.vector.scalar_tensor_tensor(out=knorm[b], in0=bank(4 + b), scalar=gains[:, 1 + b:2 + b],
                                                           in1=knorm[b], op0=ALU.mult, op1=ALU.mult)\
                                .then_inc(k_norm, 1)
                    if j == 15:
                        for t in range(TT):
                            wait(dve, v_hi, t + 1, 4, g)
                            lo(vl[:, t, :], bank(t)[:, 0:2 * DH], vh[:, t, :], v_lo)
                    split(n + RING, G_UNITS, g)
                    if j == 14:
                        for b in range(2):
                            wait(dve, k_hi, b + 1, 2, g)
                            lo(kl[:, b, :], knorm[b], kh[:, b, :], k_lo)
                wait(dve, cs_done, 1, 1, g)
                sc = bank(0).rearrange("p (i c) -> p i c", c=CPAD)

                def each(ap):
                    return ap.rearrange("p (i a) -> p i a", a=1).to_broadcast([P, REP * TT, CPAD])

                own.done(nc.vector.reduce_max(cmx[:, :], sc, axis=AX.X))
                own.settle()
                own.done(nc.vector.tensor_scalar_max(cmx[:, :], cmx[:, :], FLOOR))
                own.settle()
                own.done(nc.vector.tensor_tensor(pc[:, :, :], sc, each(cmx[:, :]), ALU.subtract))
                own.settle()
                wait(dve, rq_ready, 1, 1, g)
                nc.vector.tensor_tensor(pc[:, :, :], pc[:, :, :], each(rqs[:, :]), ALU.mult).then_inc(cs_ready, 1)
                wait(dve, c_exp, 1, 1, g)
                own.done(nc.vector.reduce_sum(csum[:, :], pc[:, :, :], axis=AX.X))
                own.settle()
                own.done(nc.vector.tensor_scalar_max(csum[:, :], csum[:, :], 1e-30))
                own.settle()
                own.done(nc.vector.reciprocal(csum[:, :], csum[:, :]))
                own.settle()
                gate3 = gates_g[:, :, :].rearrange("p t (h b) -> p h t b", b=3)
                own.done(nc.vector.tensor_tensor(csum[:, :].rearrange("p (h t) -> p h t", h=REP),
                                                 csum[:, :].rearrange("p (h t) -> p h t", h=REP),
                                                 gate3[:, :, :, 0], ALU.mult))
                own.settle()
                nc.vector.tensor_tensor(pc[:, :, :], pc[:, :, :], each(csum[:, :]), ALU.mult).then_inc(pc_ready, 1)

                def maximum(i):
                    nk = (i % TT + 1) * P
                    e = i % 2
                    wait(dve, s_done, i + 1, 16, g)
                    own.done(nc.vector.tensor_reduce(nmax[:, e, :], ps[:, 2 + 2 * e:4 + 2 * e, 0:nk], AX.X, ALU.max,
                                                     negate=True))
                    own.settle()
                    nc.vector.tensor_scalar(nb[:, e, :], nmax[:, e, :], rqs[:, i:i + 1], None, ALU.mult)\
                        .then_inc(nb_ready, 1)

                def weigh(i):
                    nk = (i % TT + 1) * P
                    e, h, t = i % 2, i // TT, i % TT
                    wait(dve, exp_done, 2 * i + 2, 32, g)
                    own.done(nc.vector.tensor_scalar_max(wgt[:, e, :], sums[:, e, :], 1e-30))
                    own.settle()
                    own.done(nc.vector.reciprocal(wgt[:, e, :], wgt[:, e, :]))
                    own.settle()
                    own.done(nc.vector.tensor_tensor(wgt[:, e, :], wgt[:, e, :], gates_g[:, t, 3 * h + 1:3 * h + 3],
                                                     ALU.mult))
                    own.settle()
                    nc.vector.tensor_scalar(pbuf[:, e, 0, 0:nk], pbuf[:, e, 0, 0:nk], wgt[:, e, 0:1], None, ALU.mult)\
                        .then_inc(p_ready, 1)
                    nc.vector.tensor_scalar(pbuf[:, e, 1, 0:nk], pbuf[:, e, 1, 0:nk], wgt[:, e, 1:2], None, ALU.mult)\
                        .then_inc(p_ready, 1)

                def pt_part(i):
                    nk = (i % TT + 1) * P
                    wait(dve, pt_hi, i + 1, 16, g)
                    lo(ptl[:, i % 2, :, 0:nk], ps[:, 6:8, 0:nk], pth[:, i % 2, :, 0:nk], pt_lo)

                for i in range(REP * TT + 2):
                    if i < REP * TT:
                        maximum(i)
                    if 1 <= i <= REP * TT:
                        weigh(i - 1)
                    if i % TT == 1 and i < REP * TT:
                        wait(dve, trc_done, i // TT + 1, 4, g)
                        nc.vector.tensor_copy(ptc[:, :], bank(0)[0:CPAD, :]).then_inc(ptc_ready, 1)
                    if i >= 2:
                        pt_part(i - 2)
            own.leave(GROUPS)
            for q in range(HEADS // 2):
                dve.wait_ge(o_hi, q + 1)
                lo(hTl[:, 2 * q:2 * q + 2, :], ot[:, 2 * q:2 * q + 2, :], hTh[:, 2 * q:2 * q + 2, :], o_lo)
            dve.wait_ge(x2_loaded, 16)
            with dve.Fori(0, 2) as cc:
                for c in range(2):
                    for q in range(O_UNITS):
                        if q == O_UNITS - 1:
                            wait(dve, units_used, O0 + c * O_UNITS + q + 1, 2 * O_UNITS, cc)
                            for t in range(TT):
                                at = x2[:, t, bass.ds(cc * 1024 + c * 512, 512)]
                                nc.vector.tensor_tensor(at, at, bank(4 * c + t), ALU.add).then_inc(x2_added, 1)
                        split(O0 + c * O_UNITS + q + RING, 2 * O_UNITS, cc)
            dve.wait_ge(x2_sq, 16)
            own.done(nc.vector.reduce_sum(rr[:, :], ss[:, :].rearrange("p (c t) -> p t c", t=TT), axis=AX.X))
            own.settle()
            nc.vector.tensor_scalar(rr[:, :], rr[:, :], 1.0 / D, EPS, ALU.mult, ALU.add).then_inc(rms_den, 1)
            dve.wait_ge(rms_ready, TT + 1)
            dve.wait_ge(gain2_loaded, 16)
            for t in range(TT):
                nc.vector.scalar_tensor_tensor(out=rows_of_x[:, t, :], in0=x2[:, t, :], scalar=rr[:, t:t + 1],
                                               in1=gain_row, op0=ALU.mult, op1=ALU.mult).then_inc(h_ready, 1)
            hT_part(16)

            def slab(s, last):
                for j in range(F_UNITS):
                    n = F0 + j
                    if j in (7, 15):
                        wait(dve, units_used, n + 1, F_UNITS, s)
                        k = (j - 7) // 4
                        for c in range(2):
                            wait(dve, silu_done, k + c + 1, 4, s)
                            nc.vector.tensor_tensor(flat_p[:, 1024 + c * 512:1536 + c * 512],
                                                    flat_p[:, c * 512:(c + 1) * 512], bank(j // 8 * 4 + 2 + c), ALU.mult)\
                                .then_inc(m_ready, 1)
                        for c in range(2):
                            wait(dve, m_hi, k + c + 1, 4, s)
                            lo(mTl[:, k + c, :], flat_p[:, 1024 + c * 512:1536 + c * 512], mTh[:, k + c, :], m_lo)
                    if j > 16 and j % 2:
                        wait(dve, units_used, n + 1, F_UNITS, s)
                        c = (j - 17) // 2
                        for t in range(TT):
                            at = x2[:, t, c * 512:(c + 1) * 512]
                            nc.vector.tensor_tensor(at, at, bank(4 * (c % 2) + t), ALU.add).then_inc(y_added, 1)
                    if not last or j + RING < F_UNITS:
                        split(n + RING, F_UNITS, s)

            with dve.Fori(0, SLABS - 1) as s:
                slab(s, False)
            slab(SLABS - 1, True)

        @block.tensor
        def _(pe):
            def mm(out_, a, b, start=False, stop=False):
                return nc.tensor.matmul(out_, a, b, start=start, stop=stop, skip_group_check=True)

            def mm3(out_, a, b, start, stop):
                mm(out_, a[0], b[0], start=start)
                mm(out_, a[0], b[1])
                return mm(out_, a[1], b[0], stop=stop)

            def arrive(n, per=0, i=None):
                wait(pe, lo_ready, n + 1, per, i)

            def columns_unit(n, q, banks):
                for half, bk in enumerate(banks):
                    for kk in range(4):
                        k, at = 4 * q + kk, slice(kk * 256 + half * P, kk * 256 + half * P + P)
                        last = mm3(bank(bk), (wh[:, n % RING, at], wl[:, n % RING, at]), (hTh[:, k, :], hTl[:, k, :]),
                                   k == 0, k == KD - 1)
                last.then_inc(units_used, 1)

            def tokens_unit(n, q, kc, width, ah, al, banks, k_all):
                for t in range(TT):
                    for kk in range(kc):
                        k, at = kc * q + kk, slice(kk * width, (kk + 1) * width)
                        ts = slice(t * P, (t + 1) * P)
                        last = mm3(bank(banks[t])[:, 0:width], (ah[:, k, ts], al[:, k, ts]),
                                   (wh[:, n % RING, at], wl[:, n % RING, at]), k == 0, k == k_all - 1)
                last.then_inc(units_used, 1)

            def transposed_tiles(first):
                for t in range(TT):
                    pe.wait_ge(h_ready, first // 4 + t + 1)
                    for q in range(4):
                        n = first + 4 * t + q
                        if t >= 2:
                            pe.wait_ge(hT_lo, n - 8 + 1)
                        elif first == 0 and t == 0 and q == 0:
                            pe.wait_ge(cols_ready, 1)
                        for kk in range(4):
                            k = 4 * q + kk
                            last = nc.tensor.transpose(bank(4 * (t % 2) + q)[:, kk * P:(kk + 1) * P],
                                                       rows_of_x[:, t, k * P:(k + 1) * P], ident[:, :])
                        last.then_inc(hT_banks, 1)

            pe.wait_ge(consts_ready, 3)
            pe.wait_ge(zeroed, 8)
            pe.wait_ge(rows_loaded, 64)
            nc.tensor.transpose(bank(0)[:, 0:70], rows[0:70, :], ident[0:70, 0:70]).then_inc(rowsT_done, 1)
            transposed_tiles(0)
            pe.wait_ge(hT_lo, 16)
            pe.wait_ge(wg_lo, 1)
            for t in range(TT):
                ts = slice(t * P, (t + 1) * P)
                for k in range(KD):
                    last = mm3(bank(4)[:, t * NG:(t + 1) * NG], (hTh[:, k, ts], hTl[:, k, ts]),
                               (wgh[:, k, :], wgl[:, k, :]), k == 0, k == KD - 1)
            last.then_inc(gates_done, 1)
            pe.wait_ge(cols_ready, 2)
            for ty in range(2):
                for j in range(CMP_UNITS):
                    n = ty * CMP_UNITS + j
                    arrive(n)
                    if j < 8:
                        columns_unit(n, j % 4, (2 * (j // 4), 2 * (j // 4) + 1))
                    else:
                        if j == 8:
                            pe.wait_ge(c_lo, 4 * ty + 4)
                            pe.wait_ge(gelu_done, 1) if ty else pe.wait_ge(gate_arg, 1)
                        for ll in range(8):
                            l = 8 * (j - 8) + ll
                            o, e = l % CMP_STRIDE, l // CMP_STRIDE
                            at = slice(ll * P, (ll + 1) * P)
                            w = (wh[:, n % RING, at], wl[:, n % RING, at])
                            mm3(bank(4)[:, 0:N_CMP * GROUPS], w,
                                (cbh[:, o, e:e + N_CMP, :].rearrange("p c g -> p (c g)"),
                                 cbl[:, o, e:e + N_CMP, :].rearrange("p c g -> p (c g)")), l == 0, l == CMP_LEN - 1)
                            p0 = ty * CMP_LEN + l
                            last = mm3(bank(5)[:, 0:2], w, (posh[:, p0:p0 + 2], posl[:, p0:p0 + 2]),
                                       l == 0, l == CMP_LEN - 1)
                        last.then_inc(units_used, 1)
                    if n == CMP_UNITS:
                        pe.wait_ge(gelu_done, 1)
                        pe.wait_ge(w2_loaded, 16)
                        mm(bank(6)[:, 0:N_CMP * GROUPS], w2[:, 0, :], hdn[:, 0, :, :].rearrange("p c g -> p (c g)"),
                           True, True).then_inc(kc_done, 1)
                    if n == CMP_UNITS + 2:
                        pe.wait_ge(kc_sq, 1)
                        mm(bank(7)[:, 0:N_CMP * GROUPS], inv128[:, :], sq[0][:, 0:N_CMP * GROUPS], True, True)\
                            .then_inc(kcsum_done, 1)
            pe.wait_ge(gelu_done, 2)
            pe.wait_ge(kc_ready, 1)
            for grp in range(GROUPS):
                last = mm(bank(6)[0:N_CMP, grp * DH:(grp + 1) * DH], hdn[:, 1, :, grp], w2[:, 1, :], True, True)
            last.then_inc(vc_done, 1)
            pe.wait_ge(vc_ready, 1)
            with pe.Fori(0, GROUPS) as g:
                def query_sums(h0):
                    wait(pe, sq_ready, h0 + 2, 6, g)
                    for h in (h0, h0 + 1):
                        for t in range(TT):
                            last = mm(bank(6)[:, h * TT + t:h * TT + t + 1], sq[h % 2][:, t * P:(t + 1) * P],
                                      inv128[:, 0:1], True, True)
                    last.then_inc(rq_done, 1)

                for j in range(G_UNITS):
                    n = G0 + j
                    arrive(n, G_UNITS, g)
                    if j < 8:
                        columns_unit(n, j % 4, (2 * (j // 4), 2 * (j // 4) + 1))
                    elif j < 12:
                        columns_unit(n, j % 4, (4, 5))
                    else:
                        if j == 12:
                            wait(pe, q_lo, 4, 4, g)
                        tokens_unit(n, j - 12, 4, 2 * DH, hTh, hTl, (0, 1, 2, 3), KD)
                    if j == 6:
                        query_sums(0)
                    if j == 10:
                        query_sums(2)
                    if j == 12:
                        wait(pe, sq_ready, 6, 6, g)
                        mm(bank(7), inv128[:, :], sq[0], True, True).then_inc(ksum_done, 1)
                    if j == 13:
                        wait(pe, rq_den, 1, 1, g)
                        mm(bank(6), inv128[:, :], sq[1], True, True).then_inc(ksum_done, 1)
                wait(pe, v_lo, 4, 4, g)
                wait(pe, q_lo, 4, 4, g)
                wait(pe, group_ready, 1, 1, g)
                for i in range(REP * TT):
                    h, t = i // TT, i % TT
                    ts, at = slice(t * P, (t + 1) * P), bank(0)[:, i * CPAD:(i + 1) * CPAD]
                    mm3(at, (qh[:, h, ts], ql[:, h, ts]), (kcgh[:, :], kcgl[:, :]), True, False)
                    last = mm(at, ident16[:, :], causal_cmp[:, t, :], stop=True)
                last.then_inc(cs_done, 1)

                def scores(i):
                    h, t, e = i // TT, i % TT, i % 2
                    ts, nk = slice(t * P, (t + 1) * P), (t + 1) * P
                    if i >= 2:
                        wait(pe, exp_done, 2 * (i - 1), 32, g)
                    for b in range(2):
                        bk = bank(2 + 2 * e + b)
                        mm3(bk[:, 0:nk], (qh[:, h, ts], ql[:, h, ts]), (kh[:, b, 0:nk], kl[:, b, 0:nk]), True, False)
                        last = mm(bk[:, t * P:nk], ident16[:, :], causal[:, :], stop=True)
                    last.then_inc(s_done, 1)

                def values(i):
                    h, t, e = i // TT, i % TT, i % 2
                    if t == 0:
                        wait(pe, ptc_ready, h + 1, 4, g)
                        if h:
                            wait(pe, o_ready, h, REP, g)
                        mm(bank(1), vcg[:, :], ptc[:, :], start=True)
                    wait(pe, pt_lo, i + 1, 16, g)
                    for b in range(2):
                        for k in range(t + 1):
                            ks, vs = slice(k * P, (k + 1) * P), slice(b * DH, (b + 1) * DH)
                            last = mm3(bank(1)[:, t * P:(t + 1) * P], (vh[:, k, vs], vl[:, k, vs]),
                                       (pth[:, e, b, ks], ptl[:, e, b, ks]), False, b == 1 and k == t)
                    last.then_inc(pv_done, 1)

                wait(pe, k_lo, 2, 2, g)
                scores(0)
                scores(1)
                for i in range(REP * TT):
                    h, t, e = i // TT, i % TT, i % 2
                    if t == 0:
                        wait(pe, pc_ready, 1, 1, g)
                        if h:
                            wait(pe, ptc_ready, h, 4, g)
                        for tt in range(TT):
                            last = nc.tensor.transpose(bank(0)[0:CPAD, tt * P:(tt + 1) * P], pc[:, h * TT + tt, :],
                                                       ident[:, :])
                        last.then_inc(trc_done, 1)
                    wait(pe, p_ready, 2 * i + 2, 32, g)
                    if i:
                        wait(pe, pt_lo, i, 16, g)
                    for b in range(2):
                        for k in range(t + 1):
                            ks = slice(k * P, (k + 1) * P)
                            last = nc.tensor.transpose(bank(6 + b)[:, ks], pbuf[:, e, b, ks], ident[:, :])
                    last.then_inc(tr_done, 1)
                    if i + 2 < REP * TT:
                        scores(i + 2)
                    if i:
                        values(i - 1)
                values(REP * TT - 1)
                wait(pe, o_ready, REP, REP, g)
            with pe.Fori(0, 2) as cc:
                for c in range(2):
                    for q in range(O_UNITS):
                        n = O0 + c * O_UNITS + q
                        if c == 1 and q == 0:
                            wait(pe, x2_added, 1, 8, cc)
                        if c == 1 and q == 1:
                            wait(pe, x2_added, 4, 8, cc)
                        pe.wait_ge(o_lo, q + 1)
                        arrive(n, 2 * O_UNITS, cc)
                        tokens_unit(n, q, 2, 512, hTh, hTl, range(4 * c, 4 * c + 4), KD)
            pe.wait_ge(x2_added, 16)
            transposed_tiles(16)
            pe.wait_ge(hT_lo, 32)

            def slab(s):
                for j in range(F_UNITS):
                    n = F0 + j
                    arrive(n, F_UNITS, s)
                    if j == 8:
                        wait(pe, m_ready, 1, 4, s)
                    if j < 16:
                        columns_unit(n, (j % 8) // 2, (j // 8 * 4 + j % 2 * 2, j // 8 * 4 + j % 2 * 2 + 1))
                        continue
                    c, q = (j - 16) // 2, j % 2
                    if c == 0:
                        wait(pe, m_lo, 2 * q + 2, 4, s)
                    if c < 2 and q == 0:
                        wait(pe, m_ready, 2 * c + 2, 4, s)
                    if c >= 2 and q == 0:
                        wait(pe, y_added, 4 * (c - 1), 16, s)
                    if c == 3 and q == 1:
                        wait(pe, y_added, 12, 16, s)
                    base = 4 * (c % 2)
                    tokens_unit(n, q, 2, 512, mTh, mTl, range(base, base + 4), 4)

            with pe.Fori(0, SLABS - 1) as s:
                slab(s)
            slab(SLABS - 1)


DVE_GROUP = 3 + 7 + 16 * 4


_INS = ['x', 'norm_mix_g', 'norm_ffn_g', 'nsa_w_in', 'nsa_b_gate', 'nsa_q_norm_g', 'nsa_k_norm_g', 'nsa_cmp_pos',
        'nsa_cmp_w1', 'nsa_cmp_b1', 'nsa_cmp_w2', 'nsa_w_out', 'ffn_w_gate', 'ffn_w_up', 'ffn_w_down']
_OUTS = [((1, 512, 2048), 'float32')]


def kernel(**inputs):
    import numpy as _np
    import concourse.bacc as _bacc
    from concourse import mybir as _mybir
    from concourse.bass_utils import run_bass_kernel_spmd as _run

    nc = _bacc.Bacc("TRN2", target_bir_lowering=False, num_devices=1)
    arrays, args = {}, []
    for name in _INS:
        a = _np.ascontiguousarray(inputs[name])
        arrays[f"in_{name}_dram"] = a
        args.append(nc.dram_tensor(f"in_{name}_dram", a.shape, _mybir.dt.from_np(a.dtype), kind="ExternalInput").ap())
    for i, (shape, dtype) in enumerate(_OUTS):
        dt = _mybir.dt.from_np(_np.dtype(dtype))
        args.append(nc.dram_tensor(f"out_{i}_dram", shape, dt, kind="ExternalOutput").ap())
    nsa_swiglu_block(nc, *args)
    r = _run(nc, [arrays], core_ids=[0])
    got = tuple(r.results[0][f"out_{i}_dram"] for i in range(len(_OUTS)))
    return got[0]
```

```python
import concourse.bass as bass
from concourse import mybir
from contextlib import ExitStack

P = 128
S, D = 512, 2048
HEADS, GROUPS, DH = 16, 4, 128
REP = HEADS // GROUPS
CMP_LEN, CMP_STRIDE = 32, 16
N_CMP = (S - CMP_LEN) // CMP_STRIDE + 1
CPAD = 32
SEL_BLOCK, N_SELECT, WINDOW = 64, 16, 512
D_FF = 5632
EPS = 1e-6
MASKED = -2.0 ** 100
FLOOR = -2.0 ** 66

TT = S // P
KD = D // P
QCOL = 0
KVCOL = [HEADS * DH + n * GROUPS * DH for n in range(6)]
GATECOL = HEADS * DH + 6 * GROUPS * DH
NG = 3 * HEADS

UNIT = 1024
RAW, RING = 2, 4
CMP_UNITS = 12
T0 = 2 * CMP_UNITS
P0, P_UNITS = T0 + 2, 16
A0 = P0 + GROUPS * P_UNITS
B0 = A0 + 24
F0, F_UNITS = B0 + 8, 24
SLABS = D_FF // 512
LAST = GROUPS - 1
OWN = LAST * REP

STEPS = REP * 2 * TT
HEAD_FILL = [0, 1, 2, 3]
FILL_P = [[4], [5], [6], [7], [8], [], [9], [10], [11], [], [12], [13], [14], [15], [], [16], [17], [],
          [18], [19], [20], [21], [22], [23], [], [24], [25], [26], [27], [28], [29], [30]]
TAIL_P = [31]
FILL_A = [[], [], [], []] * 8
TAIL_A = [47]
_next = 4
for _i in range(STEPS):
    _n = 0 if _i % TT == 1 else 1 if _i in (6, 7, 26, 27, 31) else 2
    FILL_A[_i] = list(range(_next, _next + _n))
    _next += _n
V_AT, K_AT, Q_AT = (next(i for i, f in enumerate(FILL_P) if u in f) for u in (7, 15, 23))
KSUM_AT, KB_AT, KB2_AT, QSUM_AT, KSPLIT_AT = K_AT + 2, K_AT + 5, K_AT + 7, Q_AT + 3, STEPS - 2

assert S // SEL_BLOCK <= N_SELECT and WINDOW >= S
assert _next == TAIL_A[0] and len(FILL_P) == STEPS


def nsa_swiglu_block(nc, x, mix_g, ffn_g, w_in, b_gate, q_g, k_g, cmp_pos, cmp_w1, cmp_b1, cmp_w2,
                     w_out, w_gate, w_up, w_down, out):
    f32, f32r, bf16 = mybir.dt.float32, mybir.dt.float32r, mybir.dt.bfloat16
    ACT, ALU, AX = mybir.ActivationFunctionType, mybir.AluOpType, mybir.AxisListType
    NC4 = N_CMP * GROUPS
    ctx = ExitStack()
    with ctx:
        def sb(name, shape, dt=f32):
            return ctx.enter_context(nc.sbuf_tensor(name, shape, dt))

        def over(name, shape, at, dt=f32):
            return nc.alloc_sbuf_tensor_at(name, shape, dt, offset=at)

        def sem(name):
            return ctx.enter_context(nc.semaphore(name))

        hTh, hTl = sb("hTh", [P, KD, S], f32r), sb("hTl", [P, KD, S], f32r)
        raw = sb("raw", [P, RAW, UNIT])
        wh, wl = sb("wh", [P, RING, UNIT], f32r), sb("wl", [P, RING, UNIT], f32r)
        x_rows = sb("x_rows", [P, TT, D])
        ot = x_rows[:, :, :].rearrange("p t d -> p (t d)").rearrange("p (h s) -> p h s", s=S)
        x2 = x_rows
        q_at = nc.sbuf_base
        qh, ql = sb("qh", [P, REP, S], f32r), sb("ql", [P, REP, S], f32r)
        kh, kl = sb("kh", [P, 2, S], f32r), sb("kl", [P, 2, S], f32r)
        vh, vl = sb("vh", [P, TT, 2 * DH], f32r), sb("vl", [P, TT, 2 * DH], f32r)
        CB = [P, CMP_STRIDE, S // CMP_STRIDE + 2, GROUPS]
        x_sq = over("x_sq", [P, 2, D], q_at)
        cbh, cbl = over("cbh", CB, q_at, f32r), over("cbl", CB, q_at + 4 * CB[1] * CB[2] * CB[3], f32r)
        h_rows = over("h_rows", [P, 2, TT, 512], q_at)
        mTh, mTl = over("mTh", [P, 4, S], q_at + 16 * 1024, f32r), over("mTl", [P, 4, S], q_at + 24 * 1024, f32r)
        stage_at = nc.sbuf_base
        kst, vst = sb("kst", [P, 2, S]), sb("vst", [P, 2, S])
        gain_row = over("gain_row", [P, D], stage_at)
        ffn_work = over("ffn_work", [P, 4, S], stage_at)
        pbuf = sb("pbuf", [P, 2, S])
        PT_AT = [0, 3, 6, 4]
        pt_at = nc.sbuf_base
        pth, ptl = sb("pth", [P, 10, P], f32r), sb("ptl", [P, 10, P], f32r)
        w2 = over("w2", [P, 2, DH], pt_at)
        hdn = over("hdn", [P, 2, N_CMP, GROUPS], pt_at + 1024)
        rows = over("rows", [P, P], pt_at + 2048)
        sq = sb("sq", [P, 2, S])
        diag = sq[:, :, :].rearrange("p a s -> p (a s)").rearrange("p (j c) -> p j c", c=P)
        rbc = over("rbc", [P, S], nc.sbuf_base - 4 * S)
        ident, ident16 = sb("ident", [P, P]), sb("ident16", [P, P], bf16)
        inv128 = sb("inv128", [P, P])
        neg_half = sb("neg_half", [P, 1])
        causal = sb("causal", [P, P], bf16)
        causal_cmp = sb("causal_cmp", [P, TT, CPAD], bf16)
        cols = sb("cols", [P, 72])
        gains = sb("gains", [P, 3])
        bgate = sb("bgate", [P, NG])
        gates = sb("gates", [P, TT, NG])
        gates_g = sb("gates_g", [P, TT, 3 * REP])
        hb = sb("hb", [P, 2])
        kch, kcl = sb("kch", [P, GROUPS, CPAD], f32r), sb("kcl", [P, GROUPS, CPAD], f32r)
        kcg = sb("kcg", [P, 2, CPAD], f32r)
        vc, vcg = sb("vc", [CPAD, GROUPS, DH]), sb("vcg", [CPAD, DH])
        pc = sb("pc", [P, REP * TT, CPAD])
        ptc = sb("ptc", [CPAD, S])
        rqs, rqn = sb("rqs", [P, REP * TT]), sb("rqn", [P, REP * TT])
        krr = sb("krr", [P, 8])
        ss, rr = sb("ss", [P, 16]), sb("rr", [P, 4])
        cmx, csum = sb("cmx", [P, REP * TT]), sb("csum", [P, REP * TT])
        nmax, nb, sums, wgt = (sb(n, [P, 2]) for n in ("nmax", "nb", "sums", "wgt"))

        ps = ctx.enter_context(nc.psum_tensor("ps", [P, 8, S], f32))

        def bank(b):
            return ps[:, b, :]

        rows_loaded, gain_loaded, gain2_loaded = sem("rows_loaded"), sem("gain_loaded"), sem("gain2_loaded")
        w2_loaded, bgate_loaded = sem("w2_loaded"), sem("bgate_loaded")
        x_loaded = [sem(f"x_loaded{t}") for t in range(TT)]
        x2_loaded = sem("x2_loaded")
        raw_loaded = [sem(f"raw_loaded{i}") for i in range(RAW)]
        hi_ready, lo_ready, units_used = sem("hi_ready"), sem("lo_ready"), sem("units_used")
        zeroed, consts_ready, ident16_ready = sem("zeroed"), sem("consts_ready"), sem("ident16_ready")
        vector_done = sem("vector_done")
        ss_done, rms_den, rms_root, h_ready = sem("ss_done"), sem("rms_den"), sem("rms_root"), sem("h_ready")
        hT_banks, hT_hi, hT_lo = sem("hT_banks"), sem("hT_hi"), sem("hT_lo")
        rowsT_done, cols_ready, pos_hi, pos_lo = sem("rowsT_done"), sem("cols_ready"), sem("pos_hi"), sem("pos_lo")
        gateT_copied, gates_done = sem("gateT_copied"), sem("gates_done")
        gate_arg, gate_exp, gates_ready = sem("gate_arg"), sem("gate_exp"), sem("gates_ready")
        c_hi, c_lo, hb_ready, gelu_done = sem("c_hi"), sem("c_lo"), sem("hb_ready"), sem("gelu_done")
        kc_done, kc_sq, kc_raw, kcsum_done, kc_den = (sem(n) for n in ("kc_done", "kc_sq", "kc_raw", "kcsum_done", "kc_den"))
        kc_root, kc_diag, kcb_done, kc_norm = sem("kc_root"), sem("kc_diag"), sem("kcb_done"), sem("kc_norm")
        kc_hi, kc_lo, vc_done, vc_ready = sem("kc_hi"), sem("kc_lo"), sem("vc_done"), sem("vc_ready")
        vst_ready, ksq_ready, kst_ready, ksum_done = sem("vst_ready"), sem("ksq_ready"), sem("kst_ready"), sem("ksum_done")
        k_den, k_root, kdiag_ready, kb_done, k_norm = (sem(n) for n in ("k_den", "k_root", "kdiag_ready", "kb_done", "k_norm"))
        q_hi, q_lo, qsq_ready, qsum_done = sem("q_hi"), sem("q_lo"), sem("qsq_ready"), sem("qsum_done")
        q_den, rqn_ready, k_hi, k_lo, v_hi, v_lo = (sem(n) for n in ("q_den", "rqn_ready", "k_hi", "k_lo", "v_hi", "v_lo"))
        group_ready, cs_done, cs_ready, c_exp, pc_ready = (sem(n) for n in ("group_ready", "cs_done", "cs_ready", "c_exp", "pc_ready"))
        trc_done, ptc_ready = sem("trc_done"), sem("ptc_ready")
        s_done, nb_ready, exp_done, p_ready = sem("s_done"), sem("nb_ready"), sem("exp_done"), sem("p_ready")
        tr_done, pt_hi, pt_lo, pv_done, o_ready = (sem(n) for n in ("tr_done", "pt_hi", "pt_lo", "pv_done", "o_ready"))
        ot_hi, ot_lo, own_hi, own_lo = sem("ot_hi"), sem("ot_lo"), sem("own_hi"), sem("own_lo")
        x2a_added, x2b_added, x2_sq = sem("x2a_added"), sem("x2b_added"), sem("x2_sq")
        h2_ready, h2T_banks, h2T_hi, h2T_lo = sem("h2_ready"), sem("h2T_banks"), sem("h2T_hi"), sem("h2T_lo")
        r2_den, r2_root, r2_diag, rb_done = sem("r2_den"), sem("r2_root"), sem("r2_diag"), sem("rb_done")
        gs_ready, silu_done, m_ready, m_hi, m_lo = (sem(n) for n in ("gs_ready", "silu_done", "m_ready", "m_hi", "m_lo"))
        y_added, stored = sem("y_added"), sem("stored")

        w_in_v = w_in[0].rearrange("(q k p) c -> q p k c", k=4, p=P)
        w_in_8 = w_in[0].rearrange("(q k p) c -> q p k c", k=8, p=P)
        w_gate_v = w_gate[0].rearrange("(q k p) c -> q p k c", k=4, p=P)
        w_up_v = w_up[0].rearrange("(q k p) c -> q p k c", k=4, p=P)
        w1_v = cmp_w1[0].rearrange("t (j l p) c -> t j p l c", l=8, p=P)
        w_out_v = w_out[0].rearrange("(q k p) c -> q p k c", k=4, p=P)
        w_down_v = w_down[0].rearrange("(q k p) c -> p q k c", k=2, p=P)

        def wait(eng, s, base, per=0, i=0):
            eng.wait_ge(s, i * per + base if per else base)

        def ended(halves):
            return [u // 2 for u in halves if u % 2]

        class Own:
            def __init__(self, eng):
                self.eng, self.base, self.local, self.per, self.i = eng, 0, 0, 0, 0

            def done(self, ins):
                ins.then_inc(vector_done, 1)
                self.local += 1

            def settle(self):
                wait(self.eng, vector_done, self.base + self.local, self.per, self.i)

            def enter(self, i, per):
                self.base += self.local
                self.local, self.per, self.i = 0, per, i

            def leave(self, turns):
                assert self.local == self.per, (self.local, self.per)
                self.base += turns * self.per
                self.local, self.per, self.i = 0, 0, 0

        def pt_tiles(i, pt):
            t, bk = i % TT, bank(4 + i % 2)
            if t < TT - 1:
                return [(pt[:, t:t + 3 * t + 1:3, :], bk[:, 0:(t + 1) * P].rearrange("p (k c) -> p k c", c=P))]
            return [(pt[:, t:t + 7:3, :], bk[:, 0:t * P].rearrange("p (k c) -> p k c", c=P)),
                    (pt[:, PT_AT[t] + t, :], bk[:, t * P:(t + 1) * P])]

        block = ctx.enter_context(nc.Block())

        @block.sync
        def _(sp):
            def unit(n, halves, per=0, i=0):
                if n >= RAW:
                    wait(sp, lo_ready, n - RAW + 1, per, i)
                for dst, src in halves:
                    sp.dma_start(dst, src).then_inc(raw_loaded[n % RAW], 16)

            def k_halves(n, src, k):
                dst = raw[:, n % RAW, :].rearrange("p (k c) -> p k c", k=k)
                return [(dst[:, a:a + k // 2, :], src[:, a:a + k // 2, :]) for a in (0, k // 2)]

            def column_halves(n, src_a, src_b):
                dst = raw[:, n % RAW, :].rearrange("p (k c) -> p k c", k=4)
                return [(dst[:, :, 0:P], src_a), (dst[:, :, P:2 * P], src_b)]

            def group_units(first, per, g, g1):
                for b, (ca, cb) in enumerate(((KVCOL[3], KVCOL[5]), (KVCOL[2], KVCOL[4]))):
                    for q in range(4):
                        n = first + 4 * b + q
                        unit(n, column_halves(n, w_in_v[q][:, :, bass.ds(g1 * DH + ca, DH)],
                                              w_in_v[q][:, :, bass.ds(g1 * DH + cb, DH)]), per, g)
                for b in range(2):
                    for q in range(4):
                        n = first + 8 + 4 * b + q
                        unit(n, k_halves(n, w_in_v[q][:, :, bass.ds(g1 * (REP * DH) + (QCOL + b * 256), 256)], 4),
                             per, g)

            for t in range(TT):
                sp.dma_start(x_rows[:, t, :], x[0, t * P:(t + 1) * P, :]).then_inc(x_loaded[t], 16)
                if t == 0:
                    sp.dma_start(gain_row[:, :], mix_g.to_broadcast([P, D])).then_inc(gain_loaded, 16)
            for ty in range(2):
                n = ty * CMP_UNITS
                for b in range(2):
                    for q in range(4):
                        c = KVCOL[ty] + b * 256
                        unit(n, k_halves(n, w_in_v[q][:, :, c:c + 256], 4))
                        n += 1
                for j in range(4):
                    unit(n, k_halves(n, w1_v[ty, j], 8))
                    n += 1
            for q in range(2):
                unit(T0 + q, k_halves(T0 + q, w_in_8[q][:, :, GATECOL + NG - P:GATECOL + NG], 8))
            group_units(P0, 0, 0, 0)
            with sp.Fori(0, LAST) as g:
                group_units(P0 + P_UNITS, P_UNITS, g, g + 1)
            for c in range(8):
                for q in range(3):
                    n = A0 + 3 * c + q
                    unit(n, k_halves(n, w_out_v[q][:, :, c * 256:(c + 1) * 256], 4))
            for c in range(8):
                unit(B0 + c, k_halves(B0 + c, w_out_v[3][:, :, c * 256:(c + 1) * 256], 4))
            with sp.Fori(0, SLABS) as s:
                for b in range(2):
                    for q in range(4):
                        for u, w in enumerate((w_gate_v, w_up_v)):
                            n = F0 + 8 * b + 2 * q + u
                            unit(n, k_halves(n, w[q][:, :, bass.ds(s * 512 + b * 256, 256)], 4), F_UNITS, s)
                for c in range(4):
                    for q in range(2):
                        n = F0 + 16 + 2 * c + q
                        src = w_down_v[:, bass.ds(s * 2 + q, 1), :, c * 512:(c + 1) * 512]
                        unit(n, k_halves(n, src.rearrange("p q k c -> p (q k) c"), 2), F_UNITS, s)
            out_v = out[0].rearrange("(t p) d -> p t d", p=P)
            for c in range(4):
                wait(sp, y_added, (SLABS - 1) * 16 + 4 * (c + 1))
                sp.dma_start(out_v[:, :, c * 512:(c + 1) * 512], x2[:, :, c * 512:(c + 1) * 512])\
                  .then_inc(stored, 16)
            sp.wait_ge(stored, 64)

        @block.gpsimd
        def _(pool):
            pool.dma_start(rows[0:64, :], cmp_pos[0].rearrange("t l d -> (t l) d")).then_inc(rows_loaded, 16)
            pool.dma_start(rows[64:66, :], cmp_b1[0]).then_inc(rows_loaded, 16)
            pool.dma_start(rows[66:67, :], q_g).then_inc(rows_loaded, 16)
            pool.dma_start(rows[67:70, :], k_g[0]).then_inc(rows_loaded, 16)
            pool.memset(ident[:, :], 0.0).then_inc(zeroed, 1)
            pool.memset(causal[:, :], 0.0).then_inc(zeroed, 1)
            pool.memset(causal_cmp[:, :, :], 0.0).then_inc(zeroed, 1)
            pool.memset(inv128[:, :], 1.0 / P).then_inc(zeroed, 1)
            pool.memset(neg_half[:, :], -0.5).then_inc(zeroed, 1)
            pool.memset(kch[:, :, :].bitcast(f32), 0.0).then_inc(zeroed, 1)
            pool.memset(kcl[:, :, :].bitcast(f32), 0.0).then_inc(zeroed, 1)
            pool.memset(vc[:, :, :], 0.0).then_inc(zeroed, 1)
            pool.wait_ge(zeroed, 8)
            pool.affine_select(out=ident[:, :], in_=ident[:, :], compare_op=ALU.not_equal, fill=1.0, base=0,
                               pattern=[[-1, P]], channel_multiplier=1).then_inc(consts_ready, 1)
            pool.affine_select(out=causal[:, :], in_=causal[:, :], compare_op=ALU.is_ge, fill=MASKED, base=0,
                               pattern=[[-1, P]], channel_multiplier=1).then_inc(consts_ready, 1)
            pool.affine_select(out=causal_cmp[:, :, :], in_=causal_cmp[:, :, :], compare_op=ALU.is_ge,
                               fill=MASKED, base=-(CMP_LEN - 1), pattern=[[P, TT], [-CMP_STRIDE, CPAD]],
                               channel_multiplier=1).then_inc(consts_ready, 1)
            pool.dma_start(bgate[:, :], b_gate.to_broadcast([P, NG])).then_inc(bgate_loaded, 16)
            pool.dma_start(w2[:, :, :], cmp_w2[0].rearrange("t p d -> p t d")).then_inc(w2_loaded, 16)

            def inverse_root(ap, done):
                n, m = ap.shape
                pool.tensor_tensor(ap, ap, neg_half[0:n, 0:1].to_broadcast([n, m]), ALU.pow).then_inc(done, 1)

            for t in range(TT):
                pool.wait_ge(rms_den, t + 1)
                inverse_root(rr[:, t:t + 1], rms_root)
            pool.wait_ge(kc_den, 1)
            inverse_root(krr[0:NC4, 0:1], kc_root)

            def group_roots(p):
                wait(pool, k_den, 1, 1, p)
                inverse_root(krr[:, :], k_root)
                for b in range(2):
                    wait(pool, q_den, b + 1, 2, p)
                    inverse_root(rqn[:, b * 2 * TT:(b + 1) * 2 * TT], rqn_ready)

            group_roots(0)
            with pool.Fori(0, LAST) as g:
                group_roots(g + 1)
            pool.wait_ge(ot_lo, OWN // 2)
            pool.dma_start(x2[:, :, :], x[0].rearrange("(t p) d -> p t d", p=P)).then_inc(x2_loaded, 16)
            pool.dma_start(gain_row[:, :], ffn_g.to_broadcast([P, D])).then_inc(gain2_loaded, 16)
            pool.wait_ge(r2_den, 1)
            inverse_root(rr[:, :], r2_root)

        @block.scalar
        def _(act):
            def copy(dst, src):
                return nc.scalar.activation(dst, src, ACT.Copy)

            def square(dst, src):
                return nc.scalar.activation(dst, src, ACT.Square)

            def split(n, per=0, i=0):
                wait(act, raw_loaded[n % RAW], 32 * (n // RAW + 1), 32 * per // RAW, i)
                if n >= RING:
                    wait(act, units_used, n - RING + 1, per, i)
                copy(wh[:, n % RING, :], raw[:, n % RAW, :]).then_inc(hi_ready, 1)

            for t in range(TT):
                act.wait_ge(x_loaded[t], 16)
                if t >= 2:
                    act.wait_ge(ss_done, t - 1)
                nc.scalar.activation(x_sq[:, t % 2, :], x_rows[:, t, :], ACT.Square,
                                     accum_out=ss[:, t:t + 1]).then_inc(ss_done, 1)
            for n in range(RAW):
                split(n)
            for t in range(TT):
                for q in range(4):
                    n = 4 * t + q
                    act.wait_ge(hT_banks, n + 1)
                    copy(hTh[:, 4 * q:4 * q + 4, t * P:(t + 1) * P],
                         bank(4 * (t % 2) + q).rearrange("p (k c) -> p k c", k=4)).then_inc(hT_hi, 1)
            for n in range(RAW, RING):
                split(n)
            for ty in range(2):
                for j in range(CMP_UNITS):
                    n = ty * CMP_UNITS + j
                    if j in (3, 7):
                        act.wait_ge(units_used, n + 1)
                        for grp in ((j - 3) // 2, (j - 3) // 2 + 1):
                            src = bank(grp).rearrange("p (c l) -> p l c", l=CMP_STRIDE)
                            copy(cbh[:, :, 1:-1, grp], src).then_inc(c_hi, 1)
                    split(n + RING)
                    if n == CMP_UNITS:
                        act.wait_ge(kc_done, 1)
                        square(sq[:, 0, 0:NC4], bank(6)[:, 0:NC4]).then_inc(kc_sq, 1)
                    if n == CMP_UNITS + 7:
                        act.wait_ge(kc_norm, 1)
                        copy(kch[:, :, 0:N_CMP], sq[:, 0, 0:NC4].rearrange("p (c g) -> p g c", g=GROUPS))\
                            .then_inc(kc_hi, 1)
                    if j == CMP_UNITS - 1:
                        act.wait_ge(hb_ready, ty + 1)
                        nc.scalar.activation(hdn[:, ty, :, :].rearrange("p c g -> p (c g)"),
                                             bank(4)[:, GROUPS:GROUPS + NC4], ACT.Gelu_apprx_tanh,
                                             bias=hb[:, ty:ty + 1]).then_inc(gelu_done, 1)
            split(T0 + RING)
            split(T0 + 1 + RING)
            act.wait_ge(units_used, T0 + 2)
            copy(pbuf[:, 0, :], bank(5)).then_inc(gateT_copied, 1)
            act.wait_ge(gate_arg, 1)
            nc.scalar.activation(gates[:, :, :], gates[:, :, :], ACT.Exp, scale=-1.0).then_inc(gate_exp, 1)

            def values_out(per, i, p):
                wait(act, units_used, P0 + 4, per, i)
                for b in range(2):
                    copy(vst[:, b, :], bank(6 + b)).then_inc(vst_ready, 1)

            def keys_out(per, i, p):
                wait(act, units_used, P0 + 8, per, i)
                for b in range(2):
                    square(sq[:, b, :], bank(6 + b)).then_inc(ksq_ready, 1)

            def queries_out(per, i, p, h0):
                wait(act, units_used, P0 + 12 + 2 * h0, per, i)
                if h0 == 0:
                    wait(act, kb_done, 2, 2, p)
                else:
                    wait(act, qsum_done, 1, 2, p)
                for h in (h0, h0 + 1):
                    copy(qh[:, h, :], bank(6 + h - h0)).then_inc(q_hi, 1)
                    square(sq[:, h - h0, :], bank(6 + h - h0)).then_inc(qsq_ready, 1)

            def keys_split(p):
                wait(act, k_norm, 2, 2, p)
                copy(kh[:, :, :], kst[:, :, :]).then_inc(k_hi, 1)

            def values_split(p):
                wait(act, vst_ready, 2, 2, p)
                copy(vh[:, :, :].rearrange("p t c -> p (t c)"), vst[:, :, :].rearrange("p a s -> p (a s)"))\
                    .then_inc(v_hi, 1)

            for u in range(P_UNITS):
                if u == 3:
                    values_out(0, 0, 0)
                if u == 7:
                    keys_out(0, 0, 0)
                if u == 11:
                    queries_out(0, 0, 0, 0)
                if u == 15:
                    queries_out(0, 0, 0, 2)
                split(P0 + u + RING)
                if u == 12:
                    keys_split(0)
            values_split(0)

            def attention(g, fill, tail, last):
                def compressed_exp():
                    wait(act, cs_ready, 1, 1, g)
                    nc.scalar.activation(pc[:, :, :], pc[:, :, :], ACT.Exp).then_inc(c_exp, 1)

                def probs(i):
                    t, m = i % TT, i // (2 * TT) * TT + i % TT
                    nk = (t + 1) * P
                    wait(act, nb_ready, i + 1, STEPS, g)
                    nc.scalar.activation(pbuf[:, i % 2, 0:nk], bank(2 + i % 2)[:, 0:nk], ACT.Exp,
                                         bias=nb[:, i % 2:i % 2 + 1], scale=rqs[:, m:m + 1],
                                         accum_out=sums[:, i % 2:i % 2 + 1]).then_inc(exp_done, 1)

                def pt_part(i):
                    wait(act, tr_done, i + 1, STEPS, g)
                    if i >= TT and i % TT == 0:
                        wait(act, pv_done, i // TT, 2 * REP, g)
                    for dst, src in pt_tiles(i, pth):
                        last = copy(dst, src)
                    last.then_inc(pt_hi, 1)

                def head_out(h):
                    wait(act, pv_done, 2 * (h + 1), 2 * REP, g)
                    if last:
                        copy(hTh[:, OWN + h, :], bank(1)).then_inc(own_hi, 1)
                    else:
                        copy(ot[:, bass.ds(g * REP + h, 1), :].rearrange("p a b -> p (a b)"), bank(1))\
                            .then_inc(o_ready, 1)

                def first_out(q):
                    copy(hTh[:, 2 * q:2 * q + 2, :], ot[:, 2 * q:2 * q + 2, :]).then_inc(ot_hi, 1)

                def splits(units):
                    for u in units:
                        if last:
                            split(A0 + u + RING)
                        else:
                            split(P0 + P_UNITS + u + RING, P_UNITS, g)

                if last:
                    act.wait_ge(o_ready, OWN)
                    first_out(0)
                    first_out(1)
                probs(0)
                compressed_exp()
                if last:
                    for q in range(2, OWN // 2):
                        first_out(q)
                splits(ended(HEAD_FILL))
                for i in range(1, STEPS + 1):
                    if i < STEPS:
                        probs(i)
                    j = i - 1
                    pt_part(j)
                    if j >= 8 and j % 8 == 0:
                        head_out(j // 8 - 1)
                    splits(ended(fill[j]))
                    if not last:
                        if j == V_AT:
                            values_out(P_UNITS, g + 1, g + 1)
                        if j == K_AT:
                            keys_out(P_UNITS, g + 1, g + 1)
                        if j == Q_AT:
                            queries_out(P_UNITS, g + 1, g + 1, 0)
                        if j == KSPLIT_AT:
                            wait(act, s_done, STEPS, STEPS, g)
                            keys_split(g + 1)
                if not last:
                    queries_out(P_UNITS, g + 1, g + 1, 2)
                head_out(REP - 1)
                splits(ended(tail))
                if not last:
                    values_split(g + 1)

            with act.Fori(0, LAST) as g:
                attention(g, FILL_P, TAIL_P, False)
            attention(LAST, FILL_A, TAIL_A, True)
            def hidden_part(c):
                for kk in range(4):
                    act.wait_ge(h2T_banks, 4 * c + kk + 1)
                    copy(hTh[:, 4 * c + kk, :], bank(kk + 4 * (c == 3))).then_inc(h2T_hi, 1)

            for c in range(4):
                split(B0 + 2 * c + RING)
                split(B0 + 2 * c + 1 + RING)
                for t in range(TT):
                    act.wait_ge(x2b_added, 4 * c + 4)
                    if c or t:
                        act.wait_ge(x2_sq, 4 * c + t)
                    nc.scalar.activation(pbuf[:, 0, :], x2[:, t, c * 512:(c + 1) * 512], ACT.Square,
                                         accum_out=ss[:, 4 * c + t:4 * c + t + 1]).then_inc(x2_sq, 1)
                if c:
                    hidden_part(c - 1)
            hidden_part(3)

            def slab(s, last):
                for j in range(F_UNITS):
                    n = F0 + j
                    if j in (6, 14):
                        for c in range(2):
                            wait(act, gs_ready, (j - 6) // 4 + c + 1, 4, s)
                            nc.scalar.activation(ffn_work[:, c, :], ffn_work[:, c, :], ACT.Silu).then_inc(silu_done, 1)
                    if j in (7, 15):
                        for c in range(2):
                            wait(act, m_ready, (j - 7) // 4 + c + 1, 4, s)
                            copy(mTh[:, (j - 7) // 4 + c, :], ffn_work[:, 2 + c, :]).then_inc(m_hi, 1)
                    if not last or j + RING < F_UNITS:
                        split(n + RING, F_UNITS, s)

            with act.Fori(0, SLABS - 1) as s:
                slab(s, False)
            slab(SLABS - 1, True)

        @block.vector
        def _(dve):
            own = Own(dve)

            def lo(dst, src, hi, done):
                nc.vector.tensor_tensor(dst, src, hi.bitcast(f32), ALU.subtract).then_inc(done, 1)

            def split(n, per=0, i=0):
                wait(dve, hi_ready, n + 1, per, i)
                lo(wl[:, n % RING, :], raw[:, n % RAW, :], wh[:, n % RING, :], lo_ready)

            dve.wait_ge(consts_ready, 1)
            nc.vector.tensor_copy(ident16[:, :], ident[:, :]).then_inc(ident16_ready, 1)
            for t in range(TT):
                dve.wait_ge(ss_done, t + 1)
                nc.vector.tensor_scalar(rr[:, t:t + 1], ss[:, t:t + 1], 1.0 / D, EPS, ALU.mult, ALU.add)\
                    .then_inc(rms_den, 1)
                if t == 0:
                    dve.wait_ge(gain_loaded, 16)
                dve.wait_ge(rms_root, t + 1)
                nc.vector.scalar_tensor_tensor(out=x_rows[:, t, :], in0=x_rows[:, t, :], scalar=rr[:, t:t + 1],
                                               in1=gain_row[:, :], op0=ALU.mult, op1=ALU.mult).then_inc(h_ready, 1)
            dve.wait_ge(rowsT_done, 1)
            nc.vector.tensor_copy(cols[:, 0:70], bank(0)[:, 0:70]).then_inc(cols_ready, 1)
            dve.wait_ge(cols_ready, 1)
            own.done(nc.vector.tensor_scalar(gains[:, :], cols[:, 67:70], cols[:, 66:67], None, ALU.mult))
            for n in range(RAW):
                split(n)
            for t in range(TT):
                for q in range(4):
                    dve.wait_ge(hT_hi, 4 * t + q + 1)
                    at = (slice(None), slice(4 * q, 4 * q + 4), slice(t * P, (t + 1) * P))
                    lo(hTl[at], bank(4 * (t % 2) + q).rearrange("p (k c) -> p k c", k=4), hTh[at], hT_lo)
            for n in range(RAW, RING):
                split(n)
            for ty in range(2):
                for j in range(CMP_UNITS):
                    n = ty * CMP_UNITS + j
                    if j == 2:
                        dve.wait_ge(units_used, n)
                        for part, at in ((0, 0), (1, S // CMP_STRIDE + 1)):
                            l0 = ty * CMP_LEN + part * CMP_STRIDE
                            pos = cols[:, l0:l0 + CMP_STRIDE].rearrange("p (l a) -> p l a", a=1)\
                                .to_broadcast([P, CMP_STRIDE, GROUPS])
                            nc.vector.tensor_copy(cbh[:, :, at, :], pos).then_inc(pos_hi, 1)
                            dve.wait_ge(pos_hi, 2 * ty + part + 1)
                            lo(cbl[:, :, at, :], pos, cbh[:, :, at, :], pos_lo)
                    if j in (3, 7):
                        for grp in ((j - 3) // 2, (j - 3) // 2 + 1):
                            dve.wait_ge(c_hi, 4 * ty + grp + 1)
                            src = bank(grp).rearrange("p (c l) -> p l c", l=CMP_STRIDE)
                            lo(cbl[:, :, 1:-1, grp], src, cbh[:, :, 1:-1, grp], c_lo)
                    split(n + RING)
                    if n == CMP_UNITS:
                        dve.wait_ge(kc_sq, 1)
                        nc.vector.tensor_scalar(sq[:, 1, 0:NC4], bank(6)[:, 0:NC4], gains[:, 0:1], None, ALU.mult)\
                            .then_inc(kc_raw, 1)
                    if n == CMP_UNITS + 2:
                        dve.wait_ge(kcsum_done, 1)
                        nc.vector.tensor_scalar(krr[0:NC4, 0:1], bank(7)[0:NC4, 0:1], EPS, P ** -2.0, ALU.add, ALU.mult)\
                            .then_inc(kc_den, 1)
                    if n == CMP_UNITS + 4:
                        dve.wait_ge(kc_root, 1)
                        nc.vector.tensor_scalar(sq[0:NC4, 0, 0:NC4], ident[0:NC4, 0:NC4], krr[0:NC4, 0:1], None, ALU.mult)\
                            .then_inc(kc_diag, 1)
                    if n == CMP_UNITS + 6:
                        dve.wait_ge(kcb_done, 1)
                        dve.wait_ge(kc_raw, 1)
                        nc.vector.tensor_tensor(sq[:, 0, 0:NC4], sq[:, 1, 0:NC4], bank(7)[:, 0:NC4], ALU.mult)\
                            .then_inc(kc_norm, 1)
                    if n == CMP_UNITS + 8:
                        dve.wait_ge(kc_hi, 1)
                        lo(kcl[:, :, 0:N_CMP], sq[:, 0, 0:NC4].rearrange("p (c g) -> p g c", g=GROUPS),
                           kch[:, :, 0:N_CMP], kc_lo)
                    if j == CMP_UNITS - 1:
                        dve.wait_ge(units_used, n + 1)
                        own.done(nc.vector.tensor_tensor(hb[:, ty:ty + 1], bank(4)[:, 0:1], cols[:, 64 + ty:65 + ty],
                                                         ALU.add))
                        own.settle()
                        nc.vector.tensor_tensor(hb[:, ty:ty + 1], bank(4)[:, S // 4:S // 4 + 1], hb[:, ty:ty + 1],
                                                ALU.add).then_inc(hb_ready, 1)
            split(T0 + RING)
            split(T0 + 1 + RING)
            dve.wait_ge(vc_done, 1)
            nc.vector.tensor_copy(vc[0:N_CMP, :, :],
                                  bank(6)[0:N_CMP, :].rearrange("p (g d) -> p g d", g=GROUPS)).then_inc(vc_ready, 1)
            dve.wait_ge(gates_done, 1)
            dve.wait_ge(bgate_loaded, 16)
            nc.vector.tensor_tensor(gates[:, :, :], bank(4).rearrange("p (t c) -> p t c", t=TT)[:, :, P - NG:P],
                                    bgate[:, :].rearrange("p (a c) -> p a c", a=1).to_broadcast([P, TT, NG]),
                                    ALU.add).then_inc(gate_arg, 1)
            dve.wait_ge(gate_exp, 1)
            own.done(nc.vector.tensor_scalar_add(gates[:, :, :], gates[:, :, :], 1.0))
            own.settle()
            nc.vector.reciprocal(gates[:, :, :], gates[:, :, :]).then_inc(gates_ready, 1)

            def keys_out(p):
                for b in range(2):
                    wait(dve, ksq_ready, b + 1, 2, p)
                    nc.vector.tensor_scalar(kst[:, b, :], bank(6 + b), gains[:, 1 + b:2 + b], None, ALU.mult)\
                        .then_inc(kst_ready, 1)

            def keys_den(p):
                wait(dve, ksum_done, 1, 1, p)
                nc.vector.tensor_scalar(krr[:, :], bank(0)[:, 0:8], EPS, P ** -2.0, ALU.add, ALU.mult)\
                    .then_inc(k_den, 1)

            def keys_diag(p):
                wait(dve, k_root, 1, 1, p)
                for j in range(8):
                    last = nc.vector.tensor_scalar(diag[:, j, :], ident[:, :], krr[:, j:j + 1], None, ALU.mult)
                last.then_inc(kdiag_ready, 1)

            def keys_norm(p, b):
                wait(dve, kst_ready, 2, 2, p)
                wait(dve, kb_done, b + 1, 2, p)
                nc.vector.tensor_tensor(kst[:, b, :], kst[:, b, :], bank(0), ALU.mult).then_inc(k_norm, 1)

            def queries_out(p, h0):
                for h in (h0, h0 + 1):
                    wait(dve, qsq_ready, h + 1, 4, p)
                    lo(ql[:, h, :], bank(6 + h - h0), qh[:, h, :], q_lo)

            def queries_den(p, h0):
                wait(dve, qsum_done, h0 // 2 + 1, 2, p)
                at = slice(h0 * TT, (h0 + 2) * TT)
                nc.vector.tensor_scalar(rqn[:, at], bank(0)[:, at], EPS, float(DH), ALU.add, ALU.mult)\
                    .then_inc(q_den, 1)

            def keys_split(p):
                wait(dve, k_hi, 1, 1, p)
                lo(kl[:, :, :], kst[:, :, :], kh[:, :, :], k_lo)

            def values_split(p):
                wait(dve, v_hi, 1, 1, p)
                lo(vl[:, :, :].rearrange("p t c -> p (t c)"), vst[:, :, :].rearrange("p a s -> p (a s)"),
                   vh[:, :, :].rearrange("p t c -> p (t c)"), v_lo)

            for u in range(P_UNITS):
                if u == 7:
                    keys_out(0)
                if u == 8:
                    keys_den(0)
                if u == 9:
                    keys_diag(0)
                if u == 10:
                    keys_norm(0, 0)
                    keys_norm(0, 1)
                if u == 11:
                    queries_out(0, 0)
                if u == 13:
                    queries_den(0, 0)
                if u == 15:
                    queries_out(0, 2)
                split(P0 + u + RING)
                if u == 12:
                    keys_split(0)
            dve.wait_ge(vc_ready, 1)
            dve.wait_ge(kc_lo, 1)
            dve.wait_ge(gates_ready, 1)

            def attention(g, fill, tail, last):
                own.done(nc.vector.tensor_copy(kcg[:, 0, :], kch[:, bass.ds(g, 1), :].bitcast(f32)
                                               .rearrange("p a c -> p (a c)")))
                own.done(nc.vector.tensor_copy(kcg[:, 1, :], kcl[:, bass.ds(g, 1), :].bitcast(f32)
                                               .rearrange("p a c -> p (a c)")))
                own.done(nc.vector.tensor_copy(gates_g[:, :, :], gates[:, :, bass.ds(g * (3 * REP), 3 * REP)]))
                nc.vector.tensor_copy(vcg[:, :], vc[:, bass.ds(g, 1), :].rearrange("p a d -> p (a d)"))\
                    .then_inc(group_ready, 1)
                queries_den(g, 2)
                values_split(g)

                def first_out(q):
                    dve.wait_ge(ot_hi, q + 1)
                    lo(hTl[:, 2 * q:2 * q + 2, :], ot[:, 2 * q:2 * q + 2, :], hTh[:, 2 * q:2 * q + 2, :], ot_lo)

                def splits(units):
                    for u in units:
                        if last and u % 3 == 2:
                            if u == 2:
                                dve.wait_ge(x2_loaded, 16)
                            dve.wait_ge(units_used, A0 + u + 1)
                            for b in range(2):
                                at = x2[:, 2 * b:2 * b + 2, u // 3 * 256:(u // 3 + 1) * 256]
                                nc.vector.tensor_tensor(at, at, bank(6 + b).rearrange("p (t c) -> p t c", t=2),
                                                        ALU.add).then_inc(x2a_added, 1)
                        if last:
                            split(A0 + u + RING)
                        else:
                            split(P0 + P_UNITS + u + RING, P_UNITS, g)

                if last:
                    first_out(0)
                    first_out(1)
                wait(dve, rqn_ready, 2, 2, g)
                own.done(nc.vector.tensor_copy(rqs[:, :], rqn[:, :]))
                own.settle()

                def each(ap):
                    return ap.rearrange("p (i a) -> p i a", a=1).to_broadcast([P, REP * TT, CPAD])

                def compressed_scores():
                    sc = ps[:, 0:2, :].rearrange("p b (i n c) -> p (b i) n c", n=2, c=CPAD)
                    wait(dve, cs_done, 1, 1, g)
                    for h in range(REP):
                        at = slice(h * TT, (h + 1) * TT)
                        last_ = nc.vector.tensor_tensor(pc[:, at, :], sc[:, at, 1, :], causal_cmp[:, :, :], ALU.add)
                    own.done(last_)
                    own.settle()
                    own.done(nc.vector.tensor_tensor(pc[:, :, :], pc[:, :, :], sc[:, :, 0, :], ALU.add))
                    own.settle()
                    own.done(nc.vector.reduce_max(cmx[:, :], pc[:, :, :], axis=AX.X))
                    own.settle()
                    own.done(nc.vector.tensor_scalar_max(cmx[:, :], cmx[:, :], FLOOR))
                    own.settle()
                    own.done(nc.vector.tensor_tensor(pc[:, :, :], pc[:, :, :], each(cmx[:, :]), ALU.subtract))
                    own.settle()
                    nc.vector.tensor_tensor(pc[:, :, :], pc[:, :, :], each(rqs[:, :]), ALU.mult).then_inc(cs_ready, 1)

                def compressed_weigh():
                    wait(dve, c_exp, 1, 1, g)
                    own.done(nc.vector.reduce_sum(csum[:, :], pc[:, :, :], axis=AX.X))
                    own.settle()
                    own.done(nc.vector.tensor_scalar_max(csum[:, :], csum[:, :], 1e-30))
                    own.settle()
                    own.done(nc.vector.reciprocal(csum[:, :], csum[:, :]))
                    own.settle()
                    gate3 = gates_g[:, :, :].rearrange("p t (h b) -> p h t b", b=3)
                    own.done(nc.vector.tensor_tensor(csum[:, :].rearrange("p (h t) -> p h t", h=REP),
                                                     csum[:, :].rearrange("p (h t) -> p h t", h=REP),
                                                     gate3[:, :, :, 0], ALU.mult))
                    own.settle()
                    nc.vector.tensor_tensor(pc[:, :, :], pc[:, :, :], each(csum[:, :]), ALU.mult).then_inc(pc_ready, 1)

                def maximum(i):
                    nk = (i % TT + 1) * P
                    e, m = slice(i % 2, i % 2 + 1), i // (2 * TT) * TT + i % TT
                    wait(dve, s_done, i + 1, STEPS, g)
                    own.done(nc.vector.tensor_reduce(nmax[:, e], bank(2 + i % 2)[:, 0:nk], AX.X, ALU.max, negate=True))
                    own.settle()
                    nc.vector.tensor_scalar(nb[:, e], nmax[:, e], rqs[:, m:m + 1], None, ALU.mult).then_inc(nb_ready, 1)

                def weigh(i):
                    h, b, t = i // (2 * TT), i // TT % 2, i % TT
                    nk, e = (t + 1) * P, slice(i % 2, i % 2 + 1)
                    wait(dve, exp_done, i + 1, STEPS, g)
                    own.done(nc.vector.tensor_scalar_max(wgt[:, e], sums[:, e], 1e-30))
                    own.settle()
                    own.done(nc.vector.reciprocal(wgt[:, e], wgt[:, e]))
                    own.settle()
                    gate = gates_g[:, t, 3 * h + 1 + b:3 * h + 2 + b]
                    nc.vector.tensor_scalar(pbuf[:, i % 2, 0:nk], pbuf[:, i % 2, 0:nk], wgt[:, e], gate, ALU.mult, ALU.mult)\
                        .then_inc(p_ready, 1)

                def pt_part(i):
                    wait(dve, pt_hi, i + 1, STEPS, g)
                    for (dst, src), (hi, _) in zip(pt_tiles(i, ptl), pt_tiles(i, pth)):
                        last_ = nc.vector.tensor_tensor(dst, src, hi.bitcast(f32), ALU.subtract)
                    last_.then_inc(pt_lo, 1)

                maximum(0)
                compressed_scores()
                if last:
                    for q in range(2, OWN // 2):
                        first_out(q)
                splits(ended(HEAD_FILL))
                for i in range(1, STEPS + 2):
                    if i < STEPS:
                        maximum(i)
                    if i <= STEPS:
                        weigh(i - 1)
                    if i == 1:
                        compressed_weigh()
                    if i % 8 == 1 and i < STEPS:
                        wait(dve, trc_done, i // 8 + 1, REP, g)
                        nc.vector.tensor_copy(ptc[:, :], bank(0)[0:CPAD, :]).then_inc(ptc_ready, 1)
                    if i < 2:
                        continue
                    j = i - 2
                    pt_part(j)
                    if last and j >= 8 and j % 8 == 0:
                        dve.wait_ge(own_hi, j // 8)
                        lo(hTl[:, OWN + j // 8 - 1, :], bank(1), hTh[:, OWN + j // 8 - 1, :], own_lo)
                    splits(ended(fill[j]))
                    if last:
                        continue
                    if j == K_AT:
                        keys_out(g + 1)
                    if j == KSUM_AT - 1:
                        keys_den(g + 1)
                    if j == KSUM_AT:
                        keys_diag(g + 1)
                    if j == KB_AT - 1:
                        keys_norm(g + 1, 0)
                    if j == KB2_AT - 1:
                        keys_norm(g + 1, 1)
                    if j == Q_AT:
                        queries_out(g + 1, 0)
                    if j == QSUM_AT - 1:
                        queries_den(g + 1, 0)
                    if j == KSPLIT_AT:
                        keys_split(g + 1)
                if last:
                    dve.wait_ge(own_hi, REP)
                    lo(hTl[:, OWN + REP - 1, :], bank(1), hTh[:, OWN + REP - 1, :], own_lo)
                else:
                    queries_out(g + 1, 2)
                splits(ended(tail))

            with dve.Fori(0, LAST) as g:
                own.enter(g, DVE_GROUP)
                attention(g, FILL_P, TAIL_P, False)
                own.leave(LAST)
            attention(LAST, FILL_A, TAIL_A, True)

            for c in range(4):
                for half in range(2):
                    u = 2 * c + half
                    dve.wait_ge(units_used, B0 + u + 1)
                    for b in range(2):
                        at = x2[:, 2 * b:2 * b + 2, u * 256:(u + 1) * 256]
                        nc.vector.tensor_tensor(at, at, bank(4 + 2 * half + b).rearrange("p (t c) -> p t c", t=2),
                                                ALU.add).then_inc(x2b_added, 1)
                    split(B0 + u + RING)
                if c == 0:
                    dve.wait_ge(gain2_loaded, 16)
                if c >= 2:
                    dve.wait_ge(h2T_banks, 4 * (c - 1))
                dve.wait_ge(x2b_added, 4 * c + 4)
                nc.vector.tensor_tensor(h_rows[:, c % 2, :, :], x2[:, :, c * 512:(c + 1) * 512],
                                        gain_row[:, c * 512:(c + 1) * 512].rearrange("p (a d) -> p a d", a=1)
                                        .to_broadcast([P, TT, 512]), ALU.mult).then_inc(h2_ready, 1)

                def hidden_part(c):
                    for kk in range(4):
                        dve.wait_ge(h2T_hi, 4 * c + kk + 1)
                        lo(hTl[:, 4 * c + kk, :], bank(kk + 4 * (c == 3)), hTh[:, 4 * c + kk, :], h2T_lo)

                if c:
                    hidden_part(c - 1)
            dve.wait_ge(x2_sq, 16)
            own.done(nc.vector.reduce_sum(rr[:, :], ss[:, :].rearrange("p (c t) -> p t c", t=TT), axis=AX.X))
            own.settle()
            own.done(nc.vector.tensor_scalar(rr[:, :], rr[:, :], 1.0 / D, EPS, ALU.mult, ALU.add))
            own.settle()
            nc.vector.tensor_scalar(rr[:, :], rr[:, :], P ** -2.0, None, ALU.mult).then_inc(r2_den, 1)
            dve.wait_ge(r2_root, 1)
            for t in range(TT):
                last = nc.vector.tensor_scalar(diag[:, t, :], ident[:, :], rr[:, t:t + 1], None, ALU.mult)
            last.then_inc(r2_diag, 1)
            hidden_part(3)
            dve.wait_ge(rb_done, 1)
            own.done(nc.vector.tensor_copy(rbc[:, :], bank(4)))
            own.settle()

            def slab(s, last):
                for j in range(F_UNITS):
                    n = F0 + j
                    k, b0 = j // 8 * 2, j // 8 * 4
                    if j in (6, 14):
                        wait(dve, units_used, n + 1, F_UNITS, s)
                        for c in range(2):
                            nc.vector.tensor_tensor(ffn_work[:, c, :], bank(b0 + c), rbc[:, :], ALU.mult)\
                                .then_inc(gs_ready, 1)
                    if j in (7, 15):
                        wait(dve, units_used, n + 1, F_UNITS, s)
                        for c in range(2):
                            own.done(nc.vector.tensor_tensor(ffn_work[:, 2 + c, :], bank(b0 + 2 + c), rbc[:, :], ALU.mult))
                        own.settle()
                        for c in range(2):
                            wait(dve, silu_done, k + c + 1, 4, s)
                            nc.vector.tensor_tensor(ffn_work[:, 2 + c, :], ffn_work[:, c, :], ffn_work[:, 2 + c, :],
                                                    ALU.mult).then_inc(m_ready, 1)
                        for c in range(2):
                            wait(dve, m_hi, k + c + 1, 4, s)
                            lo(mTl[:, k + c, :], ffn_work[:, 2 + c, :], mTh[:, k + c, :], m_lo)
                    if j > 16 and j % 2:
                        wait(dve, units_used, n + 1, F_UNITS, s)
                        c = (j - 17) // 2
                        for t in range(TT):
                            at = x2[:, t, c * 512:(c + 1) * 512]
                            nc.vector.tensor_tensor(at, at, bank(4 * (c % 2) + t), ALU.add).then_inc(y_added, 1)
                    if not last or j + RING < F_UNITS:
                        split(n + RING, F_UNITS, s)

            with dve.Fori(0, SLABS - 1) as s:
                own.enter(s, 4)
                slab(s, False)
                own.leave(SLABS - 1)
            slab(SLABS - 1, True)

        @block.tensor
        def _(pe):
            def mm(out_, a, b, start=False, stop=False):
                return nc.tensor.matmul(out_, a, b, start=start, stop=stop, skip_group_check=True)

            def mm3(out_, a, b, start, stop):
                mm(out_, a[0], b[0], start=start)
                mm(out_, a[0], b[1])
                return mm(out_, a[1], b[0], stop=stop)

            def arrive(n, per=0, i=0):
                wait(pe, lo_ready, n + 1, per, i)

            def columns_half(n, q, half, bk):
                for kk in range(4):
                    k, at = 4 * q + kk, slice(kk * 256 + half * P, kk * 256 + half * P + P)
                    last = mm3(bank(bk), (wh[:, n % RING, at], wl[:, n % RING, at]), (hTh[:, k, :], hTl[:, k, :]),
                               k == 0, k == KD - 1)
                if half:
                    last.then_inc(units_used, 1)

            def tokens_half(n, q, half, bk, k_all=KD):
                for tt in range(2):
                    for kk in range(4):
                        k, at = 4 * q + kk, slice(kk * 256, (kk + 1) * 256)
                        ts = slice((2 * half + tt) * P, (2 * half + tt + 1) * P)
                        last = mm3(bank(bk)[:, tt * 256:(tt + 1) * 256], (hTh[:, k, ts], hTl[:, k, ts]),
                                   (wh[:, n % RING, at], wl[:, n % RING, at]),
                                   q == 0 and kk == 0 and tt == 0, k == k_all - 1)
                if half:
                    last.then_inc(units_used, 1)

            pe.wait_ge(consts_ready, 3)
            pe.wait_ge(zeroed, 8)
            pe.wait_ge(rows_loaded, 64)
            nc.tensor.transpose(bank(0)[:, 0:70], rows[0:70, :], ident[0:70, 0:70]).then_inc(rowsT_done, 1)
            for t in range(TT):
                pe.wait_ge(h_ready, t + 1)
                for q in range(4):
                    n = 4 * t + q
                    if n == 0:
                        pe.wait_ge(cols_ready, 1)
                    if t >= 2:
                        pe.wait_ge(hT_lo, n - 8 + 1)
                    for kk in range(4):
                        k = 4 * q + kk
                        last = nc.tensor.transpose(bank(4 * (t % 2) + q)[:, kk * P:(kk + 1) * P],
                                                   x_rows[:, t, k * P:(k + 1) * P], ident[:, :])
                    last.then_inc(hT_banks, 1)
            pe.wait_ge(hT_lo, 16)
            for ty in range(2):
                for j in range(CMP_UNITS):
                    n = ty * CMP_UNITS + j
                    arrive(n)
                    if j < 8:
                        for half in range(2):
                            columns_half(n, j % 4, half, 2 * (j // 4) + half)
                    else:
                        if j == 8:
                            pe.wait_ge(c_lo, 4 * ty + 4)
                            pe.wait_ge(pos_lo, 2 * ty + 2)
                            if ty:
                                pe.wait_ge(gelu_done, 1)
                        for ll in range(8):
                            l = 8 * (j - 8) + ll
                            o, e = l % CMP_STRIDE, l // CMP_STRIDE
                            at = slice(ll * P, (ll + 1) * P)
                            w, win = P, slice(2 * e, 2 * e + S // CMP_STRIDE)
                            last = mm3(bank(4)[:, e * GROUPS:e * GROUPS + w], (wh[:, n % RING, at], wl[:, n % RING, at]),
                                       (cbh[:, o, win, :].rearrange("p c g -> p (c g)"),
                                        cbl[:, o, win, :].rearrange("p c g -> p (c g)")), l == 0, l == CMP_LEN - 1)
                        last.then_inc(units_used, 1)
                    if n == CMP_UNITS:
                        pe.wait_ge(gelu_done, 1)
                        pe.wait_ge(w2_loaded, 16)
                        mm(bank(6)[:, 0:NC4], w2[:, 0, :], hdn[:, 0, :, :].rearrange("p c g -> p (c g)"),
                           True, True).then_inc(kc_done, 1)
                    if n == CMP_UNITS + 2:
                        pe.wait_ge(kc_sq, 1)
                        mm(bank(7)[0:NC4, 0:1], sq[:, 0, 0:NC4], inv128[:, 0:1], True, True).then_inc(kcsum_done, 1)
                    if n == CMP_UNITS + 6:
                        pe.wait_ge(kc_diag, 1)
                        mm(bank(7)[:, 0:NC4], inv128[0:NC4, :], sq[0:NC4, 0, 0:NC4], True, True).then_inc(kcb_done, 1)
            for q in range(2):
                n = T0 + q
                arrive(n)
                for kk in range(8):
                    k, at = 8 * q + kk, slice(kk * P, (kk + 1) * P)
                    last = mm3(bank(5), (wh[:, n % RING, at], wl[:, n % RING, at]), (hTh[:, k, :], hTl[:, k, :]),
                               k == 0, k == KD - 1)
                last.then_inc(units_used, 1)
            pe.wait_ge(gelu_done, 2)
            pe.wait_ge(kc_raw, 1)
            for grp in range(GROUPS):
                last = mm(bank(6)[0:N_CMP, grp * DH:(grp + 1) * DH], hdn[:, 1, :, grp], w2[:, 1, :], True, True)
            last.then_inc(vc_done, 1)

            def proj_half(u, half, per, i, p):
                n = P0 + u
                if half == 0:
                    arrive(n, per, i)
                if u == 4:
                    wait(pe, vst_ready, half + 1, 2, p)
                if u == 8:
                    wait(pe, kst_ready, half + 1, 2, p)
                if u == 12:
                    wait(pe, q_lo, half + 1, 4, p)
                if u < 4:
                    tokens_half(n, u % 4, half, 6 + half)
                else:
                    columns_half(n, u % 4, half, 6 + half)

            def keys_sums(p):
                wait(pe, ksq_ready, 2, 2, p)
                for j in range(8):
                    last = mm(bank(0)[:, j:j + 1], sq[:, j // TT, j % TT * P:(j % TT + 1) * P], inv128[:, 0:1], True, True)
                last.then_inc(ksum_done, 1)

            def keys_bcast(p, b):
                wait(pe, kdiag_ready, 1, 1, p)
                if b:
                    wait(pe, k_norm, 1, 2, p)
                for t in range(TT):
                    last = mm(bank(0)[:, t * P:(t + 1) * P], inv128[:, :], diag[:, b * TT + t, :], True, True)
                last.then_inc(kb_done, 1)

            def queries_sums(p, h0):
                wait(pe, qsq_ready, h0 + 2, 4, p)
                if h0:
                    wait(pe, q_den, 1, 2, p)
                for h in (h0, h0 + 1):
                    for t in range(TT):
                        last = mm(bank(0)[:, h * TT + t:h * TT + t + 1], sq[:, h - h0, t * P:(t + 1) * P],
                                  inv128[:, 0:1], True, True)
                last.then_inc(qsum_done, 1)

            for u in range(P_UNITS):
                if u == 1:
                    pe.wait_ge(gateT_copied, 1)
                    for t in range(TT):
                        last = nc.tensor.transpose(bank(4)[:, t * P:(t + 1) * P], pbuf[:, 0, t * P:(t + 1) * P],
                                                   ident[:, :])
                    last.then_inc(gates_done, 1)
                if u == 0:
                    pe.wait_ge(vc_ready, 1)
                for half in range(2):
                    proj_half(u, half, 0, 0, 0)
                if u == 8:
                    keys_sums(0)
                if u == 9:
                    keys_bcast(0, 0)
                if u == 10:
                    keys_bcast(0, 1)
                if u == 12:
                    wait(pe, k_norm, 2)
                    queries_sums(0, 0)

            def attention(g, fill, tail, last_group):
                def compressed_scores():
                    wait(pe, group_ready, 1, 1, g)
                    wait(pe, q_den, 2, 2, g)
                    wait(pe, v_hi, 1, 1, g)
                    for i in range(REP * TT):
                        h, t = i // TT, i % TT
                        ts, at = slice(t * P, (t + 1) * P), i % 8 * 2 * CPAD
                        mm(bank(i // 8)[:, at:at + 2 * CPAD], qh[:, h, ts], kcg[:, :, :].rearrange("p n c -> p (n c)"),
                           start=True)
                        last = mm(bank(i // 8)[:, at:at + CPAD], ql[:, h, ts], kcg[:, 0, :], stop=True)
                    last.then_inc(cs_done, 1)

                def scores(i):
                    h, b, t = i // (2 * TT), i // TT % 2, i % TT
                    ts, nk, bk = slice(t * P, (t + 1) * P), (t + 1) * P, bank(2 + i % 2)
                    if i >= 2:
                        wait(pe, exp_done, i - 1, STEPS, g)
                    mm3(bk[:, 0:nk], (qh[:, h, ts], ql[:, h, ts]), (kh[:, b, 0:nk], kl[:, b, 0:nk]), True, False)
                    mm(bk[:, t * P:nk], ident16[:, :], causal[:, :], stop=True).then_inc(s_done, 1)

                def values(m):
                    h, b = m // 2, m % 2
                    if m == 0:
                        wait(pe, v_lo, 1, 1, g)
                    if b == 0:
                        wait(pe, ptc_ready, h + 1, REP, g)
                        if h and last_group:
                            pe.wait_ge(own_lo, h)
                        elif h:
                            wait(pe, o_ready, h, REP, g)
                        mm(bank(1), vcg[:, :], ptc[:, :], start=True)
                    wait(pe, pt_lo, TT * (m + 1), STEPS, g)
                    for k in range(TT):
                        vs, at = slice(b * DH, (b + 1) * DH), slice(PT_AT[k] + k, PT_AT[k] + TT)
                        last = mm3(bank(1)[:, k * P:], (vh[:, k, vs], vl[:, k, vs]),
                                   (pth[:, at, :].rearrange("p t c -> p (t c)"), ptl[:, at, :].rearrange("p t c -> p (t c)")),
                                   False, b == 1 and k == TT - 1)
                    last.then_inc(pv_done, 1)

                def filler(w):
                    u, half = w // 2, w % 2
                    if u == 0:
                        wait(pe, q_lo, 3 + half, 4, g)
                    if not last_group:
                        proj_half(u, half, P_UNITS, g + 1, g + 1)
                        return
                    c, q = u // 3, u % 3
                    if half == 0:
                        arrive(A0 + u)
                        if c == 0:
                            pe.wait_ge(ot_lo, 2 * q + 2)
                    if q == 0 and c:
                        pe.wait_ge(x2a_added, 2 * (c - 1) + half + 1)
                    tokens_half(A0 + u, q, half, 6 + half, 12)

                wait(pe, k_lo, 1, 1, g)
                wait(pe, q_lo, 2, 4, g)
                scores(0)
                scores(1)
                if not last_group:
                    filler(HEAD_FILL[0])
                queries_sums(g, 2)
                if not last_group:
                    filler(HEAD_FILL[1])
                compressed_scores()
                for w in HEAD_FILL[0 if last_group else 2:]:
                    filler(w)
                for i in range(STEPS):
                    t = i % TT
                    if i > TT and t == 1:
                        values(i // TT - 1)
                    for w in fill[i]:
                        filler(w)
                    if i % 8 == 0:
                        h = i // 8
                        wait(pe, pc_ready, 1, 1, g)
                        if h:
                            wait(pe, ptc_ready, h, REP, g)
                        if not last_group and h == 2:
                            wait(pe, k_den, 1, 1, g + 1)
                        if not last_group and h == 3:
                            wait(pe, k_norm, 2, 2, g + 1)
                        for tt in range(TT):
                            last = nc.tensor.transpose(bank(0)[0:CPAD, tt * P:(tt + 1) * P], pc[:, h * TT + tt, :],
                                                       ident[:, :])
                        last.then_inc(trc_done, 1)
                    wait(pe, p_ready, i + 1, STEPS, g)
                    if i >= 2:
                        wait(pe, pt_lo, i - 1, STEPS, g)
                    for k in range(t + 1):
                        ks = slice(k * P, (k + 1) * P)
                        last = nc.tensor.transpose(bank(4 + i % 2)[:, ks], pbuf[:, i % 2, ks], ident[:, :])
                    last.then_inc(tr_done, 1)
                    if i + 2 < STEPS:
                        scores(i + 2)
                    if last_group:
                        continue
                    if i == KSUM_AT:
                        wait(pe, ptc_ready, KSUM_AT // 8 + 1, REP, g)
                        keys_sums(g + 1)
                    if i == KB_AT:
                        wait(pe, ptc_ready, KB_AT // 8 + 1, REP, g)
                        keys_bcast(g + 1, 0)
                    if i == KB2_AT:
                        keys_bcast(g + 1, 1)
                    if i == QSUM_AT:
                        wait(pe, ptc_ready, QSUM_AT // 8 + 1, REP, g)
                        queries_sums(g + 1, 0)
                for w in tail:
                    filler(w)
                values(2 * REP - 1)

            with pe.Fori(0, LAST) as g:
                attention(g, FILL_P, TAIL_P, False)
            attention(LAST, FILL_A, TAIL_A, True)

            def hidden_tiles(c):
                pe.wait_ge(h2_ready, c + 1)
                if 0 < c < 3:
                    pe.wait_ge(h2T_lo, 4 * c)
                if c == 3:
                    pe.wait_ge(x2b_added, 16)
                for kk in range(4):
                    for t in range(TT):
                        last = nc.tensor.transpose(bank(kk + 4 * (c == 3))[:, t * P:(t + 1) * P],
                                                   h_rows[:, c % 2, t, kk * P:(kk + 1) * P], ident[:, :])
                    last.then_inc(h2T_banks, 1)

            pe.wait_ge(own_lo, REP)
            pe.wait_ge(x2a_added, 16)
            for c in range(8):
                arrive(B0 + c)
                if c >= 2:
                    pe.wait_ge(x2b_added, 2 * (c - 2) + 2)
                for half in range(2):
                    bk = 4 + 2 * (c % 2) + half
                    for tt in range(2):
                        for kk in range(4):
                            k, at = OWN + kk, slice(kk * 256, (kk + 1) * 256)
                            ts = slice((2 * half + tt) * P, (2 * half + tt + 1) * P)
                            last = mm3(bank(bk)[:, tt * 256:(tt + 1) * 256], (hTh[:, k, ts], hTl[:, k, ts]),
                                       (wh[:, (B0 + c) % RING, at], wl[:, (B0 + c) % RING, at]),
                                       kk == 0 and tt == 0, kk == 3)
                last.then_inc(units_used, 1)
                if c in (3, 5, 7):
                    hidden_tiles((c - 3) // 2)
            hidden_tiles(3)
            pe.wait_ge(r2_diag, 1)
            pe.wait_ge(h2T_lo, 13)
            for t in range(TT):
                last = mm(bank(4)[:, t * P:(t + 1) * P], inv128[:, :], diag[:, t, :], True, True)
            last.then_inc(rb_done, 1)

            def hidden_unit(n, j, per, s):
                for half in range(2):
                    columns_half(n, j % 8 // 2, half, j // 8 * 4 + j % 2 * 2 + half)

            def slab(s):
                for j in range(F_UNITS):
                    n = F0 + j
                    arrive(n, F_UNITS, s)
                    if j == 0:
                        pe.wait_ge(h2T_lo, 12)
                    if j == 6:
                        pe.wait_ge(h2T_lo, 16)
                    if j == 8:
                        wait(pe, m_ready, 1, 4, s)
                    if j < 16:
                        hidden_unit(n, j, F_UNITS, s)
                        continue
                    c, q = (j - 16) // 2, j % 2
                    if c == 0:
                        wait(pe, m_lo, 2 * q + 2, 4, s)
                    if c < 2 and q == 0:
                        wait(pe, m_ready, 2 * c + 2, 4, s)
                    if c >= 2 and q == 0:
                        wait(pe, y_added, 4 * (c - 1), 16, s)
                    if c == 3 and q == 1:
                        wait(pe, y_added, 12, 16, s)
                    for t in range(TT):
                        for kk in range(2):
                            k, at, ts = 2 * q + kk, slice(kk * 512, (kk + 1) * 512), slice(t * P, (t + 1) * P)
                            last = mm3(bank(4 * (c % 2) + t), (mTh[:, k, ts], mTl[:, k, ts]),
                                       (wh[:, n % RING, at], wl[:, n % RING, at]), k == 0, k == 3)
                    last.then_inc(units_used, 1)

            with pe.Fori(0, SLABS - 1) as s:
                slab(s)
            slab(SLABS - 1)


DVE_GROUP = 4 + 5 + 4 + 3 * STEPS


_INS = ['x', 'norm_mix_g', 'norm_ffn_g', 'nsa_w_in', 'nsa_b_gate', 'nsa_q_norm_g', 'nsa_k_norm_g', 'nsa_cmp_pos',
        'nsa_cmp_w1', 'nsa_cmp_b1', 'nsa_cmp_w2', 'nsa_w_out', 'ffn_w_gate', 'ffn_w_up', 'ffn_w_down']
_OUTS = [((1, 512, 2048), 'float32')]


def kernel(**inputs):
    import numpy as _np
    import concourse.bacc as _bacc
    from concourse import mybir as _mybir
    from concourse.bass_utils import run_bass_kernel_spmd as _run

    nc = _bacc.Bacc("TRN2", target_bir_lowering=False, num_devices=1)
    arrays, args = {}, []
    for name in _INS:
        a = _np.ascontiguousarray(inputs[name])
        arrays[f"in_{name}_dram"] = a
        args.append(nc.dram_tensor(f"in_{name}_dram", a.shape, _mybir.dt.from_np(a.dtype), kind="ExternalInput").ap())
    for i, (shape, dtype) in enumerate(_OUTS):
        dt = _mybir.dt.from_np(_np.dtype(dtype))
        args.append(nc.dram_tensor(f"out_{i}_dram", shape, dt, kind="ExternalOutput").ap())
    nsa_swiglu_block(nc, *args)
    r = _run(nc, [arrays], core_ids=[0])
    got = tuple(r.results[0][f"out_{i}_dram"] for i in range(len(_OUTS)))
    return got[0]
```

```python
import concourse.bass as bass
from concourse import mybir
from contextlib import ExitStack

P = 128
S, D = 512, 2048
HEADS, GROUPS, DH = 16, 4, 128
REP = HEADS // GROUPS
CMP_LEN, CMP_STRIDE = 32, 16
N_CMP = (S - CMP_LEN) // CMP_STRIDE + 1
CPAD = 32
SEL_BLOCK, N_SELECT, WINDOW = 64, 16, 512
D_FF = 5632
EPS = 1e-6
MASKED = -2.0 ** 100
FLOOR = -2.0 ** 66

TT = S // P
KD = D // P
QCOL = 0
KVCOL = [HEADS * DH + n * GROUPS * DH for n in range(6)]
GATECOL = HEADS * DH + 6 * GROUPS * DH
NG = 3 * HEADS

UNIT = 1024
RAW, RING = 2, 4
CMP_UNITS = 13
P0, P_UNITS = 2 * CMP_UNITS, 16
A0 = P0 + GROUPS * P_UNITS
B0 = A0 + 24
F0, F_UNITS = B0 + 8, 24
SLABS = D_FF // 512
LAST = GROUPS - 1
OWN = LAST * REP

STEPS = REP * 2 * TT
HEAD_FILL = [0, 1, 2, 3]
FILL_P = [[4, 5, 6], [7], [], [8], [9], [], [10], [11], [12], [13], [14], [15], [], [], [16], [17],
          [18], [19], [20], [21], [22, 23], [], [24], [25], [26], [], [27], [28], [], [], [29], [30]]
TAIL_P = [31]
FILL_A = [[4, 5], []] + [[h + 6 * c for h in half] for c in range(6) for half in ([6, 7], [8, 9], [10, 11], [])] \
    + [[42], [43], [], [], [44], [45]]
TAIL_A, END_A = [46], 47
V_AT, K_AT, Q_AT = (next(i for i, f in enumerate(FILL_P) if u in f) for u in (7, 15, 23))
KSUM_AT, KB_AT, KB2_AT, QSUM_AT, KSPLIT_AT = 13, 17, 19, 26, STEPS - 2

assert S // SEL_BLOCK <= N_SELECT and WINDOW >= S
assert sum(FILL_P, HEAD_FILL) + TAIL_P == list(range(2 * P_UNITS)) and len(FILL_P) == STEPS
assert sum(FILL_A, HEAD_FILL) + TAIL_A + [END_A] == list(range(48)) and len(FILL_A) == STEPS


def nsa_swiglu_block(nc, x, mix_g, ffn_g, w_in, b_gate, q_g, k_g, cmp_pos, cmp_w1, cmp_b1, cmp_w2,
                     w_out, w_gate, w_up, w_down, out):
    f32, f32r, bf16 = mybir.dt.float32, mybir.dt.float32r, mybir.dt.bfloat16
    ACT, ALU, AX = mybir.ActivationFunctionType, mybir.AluOpType, mybir.AxisListType
    NC4 = N_CMP * GROUPS
    ctx = ExitStack()
    with ctx:
        def sb(name, shape, dt=f32):
            return ctx.enter_context(nc.sbuf_tensor(name, shape, dt))

        def over(name, shape, at, dt=f32):
            return nc.alloc_sbuf_tensor_at(name, shape, dt, offset=at)

        def sem(name):
            return ctx.enter_context(nc.semaphore(name))

        hTh, hTl = sb("hTh", [P, KD, S], f32r), sb("hTl", [P, KD, S], f32r)
        raw = sb("raw", [P, RAW, UNIT])
        wh, wl = sb("wh", [P, RING, UNIT], f32r), sb("wl", [P, RING, UNIT], f32r)
        x_rows = sb("x_rows", [P, TT, D])
        ot = x_rows[:, :, :].rearrange("p t d -> p (t d)").rearrange("p (h s) -> p h s", s=S)
        x2 = x_rows
        q_at = nc.sbuf_base
        qh, ql = sb("qh", [P, REP, S], f32r), sb("ql", [P, REP, S], f32r)
        kh, kl = sb("kh", [P, 2, S], f32r), sb("kl", [P, 2, S], f32r)
        vh, vl = sb("vh", [P, TT, 2 * DH], f32r), sb("vl", [P, TT, 2 * DH], f32r)
        CB = [P, CMP_STRIDE, S // CMP_STRIDE + 2, GROUPS]
        x_sq = over("x_sq", [P, 2, D], q_at)
        cbh, cbl = over("cbh", CB, q_at, f32r), over("cbl", CB, q_at + 4 * CB[1] * CB[2] * CB[3], f32r)
        h_rows = over("h_rows", [P, 2, TT, 512], q_at)
        mTh, mTl = over("mTh", [P, 4, S], q_at + 16 * 1024, f32r), over("mTl", [P, 4, S], q_at + 24 * 1024, f32r)
        stage_at = nc.sbuf_base
        kst, vst = sb("kst", [P, 2, S]), sb("vst", [P, 2, S])
        gain_row = over("gain_row", [P, D], stage_at)
        ffn_work = over("ffn_work", [P, 4, S], stage_at)
        pbuf = sb("pbuf", [P, 2, S])
        PT_AT = [0, 3, 6, 4]
        pt_at = nc.sbuf_base
        pth, ptl = sb("pth", [P, 10, P], f32r), sb("ptl", [P, 10, P], f32r)
        w2 = over("w2", [P, 2, DH], pt_at)
        hdn = over("hdn", [P, N_CMP, GROUPS], pt_at + 1024)
        hdn3 = over("hdn3", [P, GROUPS, 3, CPAD], pt_at + 1536)
        rows = over("rows", [P, P], pt_at + 3072)
        sq = sb("sq", [P, 2, S])
        diag = sq[:, :, :].rearrange("p a s -> p (a s)").rearrange("p (j c) -> p j c", c=P)
        rbc = over("rbc", [P, S], nc.sbuf_base - 4 * S)
        ident, ident16 = sb("ident", [P, P]), sb("ident16", [P, P], bf16)
        inv128 = sb("inv128", [P, P])
        neg_half = sb("neg_half", [P, 1])
        causal = sb("causal", [P, P], bf16)
        causal_cmp = sb("causal_cmp", [P, TT, CPAD], bf16)
        cols = sb("cols", [P, 72])
        gains = sb("gains", [P, 3])
        bgate = sb("bgate", [P, NG])
        gates = sb("gates", [P, TT, NG])
        gates_g = sb("gates_g", [P, TT, 3 * REP])
        hb = sb("hb", [P, 2])
        kch, kcl = sb("kch", [P, GROUPS, CPAD], f32r), sb("kcl", [P, GROUPS, CPAD], f32r)
        kcg = sb("kcg", [P, 2, CPAD], f32r)
        pc3 = sb("pc3", [P, TT, 3, CPAD])
        vc, vcg = sb("vc", [3 * CPAD, GROUPS, DH], f32r), sb("vcg", [3 * CPAD, DH], f32r)
        pc = sb("pc", [P, REP * TT, CPAD])
        ptc = sb("ptc", [3 * CPAD, S], f32r)
        rqs, rqn = sb("rqs", [P, REP * TT]), sb("rqn", [P, REP * TT])
        krr = sb("krr", [P, 8])
        ss, rr = sb("ss", [P, 16]), sb("rr", [P, 4])
        cmx, csum = sb("cmx", [P, REP * TT]), sb("csum", [P, REP * TT])
        nmax, nb, sums, wgt = (sb(n, [P, 2]) for n in ("nmax", "nb", "sums", "wgt"))

        ps = ctx.enter_context(nc.psum_tensor("ps", [P, 8, S], f32))

        def bank(b):
            return ps[:, b, :]

        rows_loaded, gain_loaded, gain2_loaded = sem("rows_loaded"), sem("gain_loaded"), sem("gain2_loaded")
        w2_loaded, bgate_loaded = sem("w2_loaded"), sem("bgate_loaded")
        x_loaded = [sem(f"x_loaded{t}") for t in range(TT)]
        x2_loaded = sem("x2_loaded")
        raw_loaded = [sem(f"raw_loaded{i}") for i in range(RAW)]
        hi_ready, lo_ready, units_used = sem("hi_ready"), sem("lo_ready"), sem("units_used")
        zeroed, consts_ready, ident16_ready = sem("zeroed"), sem("consts_ready"), sem("ident16_ready")
        vector_done = sem("vector_done")
        ss_done, rms_den, rms_root, h_ready = sem("ss_done"), sem("rms_den"), sem("rms_root"), sem("h_ready")
        hT_banks, hT_hi, hT_lo = sem("hT_banks"), sem("hT_hi"), sem("hT_lo")
        rowsT_done, cols_ready, pos_hi, pos_lo = sem("rowsT_done"), sem("cols_ready"), sem("pos_hi"), sem("pos_lo")
        gateT_copied, gates_done = sem("gateT_copied"), sem("gates_done")
        gate_arg, gate_exp, gates_ready = sem("gate_arg"), sem("gate_exp"), sem("gates_ready")
        c_hi, c_lo, hb_ready, gelu_done = sem("c_hi"), sem("c_lo"), sem("hb_ready"), sem("gelu_done")
        kc_done, kc_sq, kc_raw, kcsum_done, kc_den = (sem(n) for n in ("kc_done", "kc_sq", "kc_raw", "kcsum_done", "kc_den"))
        kc_root, kc_diag, kcb_done, kc_norm = sem("kc_root"), sem("kc_diag"), sem("kcb_done"), sem("kc_norm")
        kc_hi, kc_lo, vc_done, vc_hi, vc_ready = (sem(n) for n in ("kc_hi", "kc_lo", "vc_done", "vc_hi", "vc_ready"))
        vst_ready, ksq_ready, kst_ready, ksum_done = sem("vst_ready"), sem("ksq_ready"), sem("kst_ready"), sem("ksum_done")
        k_den, k_root, kdiag_ready, kb_done, k_norm = (sem(n) for n in ("k_den", "k_root", "kdiag_ready", "kb_done", "k_norm"))
        q_hi, q_lo, qsq_ready, qsum_done = sem("q_hi"), sem("q_lo"), sem("qsq_ready"), sem("qsum_done")
        q_den, rqn_ready, k_hi, k_lo, v_hi, v_lo = (sem(n) for n in ("q_den", "rqn_ready", "k_hi", "k_lo", "v_hi", "v_lo"))
        group_ready, cs_done, cs_ready, c_exp, pc_ready = (sem(n) for n in ("group_ready", "cs_done", "cs_ready", "c_exp", "pc_ready"))
        trc_done, ptc_hi, ptc_ready = sem("trc_done"), sem("ptc_hi"), sem("ptc_ready")
        s_done, nb_ready, exp_done, p_ready = sem("s_done"), sem("nb_ready"), sem("exp_done"), sem("p_ready")
        tr_done, pt_hi, pt_lo, pv_done, o_ready = (sem(n) for n in ("tr_done", "pt_hi", "pt_lo", "pv_done", "o_ready"))
        ot_hi, ot_lo, own_hi, own_lo = sem("ot_hi"), sem("ot_lo"), sem("own_hi"), sem("own_lo")
        x2a_added, x2b_added, x2_sq = sem("x2a_added"), sem("x2b_added"), sem("x2_sq")
        h2_ready, h2T_banks, h2T_hi, h2T_lo = sem("h2_ready"), sem("h2T_banks"), sem("h2T_hi"), sem("h2T_lo")
        r2_den, r2_root, r2_diag, rb_done = sem("r2_den"), sem("r2_root"), sem("r2_diag"), sem("rb_done")
        gs_ready, silu_done, m_ready, m_hi, m_lo = (sem(n) for n in ("gs_ready", "silu_done", "m_ready", "m_hi", "m_lo"))
        y_added, stored = sem("y_added"), sem("stored")

        w_in_v = w_in[0].rearrange("(q k p) c -> q p k c", k=4, p=P)
        w_in_8 = w_in[0].rearrange("(q k p) c -> q p k c", k=8, p=P)
        w_gate_v = w_gate[0].rearrange("(q k p) c -> q p k c", k=4, p=P)
        w_up_v = w_up[0].rearrange("(q k p) c -> q p k c", k=4, p=P)
        w1_v = cmp_w1[0].rearrange("t (j l p) c -> t j p l c", l=8, p=P)
        w_out_v = w_out[0].rearrange("(q k p) c -> q p k c", k=4, p=P)
        w_down_v = w_down[0].rearrange("(q k p) c -> p q k c", k=2, p=P)

        def wait(eng, s, base, per=0, i=0):
            eng.wait_ge(s, i * per + base if per else base)

        def ended(halves):
            return [w // 2 for w in halves if w % 2]

        class Own:
            def __init__(self, eng):
                self.eng, self.base, self.local, self.per, self.i = eng, 0, 0, 0, 0

            def done(self, ins):
                ins.then_inc(vector_done, 1)
                self.local += 1

            def settle(self):
                wait(self.eng, vector_done, self.base + self.local, self.per, self.i)

            def enter(self, i, per):
                self.base += self.local
                self.local, self.per, self.i = 0, per, i

            def leave(self, turns):
                assert self.local == self.per, (self.local, self.per)
                self.base += turns * self.per
                self.local, self.per, self.i = 0, 0, 0

        H_BANKS = [0, 1, 2, 3, 4, 5, 6, 7, 2, 3, 4, 5, 6, 7, 2, 3]

        def proj_bank(p, part):
            return 2 if isinstance(p, int) and p == 0 and part % 2 == 0 else 6

        def pt_tiles(i, pt):
            t, bk = i % TT, bank(4 + i % 2)
            if t < TT - 1:
                return [(pt[:, t:t + 3 * t + 1:3, :], bk[:, 0:(t + 1) * P].rearrange("p (k c) -> p k c", c=P))]
            return [(pt[:, t:t + 7:3, :], bk[:, 0:t * P].rearrange("p (k c) -> p k c", c=P)),
                    (pt[:, PT_AT[t] + t, :], bk[:, t * P:(t + 1) * P])]

        block = ctx.enter_context(nc.Block())

        @block.sync
        def _(sp):
            def unit(n, halves, per=0, i=0):
                if n >= RAW:
                    wait(sp, lo_ready, n - RAW + 1, per, i)
                for dst, src in halves:
                    sp.dma_start(dst, src).then_inc(raw_loaded[n % RAW], 16)

            def k_halves(n, src, k):
                dst = raw[:, n % RAW, :].rearrange("p (k c) -> p k c", k=k)
                return [(dst[:, a:a + k // 2, :], src[:, a:a + k // 2, :]) for a in (0, k // 2)]

            def column_halves(n, src_a, src_b):
                dst = raw[:, n % RAW, :].rearrange("p (k c) -> p k c", k=4)
                return [(dst[:, :, 0:P], src_a), (dst[:, :, P:2 * P], src_b)]

            def group_units(first, per, g, g1):
                for b, (ca, cb) in enumerate(((KVCOL[3], KVCOL[5]), (KVCOL[2], KVCOL[4]))):
                    for q in range(4):
                        n = first + 4 * b + q
                        unit(n, column_halves(n, w_in_v[q][:, :, bass.ds(g1 * DH + ca, DH)],
                                              w_in_v[q][:, :, bass.ds(g1 * DH + cb, DH)]), per, g)
                for b in range(2):
                    for q in range(4):
                        n = first + 8 + 4 * b + q
                        unit(n, k_halves(n, w_in_v[q][:, :, bass.ds(g1 * (REP * DH) + (QCOL + b * 256), 256)], 4),
                             per, g)

            for t in range(TT):
                sp.dma_start(x_rows[:, t, :], x[0, t * P:(t + 1) * P, :]).then_inc(x_loaded[t], 16)
                if t == 0:
                    sp.dma_start(gain_row[:, :], mix_g.to_broadcast([P, D])).then_inc(gain_loaded, 16)
            for ty in range(2):
                n = ty * CMP_UNITS
                for b in range(2):
                    for q in range(4):
                        c = KVCOL[ty] + b * 256
                        unit(n, k_halves(n, w_in_v[q][:, :, c:c + 256], 4))
                        n += 1
                unit(n, k_halves(n, w_in_8[ty][:, :, GATECOL + NG - P:GATECOL + NG], 8))
                for j in range(4):
                    unit(n + 1 + j, k_halves(n + 1 + j, w1_v[ty, j], 8))
            group_units(P0, 0, 0, 0)
            with sp.Fori(0, LAST) as g:
                group_units(P0 + P_UNITS, P_UNITS, g, g + 1)
            for c in range(8):
                for q in range(3):
                    n = A0 + 3 * c + q
                    unit(n, k_halves(n, w_out_v[q][:, :, c * 256:(c + 1) * 256], 4))
            for c in range(8):
                unit(B0 + c, k_halves(B0 + c, w_out_v[3][:, :, c * 256:(c + 1) * 256], 4))
            with sp.Fori(0, SLABS) as s:
                for b in range(2):
                    for q in range(4):
                        for u, w in enumerate((w_gate_v, w_up_v)):
                            n = F0 + 8 * b + 2 * q + u
                            unit(n, k_halves(n, w[q][:, :, bass.ds(s * 512 + b * 256, 256)], 4), F_UNITS, s)
                for c in range(4):
                    for q in range(2):
                        n = F0 + 16 + 2 * c + q
                        src = w_down_v[:, bass.ds(s * 2 + q, 1), :, c * 512:(c + 1) * 512]
                        unit(n, k_halves(n, src.rearrange("p q k c -> p (q k) c"), 2), F_UNITS, s)
            out_v = out[0].rearrange("(t p) d -> p t d", p=P)
            for c in range(4):
                wait(sp, y_added, (SLABS - 1) * 16 + 4 * (c + 1))
                sp.dma_start(out_v[:, :, c * 512:(c + 1) * 512], x2[:, :, c * 512:(c + 1) * 512])\
                  .then_inc(stored, 16)
            sp.wait_ge(stored, 64)

        @block.gpsimd
        def _(pool):
            pool.dma_start(rows[0:64, :], cmp_pos[0].rearrange("t l d -> (t l) d")).then_inc(rows_loaded, 16)
            pool.dma_start(rows[64:66, :], cmp_b1[0]).then_inc(rows_loaded, 16)
            pool.dma_start(rows[66:67, :], q_g).then_inc(rows_loaded, 16)
            pool.dma_start(rows[67:70, :], k_g[0]).then_inc(rows_loaded, 16)
            pool.memset(ident[:, :], 0.0).then_inc(zeroed, 1)
            pool.memset(causal[:, :], 0.0).then_inc(zeroed, 1)
            pool.memset(causal_cmp[:, :, :], 0.0).then_inc(zeroed, 1)
            pool.memset(inv128[:, :], 1.0 / P).then_inc(zeroed, 1)
            pool.memset(neg_half[:, :], -0.5).then_inc(zeroed, 1)
            pool.memset(kch[:, :, :].bitcast(f32), 0.0).then_inc(zeroed, 1)
            pool.memset(kcl[:, :, :].bitcast(f32), 0.0).then_inc(zeroed, 1)
            pool.memset(hdn3[:, :, :, N_CMP:], 0.0).then_inc(zeroed, 1)
            pool.wait_ge(zeroed, 8)
            pool.affine_select(out=ident[:, :], in_=ident[:, :], compare_op=ALU.not_equal, fill=1.0, base=0,
                               pattern=[[-1, P]], channel_multiplier=1).then_inc(consts_ready, 1)
            pool.affine_select(out=causal[:, :], in_=causal[:, :], compare_op=ALU.is_ge, fill=MASKED, base=0,
                               pattern=[[-1, P]], channel_multiplier=1).then_inc(consts_ready, 1)
            pool.affine_select(out=causal_cmp[:, :, :], in_=causal_cmp[:, :, :], compare_op=ALU.is_ge,
                               fill=MASKED, base=-(CMP_LEN - 1), pattern=[[P, TT], [-CMP_STRIDE, CPAD]],
                               channel_multiplier=1).then_inc(consts_ready, 1)
            pool.dma_start(bgate[:, :], b_gate.to_broadcast([P, NG])).then_inc(bgate_loaded, 16)
            pool.dma_start(w2[:, :, :], cmp_w2[0].rearrange("t p d -> p t d")).then_inc(w2_loaded, 16)

            def inverse_root(ap, done):
                n, m = ap.shape
                pool.tensor_tensor(ap, ap, neg_half[0:n, 0:1].to_broadcast([n, m]), ALU.pow).then_inc(done, 1)

            for t in range(TT):
                pool.wait_ge(rms_den, t + 1)
                inverse_root(rr[:, t:t + 1], rms_root)
            pool.wait_ge(kc_den, 1)
            inverse_root(krr[0:NC4, 0:1], kc_root)

            def group_roots(p):
                wait(pool, k_den, 1, 1, p)
                inverse_root(krr[:, :], k_root)
                for b in range(2):
                    wait(pool, q_den, b + 1, 2, p)
                    inverse_root(rqn[:, b * 2 * TT:(b + 1) * 2 * TT], rqn_ready)

            group_roots(0)
            with pool.Fori(0, LAST) as g:
                group_roots(g + 1)
            for t in range(TT):
                if t < OWN // TT:
                    pool.wait_ge(ot_lo, 2 * t + 2)
                pool.dma_start(x2[:, t, :], x[0, t * P:(t + 1) * P, :]).then_inc(x2_loaded, 16)
            pool.dma_start(gain_row[:, :], ffn_g.to_broadcast([P, D])).then_inc(gain2_loaded, 16)
            pool.wait_ge(r2_den, 1)
            inverse_root(rr[:, :], r2_root)

        @block.scalar
        def _(act):
            def copy(dst, src):
                return nc.scalar.activation(dst, src, ACT.Copy)

            def square(dst, src):
                return nc.scalar.activation(dst, src, ACT.Square)

            def split(n, per=0, i=0):
                wait(act, raw_loaded[n % RAW], 32 * (n // RAW + 1), 32 * per // RAW, i)
                if n >= RING:
                    wait(act, units_used, n - RING + 1, per, i)
                copy(wh[:, n % RING, :], raw[:, n % RAW, :]).then_inc(hi_ready, 1)

            def sum_squares(t):
                act.wait_ge(x_loaded[t], 16)
                if t >= 2:
                    act.wait_ge(ss_done, t - 1)
                nc.scalar.activation(x_sq[:, t % 2, :], x_rows[:, t, :], ACT.Square,
                                     accum_out=ss[:, t:t + 1]).then_inc(ss_done, 1)

            def hidden_columns(t):
                for q in range(4):
                    act.wait_ge(hT_banks, 4 * t + q + 1)
                    copy(hTh[:, 4 * q:4 * q + 4, t * P:(t + 1) * P],
                         bank(H_BANKS[4 * t + q]).rearrange("p (k c) -> p k c", k=4)).then_inc(hT_hi, 1)

            sum_squares(0)
            sum_squares(1)
            hidden_columns(0)
            hidden_columns(1)
            split(0)
            sum_squares(2)
            split(1)
            sum_squares(3)
            hidden_columns(2)
            split(2)
            hidden_columns(3)
            split(3)
            for ty in range(2):
                for j in range(CMP_UNITS):
                    n = ty * CMP_UNITS + j
                    if j in (3, 7):
                        act.wait_ge(units_used, n + 1)
                        for grp in ((j - 3) // 2, (j - 3) // 2 + 1):
                            src = bank(grp).rearrange("p (c l) -> p l c", l=CMP_STRIDE)
                            copy(cbh[:, :, 1:-1, grp], src).then_inc(c_hi, 1)
                    if n == CMP_UNITS + 8:
                        act.wait_ge(units_used, n + 1)
                        copy(pbuf[:, 0, :], bank(5)).then_inc(gateT_copied, 1)
                    split(n + RING)
                    if n == CMP_UNITS:
                        act.wait_ge(kc_done, 1)
                        square(sq[:, 0, 0:NC4], bank(6)[:, 0:NC4]).then_inc(kc_sq, 1)
                    if n == CMP_UNITS + 7:
                        act.wait_ge(kc_norm, 1)
                        copy(kch[:, :, 0:N_CMP], sq[:, 0, 0:NC4].rearrange("p (c g) -> p g c", g=GROUPS))\
                            .then_inc(kc_hi, 1)
                    if j == CMP_UNITS - 1:
                        act.wait_ge(hb_ready, ty + 1)
                        src = bank(4)[:, GROUPS:GROUPS + NC4]
                        if ty == 0:
                            dsts = [hdn[:, :, :].rearrange("p c g -> p (c g)")]
                        else:
                            src = src.rearrange("p (c g) -> p g c", g=GROUPS)
                            dsts = [hdn3[:, :, r, 0:N_CMP] for r in range(3)]
                        for dst in dsts:
                            last = nc.scalar.activation(dst, src, ACT.Gelu_apprx_tanh, bias=hb[:, ty:ty + 1])
                        last.then_inc(gelu_done, 1)

            def values_out(per, i, p):
                wait(act, units_used, P0 + 4, per, i)
                for b in range(2):
                    copy(vst[:, b, :], bank(proj_bank(p, 0) + b)).then_inc(vst_ready, 1)

            def keys_out(per, i, p):
                wait(act, units_used, P0 + 8, per, i)
                for b in range(2):
                    square(sq[:, b, :], bank(proj_bank(p, 1) + b)).then_inc(ksq_ready, 1)

            def queries_out(per, i, p, h0):
                wait(act, units_used, P0 + 12 + 2 * h0, per, i)
                if h0 == 0:
                    wait(act, kb_done, 2, 2, p)
                else:
                    wait(act, qsum_done, 1, 2, p)
                for h in (h0, h0 + 1):
                    src = bank(proj_bank(p, 2 + h0 // 2) + h - h0)
                    copy(qh[:, h, :], src).then_inc(q_hi, 1)
                    square(sq[:, h - h0, :], src).then_inc(qsq_ready, 1)

            def keys_split(p):
                wait(act, k_norm, 2, 2, p)
                copy(kh[:, :, :], kst[:, :, :]).then_inc(k_hi, 1)

            def values_split(p):
                wait(act, vst_ready, 2, 2, p)
                copy(vh[:, :, :].rearrange("p t c -> p (t c)"), vst[:, :, :].rearrange("p a s -> p (a s)"))\
                    .then_inc(v_hi, 1)

            for u in range(P_UNITS):
                if u == 3:
                    values_out(0, 0, 0)
                if u == 7:
                    keys_out(0, 0, 0)
                if u == 11:
                    queries_out(0, 0, 0, 0)
                if u == 15:
                    queries_out(0, 0, 0, 2)
                split(P0 + u + RING)
                if u == 1:
                    act.wait_ge(vc_done, 1)
                    copy(vc[:, :, :].rearrange("p g d -> p (g d)"), bank(5)[0:3 * CPAD, :]).then_inc(vc_hi, 1)
                if u == 2:
                    act.wait_ge(gate_arg, 1)
                    nc.scalar.activation(gates[:, :, :], gates[:, :, :], ACT.Exp, scale=-1.0).then_inc(gate_exp, 1)
                if u == 12:
                    keys_split(0)
            values_split(0)

            def attention(g, fill, tail, last):
                def compressed_exp():
                    wait(act, cs_ready, 1, 1, g)
                    nc.scalar.activation(pc[:, :, :], pc[:, :, :], ACT.Exp).then_inc(c_exp, 1)

                def probs(i):
                    t, m = i % TT, i // (2 * TT) * TT + i % TT
                    nk = (t + 1) * P
                    wait(act, nb_ready, i + 1, STEPS, g)
                    nc.scalar.activation(pbuf[:, i % 2, 0:nk], bank(2 + i % 2)[:, 0:nk], ACT.Exp,
                                         bias=nb[:, i % 2:i % 2 + 1], scale=rqs[:, m:m + 1],
                                         accum_out=sums[:, i % 2:i % 2 + 1]).then_inc(exp_done, 1)

                def pt_part(i):
                    wait(act, tr_done, i + 1, STEPS, g)
                    if i >= TT and i % TT == 0:
                        wait(act, pv_done, i // TT, 2 * REP, g)
                    for dst, src in pt_tiles(i, pth):
                        last = copy(dst, src)
                    last.then_inc(pt_hi, 1)

                def head_out(h):
                    wait(act, pv_done, 2 * (h + 1), 2 * REP, g)
                    if last:
                        copy(hTh[:, OWN + h, :], bank(1)).then_inc(own_hi, 1)
                    else:
                        copy(ot[:, bass.ds(g * REP + h, 1), :].rearrange("p a b -> p (a b)"), bank(1))\
                            .then_inc(o_ready, 1)

                def first_out(q):
                    copy(hTh[:, 2 * q:2 * q + 2, :], ot[:, 2 * q:2 * q + 2, :]).then_inc(ot_hi, 1)

                def after(j):
                    ends = () if last else (V_AT, K_AT, Q_AT)
                    return ([] if j in ends else ended(fill[j])) + (ended(fill[j - 1]) if j - 1 in ends else [])

                def splits(units):
                    for u in units:
                        if last:
                            split(A0 + u + RING)
                        else:
                            split(P0 + P_UNITS + u + RING, P_UNITS, g)

                if last:
                    act.wait_ge(o_ready, OWN)
                    first_out(0)
                    first_out(1)
                probs(0)
                compressed_exp()
                if last:
                    for q in range(2, OWN // 2):
                        first_out(q)
                for i in range(1, STEPS + 1):
                    if i < STEPS:
                        probs(i)
                    if i == 1:
                        splits(ended(HEAD_FILL))
                    j = i - 1
                    if j % 8 == 0 and j < STEPS:
                        wait(act, trc_done, j // 8 + 1, REP, g)
                        copy(ptc[:, :], bank(0)[0:3 * CPAD, :]).then_inc(ptc_hi, 1)
                    pt_part(j)
                    if j >= 8 and j % 8 == 0:
                        head_out(j // 8 - 1)
                    if not last and j == V_AT:
                        values_out(P_UNITS, g + 1, g + 1)
                    if not last and j == K_AT:
                        keys_out(P_UNITS, g + 1, g + 1)
                    if not last and j == Q_AT:
                        queries_out(P_UNITS, g + 1, g + 1, 0)
                    splits(after(j))
                    if not last:
                        if j == KSPLIT_AT:
                            wait(act, s_done, STEPS, STEPS, g)
                            keys_split(g + 1)
                if not last:
                    queries_out(P_UNITS, g + 1, g + 1, 2)
                head_out(REP - 1)
                splits(ended(tail + [END_A] if last else tail))
                if not last:
                    values_split(g + 1)

            with act.Fori(0, LAST) as g:
                attention(g, FILL_P, TAIL_P, False)
            attention(LAST, FILL_A, TAIL_A, True)
            def hidden_part(c):
                for kk in range(4):
                    act.wait_ge(h2T_banks, 4 * c + kk + 1)
                    copy(hTh[:, 4 * c + kk, :], bank(kk + 4 * (c == 3))).then_inc(h2T_hi, 1)

            for c in range(4):
                split(B0 + 2 * c + RING)
                if c:
                    hidden_part(c - 1)
                split(B0 + 2 * c + 1 + RING)
                for t in range(TT):
                    act.wait_ge(x2b_added, 4 * c + 4)
                    if c or t:
                        act.wait_ge(x2_sq, 4 * c + t)
                    nc.scalar.activation(pbuf[:, 0, :], x2[:, t, c * 512:(c + 1) * 512], ACT.Square,
                                         accum_out=ss[:, 4 * c + t:4 * c + t + 1]).then_inc(x2_sq, 1)

            def slab(s, first=False, last=False):
                for j in range(F_UNITS):
                    n = F0 + j
                    if first and j == 1:
                        hidden_part(3)
                    if j in (6, 14):
                        for c in range(2):
                            wait(act, gs_ready, (j - 6) // 4 + c + 1, 4, s)
                            nc.scalar.activation(ffn_work[:, c, :], ffn_work[:, c, :], ACT.Silu).then_inc(silu_done, 1)
                    if j in (7, 15):
                        for c in range(2):
                            wait(act, m_ready, (j - 7) // 4 + c + 1, 4, s)
                            copy(mTh[:, (j - 7) // 4 + c, :], ffn_work[:, 2 + c, :]).then_inc(m_hi, 1)
                    if not last or j + RING < F_UNITS:
                        split(n + RING, F_UNITS, s)

            slab(0, first=True)
            with act.Fori(0, SLABS - 2) as s:
                slab(s + 1)
            slab(SLABS - 1, last=True)

        @block.vector
        def _(dve):
            own = Own(dve)

            def lo(dst, src, hi, done):
                nc.vector.tensor_tensor(dst, src, hi.bitcast(f32), ALU.subtract).then_inc(done, 1)

            def split(n, per=0, i=0):
                wait(dve, hi_ready, n + 1, per, i)
                lo(wl[:, n % RING, :], raw[:, n % RAW, :], wh[:, n % RING, :], lo_ready)

            dve.wait_ge(consts_ready, 1)
            nc.vector.tensor_copy(ident16[:, :], ident[:, :]).then_inc(ident16_ready, 1)
            def norm(t):
                dve.wait_ge(ss_done, t + 1)
                nc.vector.tensor_scalar(rr[:, t:t + 1], ss[:, t:t + 1], 1.0 / D, EPS, ALU.mult, ALU.add)\
                    .then_inc(rms_den, 1)
                if t == 0:
                    dve.wait_ge(gain_loaded, 16)
                dve.wait_ge(rms_root, t + 1)
                nc.vector.scalar_tensor_tensor(out=x_rows[:, t, :], in0=x_rows[:, t, :], scalar=rr[:, t:t + 1],
                                               in1=gain_row[:, :], op0=ALU.mult, op1=ALU.mult).then_inc(h_ready, 1)

            def hidden_columns(t):
                for q in range(4):
                    dve.wait_ge(hT_hi, 4 * t + q + 1)
                    at = (slice(None), slice(4 * q, 4 * q + 4), slice(t * P, (t + 1) * P))
                    lo(hTl[at], bank(H_BANKS[4 * t + q]).rearrange("p (k c) -> p k c", k=4), hTh[at], hT_lo)

            norm(0)
            norm(1)
            hidden_columns(0)
            hidden_columns(1)
            split(0)
            norm(2)
            split(1)
            norm(3)
            hidden_columns(2)
            split(2)
            hidden_columns(3)
            split(3)
            for ty in range(2):
                for j in range(CMP_UNITS):
                    n = ty * CMP_UNITS + j
                    if n == 4:
                        dve.wait_ge(rowsT_done, 1)
                        nc.vector.tensor_copy(cols[:, 0:70], bank(4)[:, 0:70]).then_inc(cols_ready, 1)
                        dve.wait_ge(cols_ready, 1)
                        own.done(nc.vector.tensor_scalar(gains[:, :], cols[:, 67:70], cols[:, 66:67], None, ALU.mult))
                    if j == 4:
                        dve.wait_ge(units_used, n)
                        for part, at in ((0, 0), (1, S // CMP_STRIDE + 1)):
                            l0 = ty * CMP_LEN + part * CMP_STRIDE
                            pos = cols[:, l0:l0 + CMP_STRIDE].rearrange("p (l a) -> p l a", a=1)\
                                .to_broadcast([P, CMP_STRIDE, GROUPS])
                            nc.vector.tensor_copy(cbh[:, :, at, :], pos).then_inc(pos_hi, 1)
                            dve.wait_ge(pos_hi, 2 * ty + part + 1)
                            lo(cbl[:, :, at, :], pos, cbh[:, :, at, :], pos_lo)
                    if j in (3, 7):
                        for grp in ((j - 3) // 2, (j - 3) // 2 + 1):
                            dve.wait_ge(c_hi, 4 * ty + grp + 1)
                            src = bank(grp).rearrange("p (c l) -> p l c", l=CMP_STRIDE)
                            lo(cbl[:, :, 1:-1, grp], src, cbh[:, :, 1:-1, grp], c_lo)
                    split(n + RING)
                    if n == CMP_UNITS:
                        dve.wait_ge(kc_sq, 1)
                        nc.vector.tensor_scalar(sq[:, 1, 0:NC4], bank(6)[:, 0:NC4], gains[:, 0:1], None, ALU.mult)\
                            .then_inc(kc_raw, 1)
                    if n == CMP_UNITS + 2:
                        dve.wait_ge(kcsum_done, 1)
                        nc.vector.tensor_scalar(krr[0:NC4, 0:1], bank(7)[0:NC4, 0:1], EPS, P ** -2.0, ALU.add, ALU.mult)\
                            .then_inc(kc_den, 1)
                    if n == CMP_UNITS + 4:
                        dve.wait_ge(kc_root, 1)
                        nc.vector.tensor_scalar(sq[0:NC4, 0, 0:NC4], ident[0:NC4, 0:NC4], krr[0:NC4, 0:1], None, ALU.mult)\
                            .then_inc(kc_diag, 1)
                    if n == CMP_UNITS + 6:
                        dve.wait_ge(kcb_done, 1)
                        dve.wait_ge(kc_raw, 1)
                        nc.vector.tensor_tensor(sq[:, 0, 0:NC4], sq[:, 1, 0:NC4], bank(7)[:, 0:NC4], ALU.mult)\
                            .then_inc(kc_norm, 1)
                    if n == CMP_UNITS + 8:
                        dve.wait_ge(kc_hi, 1)
                        lo(kcl[:, :, 0:N_CMP], sq[:, 0, 0:NC4].rearrange("p (c g) -> p g c", g=GROUPS),
                           kch[:, :, 0:N_CMP], kc_lo)
                    if j == CMP_UNITS - 1:
                        dve.wait_ge(units_used, n + 1)
                        own.done(nc.vector.tensor_tensor(hb[:, ty:ty + 1], bank(4)[:, 0:1], cols[:, 64 + ty:65 + ty],
                                                         ALU.add))
                        own.settle()
                        nc.vector.tensor_tensor(hb[:, ty:ty + 1], bank(4)[:, S // 4:S // 4 + 1], hb[:, ty:ty + 1],
                                                ALU.add).then_inc(hb_ready, 1)

            def keys_out(p):
                for b in range(2):
                    wait(dve, ksq_ready, b + 1, 2, p)
                    nc.vector.tensor_scalar(kst[:, b, :], bank(proj_bank(p, 1) + b), gains[:, 1 + b:2 + b], None, ALU.mult)\
                        .then_inc(kst_ready, 1)

            def keys_den(p):
                wait(dve, ksum_done, 1, 1, p)
                nc.vector.tensor_scalar(krr[:, :], bank(0)[:, 0:8], EPS, P ** -2.0, ALU.add, ALU.mult)\
                    .then_inc(k_den, 1)

            def keys_diag(p):
                wait(dve, k_root, 1, 1, p)
                for j in range(8):
                    last = nc.vector.tensor_scalar(diag[:, j, :], ident[:, :], krr[:, j:j + 1], None, ALU.mult)
                last.then_inc(kdiag_ready, 1)

            def keys_norm(p, b):
                wait(dve, kst_ready, 2, 2, p)
                wait(dve, kb_done, b + 1, 2, p)
                nc.vector.tensor_tensor(kst[:, b, :], kst[:, b, :], bank(0), ALU.mult).then_inc(k_norm, 1)

            def queries_out(p, h0):
                for h in (h0, h0 + 1):
                    wait(dve, qsq_ready, h + 1, 4, p)
                    lo(ql[:, h, :], bank(proj_bank(p, 2 + h0 // 2) + h - h0), qh[:, h, :], q_lo)

            def queries_den(p, h0):
                wait(dve, qsum_done, h0 // 2 + 1, 2, p)
                at = slice(h0 * TT, (h0 + 2) * TT)
                nc.vector.tensor_scalar(rqn[:, at], bank(0)[:, at], EPS, float(DH), ALU.add, ALU.mult)\
                    .then_inc(q_den, 1)

            def keys_split(p):
                wait(dve, k_hi, 1, 1, p)
                lo(kl[:, :, :], kst[:, :, :], kh[:, :, :], k_lo)

            def values_split(p):
                wait(dve, v_hi, 1, 1, p)
                lo(vl[:, :, :].rearrange("p t c -> p (t c)"), vst[:, :, :].rearrange("p a s -> p (a s)"),
                   vh[:, :, :].rearrange("p t c -> p (t c)"), v_lo)

            for u in range(P_UNITS):
                if u == 7:
                    keys_out(0)
                if u == 8:
                    keys_den(0)
                if u == 9:
                    keys_diag(0)
                if u == 10:
                    keys_norm(0, 0)
                    keys_norm(0, 1)
                if u == 11:
                    queries_out(0, 0)
                if u == 13:
                    queries_den(0, 0)
                if u == 15:
                    queries_out(0, 2)
                split(P0 + u + RING)
                if u == 1:
                    dve.wait_ge(vc_hi, 1)
                    at = vc[CPAD:2 * CPAD, :, :].rearrange("p g d -> p (g d)")
                    lo(at, bank(5)[CPAD:2 * CPAD, :], at, vc_ready)
                if u == 2:
                    dve.wait_ge(gates_done, 1)
                    dve.wait_ge(bgate_loaded, 16)
                    nc.vector.tensor_tensor(gates[:, :, :], bank(4).rearrange("p (t c) -> p t c", t=TT)[:, :, P - NG:P],
                                            bgate[:, :].rearrange("p (a c) -> p a c", a=1).to_broadcast([P, TT, NG]),
                                            ALU.add).then_inc(gate_arg, 1)
                if u == 3:
                    dve.wait_ge(gate_exp, 1)
                    own.done(nc.vector.tensor_scalar_add(gates[:, :, :], gates[:, :, :], 1.0))
                    own.settle()
                    nc.vector.reciprocal(gates[:, :, :], gates[:, :, :]).then_inc(gates_ready, 1)
                if u == 12:
                    keys_split(0)
            dve.wait_ge(vc_ready, 1)
            dve.wait_ge(kc_lo, 1)
            dve.wait_ge(gates_ready, 1)

            def attention(g, fill, tail, last):
                own.done(nc.vector.tensor_copy(kcg[:, 0, :], kch[:, bass.ds(g, 1), :].bitcast(f32)
                                               .rearrange("p a c -> p (a c)")))
                own.done(nc.vector.tensor_copy(kcg[:, 1, :], kcl[:, bass.ds(g, 1), :].bitcast(f32)
                                               .rearrange("p a c -> p (a c)")))
                own.done(nc.vector.tensor_copy(gates_g[:, :, :], gates[:, :, bass.ds(g * (3 * REP), 3 * REP)]))
                nc.vector.tensor_copy(vcg[:, :], vc[:, bass.ds(g, 1), :].bitcast(f32).rearrange("p a d -> p (a d)"))\
                    .then_inc(group_ready, 1)
                queries_den(g, 2)
                values_split(g)

                def first_out(q):
                    dve.wait_ge(ot_hi, q + 1)
                    lo(hTl[:, 2 * q:2 * q + 2, :], ot[:, 2 * q:2 * q + 2, :], hTh[:, 2 * q:2 * q + 2, :], ot_lo)

                def after(j):
                    ends = () if last else (V_AT, K_AT, Q_AT)
                    return ([] if j in ends else ended(fill[j])) + (ended(fill[j - 1]) if j - 1 in ends else [])

                def splits(units):
                    for u in units:
                        if last and u % 3 == 2:
                            if u == 2:
                                dve.wait_ge(x2_loaded, 16 * TT)
                            dve.wait_ge(units_used, A0 + u + 1)
                            for b in range(2):
                                at = x2[:, 2 * b:2 * b + 2, u // 3 * 256:(u // 3 + 1) * 256]
                                nc.vector.tensor_tensor(at, at, bank(6 + b).rearrange("p (t c) -> p t c", t=2),
                                                        ALU.add).then_inc(x2a_added, 1)
                        if last:
                            split(A0 + u + RING)
                        else:
                            split(P0 + P_UNITS + u + RING, P_UNITS, g)

                if last:
                    first_out(0)
                    first_out(1)
                wait(dve, rqn_ready, 2, 2, g)
                own.done(nc.vector.tensor_copy(rqs[:, :], rqn[:, :]))
                own.settle()

                def each(ap):
                    return ap.rearrange("p (i a) -> p i a", a=1).to_broadcast([P, REP * TT, CPAD])

                def compressed_scores():
                    sc = ps[:, 0:2, :].rearrange("p b (i n c) -> p (b i) n c", n=2, c=CPAD)
                    wait(dve, cs_done, 1, 1, g)
                    for h in range(REP):
                        at = slice(h * TT, (h + 1) * TT)
                        last_ = nc.vector.tensor_tensor(pc[:, at, :], sc[:, at, 1, :], causal_cmp[:, :, :], ALU.add)
                    own.done(last_)
                    own.settle()
                    own.done(nc.vector.tensor_tensor(pc[:, :, :], pc[:, :, :], sc[:, :, 0, :], ALU.add))
                    own.settle()
                    own.done(nc.vector.reduce_max(cmx[:, :], pc[:, :, :], axis=AX.X))
                    own.settle()
                    own.done(nc.vector.tensor_scalar_max(cmx[:, :], cmx[:, :], FLOOR))
                    own.settle()
                    own.done(nc.vector.tensor_tensor(pc[:, :, :], pc[:, :, :], each(cmx[:, :]), ALU.subtract))
                    own.settle()
                    nc.vector.tensor_tensor(pc[:, :, :], pc[:, :, :], each(rqs[:, :]), ALU.mult).then_inc(cs_ready, 1)

                def compressed_thrice(h):
                    if h:
                        wait(dve, trc_done, h, REP, g)
                    at = slice(h * TT, (h + 1) * TT)
                    nc.vector.tensor_tensor(
                        pc3[:, :, :, :], pc[:, at, :].rearrange("p t (a c) -> p t a c", a=1).to_broadcast([P, TT, 3, CPAD]),
                        csum[:, at].rearrange("p (t a b) -> p t a b", a=1, b=1).to_broadcast([P, TT, 3, CPAD]),
                        ALU.mult).then_inc(pc_ready, 1)

                def compressed_weigh():
                    wait(dve, c_exp, 1, 1, g)
                    own.done(nc.vector.reduce_sum(csum[:, :], pc[:, :, :], axis=AX.X))
                    own.settle()
                    own.done(nc.vector.tensor_scalar_max(csum[:, :], csum[:, :], 1e-30))
                    own.settle()
                    own.done(nc.vector.reciprocal(csum[:, :], csum[:, :]))
                    own.settle()
                    gate3 = gates_g[:, :, :].rearrange("p t (h b) -> p h t b", b=3)
                    own.done(nc.vector.tensor_tensor(csum[:, :].rearrange("p (h t) -> p h t", h=REP),
                                                     csum[:, :].rearrange("p (h t) -> p h t", h=REP),
                                                     gate3[:, :, :, 0], ALU.mult))
                    own.settle()
                    compressed_thrice(0)

                def maximum(i):
                    nk = (i % TT + 1) * P
                    e, m = slice(i % 2, i % 2 + 1), i // (2 * TT) * TT + i % TT
                    wait(dve, s_done, i + 1, STEPS, g)
                    own.done(nc.vector.tensor_reduce(nmax[:, e], bank(2 + i % 2)[:, 0:nk], AX.X, ALU.max, negate=True))
                    own.settle()
                    nc.vector.tensor_scalar(nb[:, e], nmax[:, e], rqs[:, m:m + 1], None, ALU.mult).then_inc(nb_ready, 1)

                def weigh(i):
                    h, b, t = i // (2 * TT), i // TT % 2, i % TT
                    nk, e = (t + 1) * P, slice(i % 2, i % 2 + 1)
                    wait(dve, exp_done, i + 1, STEPS, g)
                    own.done(nc.vector.tensor_scalar_max(wgt[:, e], sums[:, e], 1e-30))
                    own.settle()
                    own.done(nc.vector.reciprocal(wgt[:, e], wgt[:, e]))
                    own.settle()
                    gate = gates_g[:, t, 3 * h + 1 + b:3 * h + 2 + b]
                    nc.vector.tensor_scalar(pbuf[:, i % 2, 0:nk], pbuf[:, i % 2, 0:nk], wgt[:, e], gate, ALU.mult, ALU.mult)\
                        .then_inc(p_ready, 1)

                def pt_part(i):
                    wait(dve, pt_hi, i + 1, STEPS, g)
                    for (dst, src), (hi, _) in zip(pt_tiles(i, ptl), pt_tiles(i, pth)):
                        last_ = nc.vector.tensor_tensor(dst, src, hi.bitcast(f32), ALU.subtract)
                    last_.then_inc(pt_lo, 1)

                maximum(0)
                compressed_scores()
                if last:
                    for q in range(2, OWN // 2):
                        first_out(q)
                for i in range(1, STEPS + 2):
                    if i <= STEPS:
                        weigh(i - 1)
                    if i < STEPS:
                        maximum(i)
                    if i == 1:
                        compressed_weigh()
                        splits(ended(HEAD_FILL))
                    if i % 8 == 7 and i < STEPS - 1:
                        compressed_thrice(i // 8 + 1)
                    if i >= 2:
                        pt_part(i - 2)
                    if i % 8 == 1 and i < STEPS:
                        wait(dve, ptc_hi, i // 8 + 1, REP, g)
                        at = ptc[2 * CPAD:, :]
                        lo(at, bank(0)[2 * CPAD:3 * CPAD, :], at, ptc_ready)
                    if i < 2:
                        continue
                    j = i - 2
                    if last and j >= 8 and j % 8 == 0:
                        dve.wait_ge(own_hi, j // 8)
                        lo(hTl[:, OWN + j // 8 - 1, :], bank(1), hTh[:, OWN + j // 8 - 1, :], own_lo)
                    if not last and j == K_AT:
                        keys_out(g + 1)
                    if not last and j == Q_AT:
                        queries_out(g + 1, 0)
                    splits(after(j))
                    if last:
                        continue
                    if j == KSUM_AT - 1:
                        keys_den(g + 1)
                    if j == KSUM_AT:
                        keys_diag(g + 1)
                    if j == KB_AT - 1:
                        keys_norm(g + 1, 0)
                    if j == KB2_AT - 1:
                        keys_norm(g + 1, 1)
                    if j == QSUM_AT - 1:
                        queries_den(g + 1, 0)
                    if j == KSPLIT_AT:
                        keys_split(g + 1)
                if last:
                    dve.wait_ge(own_hi, REP)
                    lo(hTl[:, OWN + REP - 1, :], bank(1), hTh[:, OWN + REP - 1, :], own_lo)
                else:
                    queries_out(g + 1, 2)
                splits(ended(tail + [END_A] if last else tail))

            with dve.Fori(0, LAST) as g:
                own.enter(g, DVE_GROUP)
                attention(g, FILL_P, TAIL_P, False)
                own.leave(LAST)
            attention(LAST, FILL_A, TAIL_A, True)

            def hidden_part(c):
                for kk in range(4):
                    dve.wait_ge(h2T_hi, 4 * c + kk + 1)
                    lo(hTl[:, 4 * c + kk, :], bank(kk + 4 * (c == 3)), hTh[:, 4 * c + kk, :], h2T_lo)

            for c in range(4):
                for half in range(2):
                    u = 2 * c + half
                    dve.wait_ge(units_used, B0 + u + 1)
                    for b in range(2):
                        at = x2[:, 2 * b:2 * b + 2, u * 256:(u + 1) * 256]
                        nc.vector.tensor_tensor(at, at, bank(4 + 2 * half + b).rearrange("p (t c) -> p t c", t=2),
                                                ALU.add).then_inc(x2b_added, 1)
                    if half == 0:
                        split(B0 + u + RING)
                        if c:
                            hidden_part(c - 1)
                if c == 0:
                    dve.wait_ge(gain2_loaded, 16)
                if c >= 2:
                    dve.wait_ge(h2T_banks, 4 * (c - 1))
                dve.wait_ge(x2b_added, 4 * c + 4)
                nc.vector.tensor_tensor(h_rows[:, c % 2, :, :], x2[:, :, c * 512:(c + 1) * 512],
                                        gain_row[:, c * 512:(c + 1) * 512].rearrange("p (a d) -> p a d", a=1)
                                        .to_broadcast([P, TT, 512]), ALU.mult).then_inc(h2_ready, 1)
                split(B0 + 2 * c + 1 + RING)

            dve.wait_ge(x2_sq, 16)
            own.done(nc.vector.reduce_sum(rr[:, :], ss[:, :].rearrange("p (c t) -> p t c", t=TT), axis=AX.X))
            own.settle()
            own.done(nc.vector.tensor_scalar(rr[:, :], rr[:, :], 1.0 / D, EPS, ALU.mult, ALU.add))
            own.settle()
            nc.vector.tensor_scalar(rr[:, :], rr[:, :], P ** -2.0, None, ALU.mult).then_inc(r2_den, 1)
            dve.wait_ge(r2_root, 1)
            for t in range(TT):
                last = nc.vector.tensor_scalar(diag[:, t, :], ident[:, :], rr[:, t:t + 1], None, ALU.mult)
            last.then_inc(r2_diag, 1)

            def slab(s, first=False, last=False):
                for j in range(F_UNITS):
                    n = F0 + j
                    if first and j == 1:
                        hidden_part(3)
                    if first and j == 4:
                        dve.wait_ge(rb_done, 1)
                        own.done(nc.vector.tensor_copy(rbc[:, :], bank(4)))
                        own.settle()
                    k, b0 = j // 8 * 2, j // 8 * 4
                    if j in (6, 14):
                        wait(dve, units_used, n + 1, F_UNITS, s)
                        for c in range(2):
                            nc.vector.tensor_tensor(ffn_work[:, c, :], bank(b0 + c), rbc[:, :], ALU.mult)\
                                .then_inc(gs_ready, 1)
                    if j in (7, 15):
                        wait(dve, units_used, n + 1, F_UNITS, s)
                        for c in range(2):
                            own.done(nc.vector.tensor_tensor(ffn_work[:, 2 + c, :], bank(b0 + 2 + c), rbc[:, :], ALU.mult))
                        own.settle()
                        for c in range(2):
                            wait(dve, silu_done, k + c + 1, 4, s)
                            nc.vector.tensor_tensor(ffn_work[:, 2 + c, :], ffn_work[:, c, :], ffn_work[:, 2 + c, :],
                                                    ALU.mult).then_inc(m_ready, 1)
                        for c in range(2):
                            wait(dve, m_hi, k + c + 1, 4, s)
                            lo(mTl[:, k + c, :], ffn_work[:, 2 + c, :], mTh[:, k + c, :], m_lo)
                    if j > 16 and j % 2:
                        wait(dve, units_used, n + 1, F_UNITS, s)
                        c = (j - 17) // 2
                        for t in range(TT):
                            at = x2[:, t, c * 512:(c + 1) * 512]
                            nc.vector.tensor_tensor(at, at, bank(4 * (c % 2) + t), ALU.add).then_inc(y_added, 1)
                    if not last or j + RING < F_UNITS:
                        split(n + RING, F_UNITS, s)

            slab(0, first=True)
            with dve.Fori(0, SLABS - 2) as s:
                own.enter(s, 4)
                slab(s + 1)
                own.leave(SLABS - 2)
            slab(SLABS - 1, last=True)

        @block.tensor
        def _(pe):
            def mm(out_, a, b, start=False, stop=False):
                return nc.tensor.matmul(out_, a, b, start=start, stop=stop, skip_group_check=True)

            def mm3(out_, a, b, start, stop):
                mm(out_, a[0], b[0], start=start)
                mm(out_, a[0], b[1])
                return mm(out_, a[1], b[0], stop=stop)

            def arrive(n, per=0, i=0):
                wait(pe, lo_ready, n + 1, per, i)

            def columns_half(n, q, half, bk):
                for kk in range(4):
                    k, at = 4 * q + kk, slice(kk * 256 + half * P, kk * 256 + half * P + P)
                    last = mm3(bank(bk), (wh[:, n % RING, at], wl[:, n % RING, at]), (hTh[:, k, :], hTl[:, k, :]),
                               k == 0, k == KD - 1)
                if half:
                    last.then_inc(units_used, 1)

            def tokens_half(n, q, half, bk, k_all=KD):
                for tt in range(2):
                    for kk in range(4):
                        k, at = 4 * q + kk, slice(kk * 256, (kk + 1) * 256)
                        ts = slice((2 * half + tt) * P, (2 * half + tt + 1) * P)
                        last = mm3(bank(bk)[:, tt * 256:(tt + 1) * 256], (hTh[:, k, ts], hTl[:, k, ts]),
                                   (wh[:, n % RING, at], wl[:, n % RING, at]),
                                   q == 0 and kk == 0 and tt == 0, k == k_all - 1)
                if half:
                    last.then_inc(units_used, 1)

            pe.wait_ge(consts_ready, 1)

            def hidden_columns(t):
                pe.wait_ge(h_ready, t + 1)
                for q in range(4):
                    n = 4 * t + q
                    if n >= 8:
                        pe.wait_ge(hT_lo, max(m for m in range(n) if H_BANKS[m] == H_BANKS[n]) + 1)
                    for kk in range(4):
                        k = 4 * q + kk
                        last = nc.tensor.transpose(bank(H_BANKS[n])[:, kk * P:(kk + 1) * P],
                                                   x_rows[:, t, k * P:(k + 1) * P], ident[:, :])
                    last.then_inc(hT_banks, 1)

            def first_unit(n, tokens):
                arrive(n)
                ts = slice(tokens * S // 2, (tokens + 1) * S // 2)
                for half in range(2):
                    for kk in range(4):
                        k, at = 4 * n + kk, slice(kk * 256 + half * P, kk * 256 + half * P + P)
                        last = mm3(bank(half)[:, ts], (wh[:, n, at], wl[:, n, at]), (hTh[:, k, ts], hTl[:, k, ts]),
                                   k == 0 and tokens == 0, k == KD - 1)
                if tokens:
                    last.then_inc(units_used, 1)

            hidden_columns(0)
            hidden_columns(1)
            pe.wait_ge(hT_lo, 8)
            first_unit(0, 0)
            hidden_columns(2)
            first_unit(1, 0)
            hidden_columns(3)
            first_unit(2, 0)
            pe.wait_ge(hT_lo, 16)
            for n in range(3):
                first_unit(n, 1)
            first_unit(3, 0)
            first_unit(3, 1)
            pe.wait_ge(consts_ready, 3)
            pe.wait_ge(zeroed, 8)
            pe.wait_ge(rows_loaded, 64)
            nc.tensor.transpose(bank(4)[:, 0:70], rows[0:70, :], ident[0:70, 0:70]).then_inc(rowsT_done, 1)
            for ty in range(2):
                for j in range(CMP_UNITS):
                    n = ty * CMP_UNITS + j
                    if n < 4:
                        continue
                    arrive(n)
                    if j < 8:
                        for half in range(2):
                            columns_half(n, j % 4, half, 2 * (j // 4) + half)
                    elif j == 8:
                        for kk in range(8):
                            k, at = 8 * ty + kk, slice(kk * P, (kk + 1) * P)
                            last = mm3(bank(5), (wh[:, n % RING, at], wl[:, n % RING, at]), (hTh[:, k, :], hTl[:, k, :]),
                                       k == 0, k == KD - 1)
                        last.then_inc(units_used, 1)
                    else:
                        if j == 9:
                            pe.wait_ge(c_lo, 4 * ty + 4)
                            pe.wait_ge(cols_ready, 1)
                            pe.wait_ge(pos_lo, 2 * ty + 2)
                            if ty:
                                pe.wait_ge(gelu_done, 1)
                        for ll in range(8):
                            l = 8 * (j - 9) + ll
                            o, e = l % CMP_STRIDE, l // CMP_STRIDE
                            at = slice(ll * P, (ll + 1) * P)
                            w, win = P, slice(2 * e, 2 * e + S // CMP_STRIDE)
                            last = mm3(bank(4)[:, e * GROUPS:e * GROUPS + w], (wh[:, n % RING, at], wl[:, n % RING, at]),
                                       (cbh[:, o, win, :].rearrange("p c g -> p (c g)"),
                                        cbl[:, o, win, :].rearrange("p c g -> p (c g)")), l == 0, l == CMP_LEN - 1)
                        last.then_inc(units_used, 1)
                    if n == CMP_UNITS:
                        pe.wait_ge(gelu_done, 1)
                        pe.wait_ge(w2_loaded, 16)
                        mm(bank(6)[:, 0:NC4], w2[:, 0, :], hdn[:, :, :].rearrange("p c g -> p (c g)"),
                           True, True).then_inc(kc_done, 1)
                    if n == CMP_UNITS + 2:
                        pe.wait_ge(kc_sq, 1)
                        mm(bank(7)[0:NC4, 0:1], sq[:, 0, 0:NC4], inv128[:, 0:1], True, True).then_inc(kcsum_done, 1)
                    if n == CMP_UNITS + 6:
                        pe.wait_ge(kc_diag, 1)
                        mm(bank(7)[:, 0:NC4], inv128[0:NC4, :], sq[0:NC4, 0, 0:NC4], True, True).then_inc(kcb_done, 1)
            def proj_half(u, half, per, i, p):
                n = P0 + u
                if half == 0:
                    arrive(n, per, i)
                if isinstance(p, int) and p == 0:
                    if u == 4:
                        wait(pe, vc_ready, 1)
                    if u == 8:
                        wait(pe, vst_ready, half + 1)
                    if u == 12:
                        wait(pe, kst_ready, half + 1)
                else:
                    if u == 4:
                        wait(pe, vst_ready, half + 1, 2, p)
                    if u == 8:
                        wait(pe, kst_ready, half + 1, 2, p)
                    if u == 12:
                        wait(pe, q_lo, half + 1, 4, p)
                bk = proj_bank(p, u // 4) + half
                if u < 4:
                    tokens_half(n, u % 4, half, bk)
                else:
                    columns_half(n, u % 4, half, bk)

            def keys_sums(p):
                wait(pe, ksq_ready, 2, 2, p)
                for j in range(8):
                    last = mm(bank(0)[:, j:j + 1], sq[:, j // TT, j % TT * P:(j % TT + 1) * P], inv128[:, 0:1], True, True)
                last.then_inc(ksum_done, 1)

            def keys_bcast(p, b):
                wait(pe, kdiag_ready, 1, 1, p)
                if b:
                    wait(pe, k_norm, 1, 2, p)
                for t in range(TT):
                    last = mm(bank(0)[:, t * P:(t + 1) * P], inv128[:, :], diag[:, b * TT + t, :], True, True)
                last.then_inc(kb_done, 1)

            def queries_sums(p, h0):
                wait(pe, qsq_ready, h0 + 2, 4, p)
                if h0:
                    wait(pe, q_den, 1, 2, p)
                for h in (h0, h0 + 1):
                    for t in range(TT):
                        last = mm(bank(0)[:, h * TT + t:h * TT + t + 1], sq[:, h - h0, t * P:(t + 1) * P],
                                  inv128[:, 0:1], True, True)
                last.then_inc(qsum_done, 1)

            for u in range(P_UNITS):
                if u == 1:
                    pe.wait_ge(gelu_done, 2)
                    pe.wait_ge(gateT_copied, 1)
                    for grp in range(GROUPS):
                        last = mm(bank(5)[0:3 * CPAD, grp * DH:(grp + 1) * DH],
                                  hdn3[:, grp, :, :].rearrange("p r c -> p (r c)"), w2[:, 1, :], True, True)
                    last.then_inc(vc_done, 1)
                if u == 2:
                    for t in range(TT):
                        last = nc.tensor.transpose(bank(4)[:, t * P:(t + 1) * P], pbuf[:, 0, t * P:(t + 1) * P],
                                                   ident[:, :])
                    last.then_inc(gates_done, 1)
                for half in range(2):
                    proj_half(u, half, 0, 0, 0)
                if u == 8:
                    keys_sums(0)
                if u == 9:
                    keys_bcast(0, 0)
                if u == 10:
                    keys_bcast(0, 1)
                if u == 12:
                    wait(pe, k_norm, 2)
                    queries_sums(0, 0)

            def attention(g, fill, tail, last_group):
                def compressed_scores():
                    wait(pe, group_ready, 1, 1, g)
                    wait(pe, q_den, 2, 2, g)
                    wait(pe, v_hi, 1, 1, g)
                    for i in range(REP * TT):
                        h, t = i // TT, i % TT
                        ts, at = slice(t * P, (t + 1) * P), i % 8 * 2 * CPAD
                        mm(bank(i // 8)[:, at:at + 2 * CPAD], qh[:, h, ts], kcg[:, :, :].rearrange("p n c -> p (n c)"),
                           start=True)
                        last = mm(bank(i // 8)[:, at:at + CPAD], ql[:, h, ts], kcg[:, 0, :], stop=True)
                    last.then_inc(cs_done, 1)

                def scores(i):
                    h, b, t = i // (2 * TT), i // TT % 2, i % TT
                    ts, nk, bk = slice(t * P, (t + 1) * P), (t + 1) * P, bank(2 + i % 2)
                    if i >= 2:
                        wait(pe, exp_done, i - 1, STEPS, g)
                    mm3(bk[:, 0:nk], (qh[:, h, ts], ql[:, h, ts]), (kh[:, b, 0:nk], kl[:, b, 0:nk]), True, False)
                    mm(bk[:, t * P:nk], ident16[:, :], causal[:, :], stop=True).then_inc(s_done, 1)

                def values(m):
                    h, b = m // 2, m % 2
                    if m == 0:
                        wait(pe, v_lo, 1, 1, g)
                    if b == 0:
                        wait(pe, ptc_ready, h + 1, REP, g)
                        if h and last_group:
                            pe.wait_ge(own_lo, h)
                        elif h:
                            wait(pe, o_ready, h, REP, g)
                        mm(bank(1), vcg[:, :], ptc[:, :], start=True)
                    wait(pe, pt_lo, TT * (m + 1), STEPS, g)
                    for k in range(TT):
                        vs, at = slice(b * DH, (b + 1) * DH), slice(PT_AT[k] + k, PT_AT[k] + TT)
                        last = mm3(bank(1)[:, k * P:], (vh[:, k, vs], vl[:, k, vs]),
                                   (pth[:, at, :].rearrange("p t c -> p (t c)"), ptl[:, at, :].rearrange("p t c -> p (t c)")),
                                   False, b == 1 and k == TT - 1)
                    last.then_inc(pv_done, 1)

                def filler(w):
                    u, half = w // 2, w % 2
                    if u == 0:
                        wait(pe, q_lo, 3 + half, 4, g)
                    if not last_group:
                        proj_half(u, half, P_UNITS, g + 1, g + 1)
                        return
                    c, q = u // 3, u % 3
                    if half == 0:
                        arrive(A0 + u)
                        if c == 0:
                            pe.wait_ge(ot_lo, 2 * q + 2)
                    if q == 0 and c:
                        pe.wait_ge(x2a_added, 2 * (c - 1) + half + 1)
                    tokens_half(A0 + u, q, half, 6 + half, 12)

                wait(pe, k_lo, 1, 1, g)
                wait(pe, q_lo, 2, 4, g)
                scores(0)
                scores(1)
                if not last_group:
                    filler(HEAD_FILL[0])
                queries_sums(g, 2)
                if not last_group:
                    filler(HEAD_FILL[1])
                compressed_scores()
                for w in HEAD_FILL[0 if last_group else 2:]:
                    filler(w)
                for i in range(STEPS):
                    t = i % TT
                    if i > TT and t == 1:
                        values(i // TT - 1)
                    for w in fill[i]:
                        filler(w)
                    if i % 8 == 0:
                        h = i // 8
                        wait(pe, pc_ready, h + 1, REP, g)
                        if h:
                            wait(pe, ptc_ready, h, REP, g)
                        if not last_group and h == 2:
                            wait(pe, k_den, 1, 1, g + 1)
                        if not last_group and h == 3:
                            wait(pe, k_norm, 2, 2, g + 1)
                        for tt in range(TT):
                            last = nc.tensor.transpose(bank(0)[0:3 * CPAD, tt * P:(tt + 1) * P],
                                                       pc3[:, tt, :, :].rearrange("p r c -> p (r c)"), ident[:, :])
                        last.then_inc(trc_done, 1)
                    wait(pe, p_ready, i + 1, STEPS, g)
                    if i >= 2:
                        wait(pe, pt_lo, i - 1, STEPS, g)
                    for k in range(t + 1):
                        ks = slice(k * P, (k + 1) * P)
                        last = nc.tensor.transpose(bank(4 + i % 2)[:, ks], pbuf[:, i % 2, ks], ident[:, :])
                    last.then_inc(tr_done, 1)
                    if i + 2 < STEPS:
                        scores(i + 2)
                    if last_group:
                        continue
                    if i == KSUM_AT:
                        wait(pe, ptc_ready, KSUM_AT // 8 + 1, REP, g)
                        keys_sums(g + 1)
                    if i == KB_AT:
                        wait(pe, ptc_ready, KB_AT // 8 + 1, REP, g)
                        keys_bcast(g + 1, 0)
                    if i == KB2_AT:
                        keys_bcast(g + 1, 1)
                    if i == QSUM_AT:
                        wait(pe, ptc_ready, QSUM_AT // 8 + 1, REP, g)
                        queries_sums(g + 1, 0)
                for w in tail:
                    filler(w)
                values(2 * REP - 1)
                if last_group:
                    filler(END_A)

            with pe.Fori(0, LAST) as g:
                attention(g, FILL_P, TAIL_P, False)
            attention(LAST, FILL_A, TAIL_A, True)

            def hidden_tiles(c):
                pe.wait_ge(h2_ready, c + 1)
                if 0 < c < 3:
                    pe.wait_ge(h2T_lo, 4 * c)
                if c == 3:
                    pe.wait_ge(x2b_added, 16)
                for kk in range(4):
                    for t in range(TT):
                        last = nc.tensor.transpose(bank(kk + 4 * (c == 3))[:, t * P:(t + 1) * P],
                                                   h_rows[:, c % 2, t, kk * P:(kk + 1) * P], ident[:, :])
                    last.then_inc(h2T_banks, 1)

            pe.wait_ge(own_lo, REP)
            for c in range(8):
                arrive(B0 + c)
                if c == 1:
                    pe.wait_ge(x2a_added, 16)
                if c >= 2:
                    pe.wait_ge(x2b_added, 2 * (c - 2) + 2)
                for half in range(2):
                    bk = 4 + 2 * (c % 2) + half
                    for tt in range(2):
                        for kk in range(4):
                            k, at = OWN + kk, slice(kk * 256, (kk + 1) * 256)
                            ts = slice((2 * half + tt) * P, (2 * half + tt + 1) * P)
                            last = mm3(bank(bk)[:, tt * 256:(tt + 1) * 256], (hTh[:, k, ts], hTl[:, k, ts]),
                                       (wh[:, (B0 + c) % RING, at], wl[:, (B0 + c) % RING, at]),
                                       kk == 0 and tt == 0, kk == 3)
                last.then_inc(units_used, 1)
                if c in (2, 4, 6):
                    hidden_tiles((c - 2) // 2)

            def norm_bcast():
                pe.wait_ge(r2_diag, 1)
                pe.wait_ge(h2T_lo, 13)
                for t in range(TT):
                    last = mm(bank(4)[:, t * P:(t + 1) * P], inv128[:, :], diag[:, t, :], True, True)
                last.then_inc(rb_done, 1)

            def hidden_unit(n, j, per, s):
                for half in range(2):
                    columns_half(n, j % 8 // 2, half, j // 8 * 4 + j % 2 * 2 + half)

            def slab(s, first=False):
                for j in range(F_UNITS):
                    n = F0 + j
                    arrive(n, F_UNITS, s)
                    if first and j == 0:
                        pe.wait_ge(h2T_lo, 12)
                    if first and j == 1:
                        hidden_tiles(3)
                    if first and j == 4:
                        norm_bcast()
                    if first and j == 6:
                        pe.wait_ge(h2T_lo, 16)
                    if j == 8:
                        wait(pe, gs_ready, 2, 4, s)
                    if j < 16:
                        hidden_unit(n, j, F_UNITS, s)
                        continue
                    c, q = (j - 16) // 2, j % 2
                    if c == 0:
                        wait(pe, m_lo, 2 * q + 2, 4, s)
                    if c < 2 and q == 0:
                        wait(pe, m_ready, 2 * c + 2, 4, s)
                    if c >= 2 and q == 0:
                        wait(pe, y_added, 4 * (c - 1), 16, s)
                    if c == 3 and q == 1:
                        wait(pe, y_added, 12, 16, s)
                    for t in range(TT):
                        for kk in range(2):
                            k, at, ts = 2 * q + kk, slice(kk * 512, (kk + 1) * 512), slice(t * P, (t + 1) * P)
                            last = mm3(bank(4 * (c % 2) + t), (mTh[:, k, ts], mTl[:, k, ts]),
                                       (wh[:, n % RING, at], wl[:, n % RING, at]), k == 0, k == 3)
                    last.then_inc(units_used, 1)

            slab(0, first=True)
            with pe.Fori(0, SLABS - 2) as s:
                slab(s + 1)
            slab(SLABS - 1)


DVE_GROUP = 4 + 5 + 4 + 3 * STEPS


_INS = ['x', 'norm_mix_g', 'norm_ffn_g', 'nsa_w_in', 'nsa_b_gate', 'nsa_q_norm_g', 'nsa_k_norm_g', 'nsa_cmp_pos',
        'nsa_cmp_w1', 'nsa_cmp_b1', 'nsa_cmp_w2', 'nsa_w_out', 'ffn_w_gate', 'ffn_w_up', 'ffn_w_down']
_OUTS = [((1, 512, 2048), 'float32')]


def kernel(**inputs):
    import numpy as _np
    import concourse.bacc as _bacc
    from concourse import mybir as _mybir
    from concourse.bass_utils import run_bass_kernel_spmd as _run

    nc = _bacc.Bacc("TRN2", target_bir_lowering=False, num_devices=1)
    arrays, args = {}, []
    for name in _INS:
        a = _np.ascontiguousarray(inputs[name])
        arrays[f"in_{name}_dram"] = a
        args.append(nc.dram_tensor(f"in_{name}_dram", a.shape, _mybir.dt.from_np(a.dtype), kind="ExternalInput").ap())
    for i, (shape, dtype) in enumerate(_OUTS):
        dt = _mybir.dt.from_np(_np.dtype(dtype))
        args.append(nc.dram_tensor(f"out_{i}_dram", shape, dt, kind="ExternalOutput").ap())
    nsa_swiglu_block(nc, *args)
    r = _run(nc, [arrays], core_ids=[0])
    got = tuple(r.results[0][f"out_{i}_dram"] for i in range(len(_OUTS)))
    return got[0]
```
